# Optimizing a Trainium2 kernel written in Bass

```python
import math
import jax, jax.numpy as jnp
from jax import lax
import numpy as np

D_MODEL = 1024
BATCH = 1
SEQ = 512
DEPTH = 2

GDN_HEADS = 4
GDN_DK = 128
GDN_DV = 128
GDN_CONV = 4
GDN_CHUNK = 64
RWKV_HEADS = 8
RWKV_N = 64
RWKV_DECAY_LORA = 64
RWKV_AAA_LORA = 64
RWKV_GATE_LORA = 128
RWKV_LN_EPS = 64e-5
NSA_HEADS = 16
NSA_GROUPS = 2
NSA_HD = 64
CMP_LEN = 32
CMP_STRIDE = 16
CMP_HIDDEN = 256
SEL_BLOCK = 64
SEL_TOPN = 16
WINDOW = 512
NSA_QBLOCK = 64
ROPE_THETA = 500000.0
ROPE_DIM = NSA_HD // 4
D_FF = 4 * D_MODEL
NORM_EPS = 1e-6

GDN_QK_W = GDN_HEADS * GDN_DK
GDN_V_W = GDN_HEADS * GDN_DV
GDN_CONV_W = 2 * GDN_QK_W + GDN_V_W
GDN_W = GDN_CONV_W + GDN_V_W + 2 * GDN_HEADS
RWKV_W = RWKV_HEADS * RWKV_N
RWKV_IN_W = 3 * RWKV_W + RWKV_DECAY_LORA + RWKV_AAA_LORA + RWKV_GATE_LORA
AB_IN_W = GDN_W + RWKV_IN_W
AB_OUT_W = GDN_V_W + RWKV_W
NSA_KV_W = NSA_GROUPS * NSA_HD
NSA_IN_W = NSA_HEADS * NSA_HD + 6 * NSA_KV_W + 3 * NSA_HEADS
NSA_OUT_W = NSA_HEADS * NSA_HD
N_EVEN = (DEPTH + 1) // 2
N_ODD = DEPTH // 2

kernel_name = 'hybrid_gdn_rwkv7_nsa_trunk'

def rmsnorm(x, w):
    x32 = x.astype(jnp.float32)
    y = x32 * lax.rsqrt(jnp.mean(x32 * x32, axis=-1, keepdims=True) + NORM_EPS)
    return (y * w.astype(jnp.float32)).astype(x.dtype)

def l2norm(x):
    return x * lax.rsqrt(jnp.sum(x * x, axis=-1, keepdims=True) + 1e-6)

def partial_rotary(x, pos):
    half = ROPE_DIM // 2
    inv_freq = ROPE_THETA ** (-jnp.arange(half, dtype=jnp.float32) * (2.0 / ROPE_DIM))
    ang = pos.astype(jnp.float32)[:, None, :, None] * inv_freq
    cos = jnp.cos(ang).astype(x.dtype)
    sin = jnp.sin(ang).astype(x.dtype)
    x1, x2, rest = x[..., :half], x[..., half:ROPE_DIM], x[..., ROPE_DIM:]
    return jnp.concatenate([x1 * cos - x2 * sin, x2 * cos + x1 * sin, rest], axis=-1)

def masked_softmax(s, mask):
    s = jnp.where(mask, s.astype(jnp.float32), -jnp.inf)
    m = jnp.max(s, axis=-1, keepdims=True)
    m = jnp.where(jnp.isfinite(m), m, 0.0)
    e = jnp.where(mask, jnp.exp(s - m), 0.0)
    return e / jnp.maximum(jnp.sum(e, axis=-1, keepdims=True), 1e-30)

def causal_dwconv(x, w):
    return lax.conv_general_dilated(
        x, w[:, None, :].astype(x.dtype), window_strides=(1,),
        padding=[(w.shape[0] - 1, 0)], dimension_numbers=('NWC', 'WIO', 'NWC'),
        feature_group_count=x.shape[-1])

def gated_delta_chunked(q, k, v, beta, g):
    B_, H_, T_, dk = q.shape
    dv = v.shape[-1]
    C = GDN_CHUNK
    NC = T_ // C
    q = q.reshape(B_, H_, NC, C, dk)
    k = k.reshape(B_, H_, NC, C, dk)
    v = v.reshape(B_, H_, NC, C, dv)
    beta = beta.reshape(B_, H_, NC, C)
    gc = jnp.cumsum(g.reshape(B_, H_, NC, C), axis=-1)
    tril = jnp.tril(jnp.ones((C, C), bool))
    strict = jnp.tril(jnp.ones((C, C), bool), -1)
    decay = jnp.exp(jnp.where(tril, gc[..., :, None] - gc[..., None, :], -jnp.inf))
    a_mat = jnp.where(strict, beta[..., :, None] * jnp.einsum('bhncd,bhned->bhnce', k, k) * decay, 0.0)
    rhs = jnp.concatenate([v * beta[..., None], k * (beta * jnp.exp(gc))[..., None]], axis=-1)
    sol = lax.linalg.triangular_solve(a_mat + jnp.eye(C, dtype=a_mat.dtype), rhs,
                                      left_side=True, lower=True, unit_diagonal=True)
    u, w = sol[..., :dv], sol[..., dv:]
    intra = jnp.where(tril, jnp.einsum('bhncd,bhned->bhnce', q, k) * decay, 0.0)
    q_g = q * jnp.exp(gc)[..., None]
    k_g = k * jnp.exp(gc[..., -1:] - gc)[..., None]
    g_last = jnp.exp(gc[..., -1])

    def step(S, inp):
        u_n, w_n, q_n, k_n, a_n, gl = inp
        v_new = u_n - jnp.einsum('bhcd,bhdv->bhcv', w_n, S)
        o = jnp.einsum('bhcd,bhdv->bhcv', q_n, S) + jnp.einsum('bhce,bhev->bhcv', a_n, v_new)
        S = S * gl[..., None, None] + jnp.einsum('bhcd,bhcv->bhdv', k_n, v_new)
        return S, o

    xs = tuple(jnp.moveaxis(t, 2, 0) for t in (u, w, q_g, k_g, intra, g_last))
    S0 = jnp.zeros((B_, H_, dk, dv), jnp.float32)
    _, o = lax.scan(step, S0, xs)
    return jnp.moveaxis(o, 0, 2).reshape(B_, H_, T_, dv)

def gdn_mixer(f, conv_w, a_log, dt_bias, norm_w):
    B_, T_, _ = f.shape
    qkv = jax.nn.silu(causal_dwconv(f[..., :GDN_CONV_W], conv_w))
    q = qkv[..., :GDN_QK_W]
    k = qkv[..., GDN_QK_W:2 * GDN_QK_W]
    v = qkv[..., 2 * GDN_QK_W:]
    z = f[..., GDN_CONV_W:GDN_CONV_W + GDN_V_W]
    b = f[..., GDN_CONV_W + GDN_V_W:GDN_CONV_W + GDN_V_W + GDN_HEADS]
    a = f[..., GDN_CONV_W + GDN_V_W + GDN_HEADS:]

    def heads(t, d):
        return t.reshape(B_, T_, GDN_HEADS, d).transpose(0, 2, 1, 3)

    q = l2norm(heads(q, GDN_DK)) * GDN_DK ** -0.5
    k = l2norm(heads(k, GDN_DK))
    v = heads(v, GDN_DV)
    beta = jax.nn.sigmoid(b).transpose(0, 2, 1)
    g = (-jnp.exp(a_log) * jax.nn.softplus(a + dt_bias)).transpose(0, 2, 1)
    o = gated_delta_chunked(q, k, v, beta, g).transpose(0, 2, 1, 3)
    o = rmsnorm(o, norm_w) * jax.nn.silu(z.reshape(B_, T_, GDN_HEADS, GDN_DV))
    return o.reshape(B_, T_, GDN_V_W)

def rwkv7_mixer(f, mu, w0, w2, a0, a2, g2, k_k, k_a, r_k, ln_w, ln_b):
    B_, T_, _ = f.shape
    f_prev = jnp.concatenate([jnp.zeros_like(f[:, :1]), f[:, :-1]], axis=1)
    f = f + (f_prev - f) * mu
    W = RWKV_W
    r, k, v = f[..., :W], f[..., W:2 * W], f[..., 2 * W:3 * W]
    o0 = 3 * W
    wd = f[..., o0:o0 + RWKV_DECAY_LORA]
    ad = f[..., o0 + RWKV_DECAY_LORA:o0 + RWKV_DECAY_LORA + RWKV_AAA_LORA]
    gd = f[..., o0 + RWKV_DECAY_LORA + RWKV_AAA_LORA:]
    w_log = -jax.nn.softplus(-(w0 + jnp.tanh(wd) @ w2)) - 0.5
    decay = jnp.exp(-jnp.exp(w_log))
    a = jax.nn.sigmoid(a0 + ad @ a2)
    g = jax.nn.sigmoid(gd) @ g2

    def heads(t):
        return t.reshape(B_, T_, RWKV_HEADS, RWKV_N)

    kk = l2norm(heads(k * k_k))
    k = k * (1.0 + (a - 1.0) * k_a)
    r_h, k_h, v_h, w_h, a_h = heads(r), heads(k), heads(v), heads(decay), heads(a)

    def step(S, inp):
        r_t, w_t, k_t, v_t, kk_t, a_t = inp
        sa = jnp.einsum('bhvk,bhk->bhv', S, -kk_t)
        S = (S * w_t[:, :, None, :] + sa[..., None] * (kk_t * a_t)[:, :, None, :]
             + v_t[..., None] * k_t[:, :, None, :])
        return S, jnp.einsum('bhvk,bhk->bhv', S, r_t)

    xs = tuple(jnp.moveaxis(t, 1, 0) for t in (r_h, w_h, k_h, v_h, kk, a_h))
    S0 = jnp.zeros((B_, RWKV_HEADS, RWKV_N, RWKV_N), jnp.float32)
    _, y = lax.scan(step, S0, xs)
    y = jnp.moveaxis(y, 0, 1)
    mean = jnp.mean(y, axis=-1, keepdims=True)
    var = jnp.mean(jnp.square(y - mean), axis=-1, keepdims=True)
    y = ((y - mean) * lax.rsqrt(var + RWKV_LN_EPS)).reshape(B_, T_, W) * ln_w + ln_b
    bonus = jnp.sum(r_h * k_h * r_k, axis=-1, keepdims=True) * v_h
    return (y + bonus.reshape(B_, T_, W)) * g

def compress_blocks(t, pe, w1, w2):
    B_, G_, T_, d = t.shape
    c = t.reshape(B_, G_, T_ // CMP_STRIDE, CMP_STRIDE, d)
    blocks = jnp.concatenate([c[:, :, :-1], c[:, :, 1:]], axis=3) + pe
    h = jax.nn.silu(blocks.reshape(B_, G_, -1, CMP_LEN * d) @ w1)
    return h @ w2

def nsa_mixer(f, pos, pe_k, w1_k, w2_k, pe_v, w1_v, w2_v):
    B_, T_, _ = f.shape
    H, G, D = NSA_HEADS, NSA_GROUPS, NSA_HD
    HPG = H // G
    QW, KV = H * D, G * D
    q = f[..., :QW].reshape(B_, T_, H, D).transpose(0, 2, 1, 3)
    k_c, v_c, k_s, v_s, k_w, v_w = [
        f[..., QW + i * KV:QW + (i + 1) * KV].reshape(B_, T_, G, D).transpose(0, 2, 1, 3)
        for i in range(6)]
    gates = jax.nn.sigmoid(f[..., QW + 6 * KV:]).reshape(B_, T_, H, 3).transpose(0, 2, 1, 3)
    q = partial_rotary(q, pos) * D ** -0.5
    k_s = partial_rotary(k_s, pos)
    k_w = partial_rotary(k_w, pos)
    n_cmp = T_ // CMP_STRIDE - 1
    kc = partial_rotary(compress_blocks(k_c, pe_k, w1_k, w2_k), pos[:, CMP_LEN - 1::CMP_STRIDE])
    vc = compress_blocks(v_c, pe_v, w1_v, w2_v)
    n_sel = T_ // SEL_BLOCK
    n_top = min(SEL_TOPN, n_sel)
    ks_blk = k_s.reshape(B_, G, n_sel, SEL_BLOCK, D)
    vs_blk = v_s.reshape(B_, G, n_sel, SEL_BLOCK, D)
    pad = ((0, 0), (0, 0), (WINDOW, 0), (0, 0))
    kw_pad = jnp.pad(k_w, pad)
    vw_pad = jnp.pad(v_w, pad)
    c_start = jnp.arange(n_cmp) * CMP_STRIDE
    s_start = jnp.arange(n_sel) * SEL_BLOCK
    overlap = jnp.clip(jnp.minimum(c_start[:, None] + CMP_LEN, s_start[None, :] + SEL_BLOCK)
                       - jnp.maximum(c_start[:, None], s_start[None, :]), 0, None).astype(jnp.float32) / CMP_LEN
    cmp_end = c_start + CMP_LEN - 1
    sel_id = jnp.arange(n_sel)
    bi = jnp.arange(B_)[:, None, None, None]
    gi = jnp.arange(G)[None, :, None, None]

    def q_block(i):
        s = i * NSA_QBLOCK
        t = s + jnp.arange(NSA_QBLOCK)
        qb = lax.dynamic_slice_in_dim(q, s, NSA_QBLOCK, axis=2).reshape(B_, G, HPG, NSA_QBLOCK, D)
        sc = jnp.einsum('bghqd,bgnd->bghqn', qb, kc, preferred_element_type=jnp.float32)
        p_c = masked_softmax(sc, cmp_end[None, :] <= t[:, None])
        o_c = jnp.einsum('bghqn,bgnd->bghqd', p_c, vc)
        imp = jnp.einsum('bghqn,nj->bgqj', p_c, overlap)
        cur = t[:, None] // SEL_BLOCK
        valid = sel_id[None, :] <= cur
        forced = (sel_id[None, :] == 0) | (sel_id[None, :] == cur) | (sel_id[None, :] == cur - 1)
        score = jnp.where(valid, jnp.where(forced, jnp.inf, imp), -jnp.inf)
        _, idx = lax.top_k(score, n_top)
        ksel = ks_blk[bi, gi, idx].reshape(B_, G, NSA_QBLOCK, n_top * SEL_BLOCK, D)
        vsel = vs_blk[bi, gi, idx].reshape(B_, G, NSA_QBLOCK, n_top * SEL_BLOCK, D)
        kpos = (idx[..., None] * SEL_BLOCK + jnp.arange(SEL_BLOCK)).reshape(B_, G, NSA_QBLOCK, -1)
        ss = jnp.einsum('bghqd,bgqkd->bghqk', qb, ksel, preferred_element_type=jnp.float32)
        p_s = masked_softmax(ss, (kpos <= t[:, None])[:, :, None])
        o_s = jnp.einsum('bghqk,bgqkd->bghqd', p_s, vsel)
        kwb = lax.dynamic_slice_in_dim(kw_pad, s, WINDOW + NSA_QBLOCK, axis=2)
        vwb = lax.dynamic_slice_in_dim(vw_pad, s, WINDOW + NSA_QBLOCK, axis=2)
        kp = s - WINDOW + jnp.arange(WINDOW + NSA_QBLOCK)
        wmask = (kp[None, :] >= 0) & (kp[None, :] <= t[:, None]) & (kp[None, :] > t[:, None] - WINDOW)
        sw = jnp.einsum('bghqd,bgkd->bghqk', qb, kwb, preferred_element_type=jnp.float32)
        p_w = masked_softmax(sw, wmask)
        o_w = jnp.einsum('bghqk,bgkd->bghqd', p_w, vwb)
        gb = lax.dynamic_slice_in_dim(gates, s, NSA_QBLOCK, axis=2).reshape(B_, G, HPG, NSA_QBLOCK, 3)
        o = gb[..., 0:1] * o_c + gb[..., 1:2] * o_s + gb[..., 2:3] * o_w
        return o.reshape(B_, H, NSA_QBLOCK, D)

    o = lax.map(q_block, jnp.arange(T_ // NSA_QBLOCK))
    return o.transpose(1, 0, 3, 2, 4).reshape(B_, T_, H * D)

def setup_inputs(seed: int = 0) -> dict:
    key = jax.random.key(seed)
    keys = iter(jax.random.split(key, 40))

    def nrm(shape, scale):
        return jax.random.normal(next(keys), shape, jnp.float32) * scale

    def gain(shape):
        return 1.0 + 0.05 * jax.random.normal(next(keys), shape, jnp.float32)

    def unif(shape, lo, hi):
        return jax.random.uniform(next(keys), shape, jnp.float32, lo, hi)

    E, O = N_EVEN, N_ODD
    x = nrm((BATCH, SEQ, D_MODEL), 1.0)
    positions = (jax.random.randint(next(keys), (BATCH, 1), 0, 1024, dtype=jnp.int32)
                 + jnp.arange(SEQ, dtype=jnp.int32)[None, :])
    dt = jnp.exp(unif((E, GDN_HEADS), math.log(1e-3), math.log(1e-1)))
    return {
        'x': x,
        'positions': positions,
        'norm_mix_pre': gain((DEPTH, D_MODEL)),
        'norm_mix_post': gain((DEPTH, D_MODEL)),
        'norm_ffn_pre': gain((DEPTH, D_MODEL)),
        'norm_ffn_post': gain((DEPTH, D_MODEL)),
        'w_ffn_up': nrm((DEPTH, D_MODEL, D_FF), D_MODEL ** -0.5),
        'w_ffn_down': nrm((DEPTH, D_FF, D_MODEL), D_FF ** -0.5),
        'ab_w_in': nrm((E, D_MODEL, AB_IN_W), D_MODEL ** -0.5),
        'ab_w_out': nrm((E, AB_OUT_W, D_MODEL), AB_OUT_W ** -0.5),
        'gdn_conv': nrm((E, GDN_CONV, GDN_CONV_W), GDN_CONV ** -0.5),
        'gdn_a_log': jnp.log(unif((E, GDN_HEADS), 1.0, 16.0)),
        'gdn_dt_bias': dt + jnp.log(-jnp.expm1(-dt)),
        'gdn_norm': gain((E, GDN_DV)),
        'rwkv_mu': unif((E, RWKV_IN_W), 0.0, 1.0),
        'rwkv_w0': unif((E, RWKV_W), -6.0, -1.0),
        'rwkv_w2': nrm((E, RWKV_DECAY_LORA, RWKV_W), 0.5 * RWKV_DECAY_LORA ** -0.5),
        'rwkv_a0': nrm((E, RWKV_W), 0.1),
        'rwkv_a2': nrm((E, RWKV_AAA_LORA, RWKV_W), 0.5 * RWKV_AAA_LORA ** -0.5),
        'rwkv_g2': nrm((E, RWKV_GATE_LORA, RWKV_W), RWKV_GATE_LORA ** -0.5),
        'rwkv_k_k': 0.85 + nrm((E, RWKV_W), 0.05),
        'rwkv_k_a': gain((E, RWKV_W)),
        'rwkv_r_k': nrm((E, RWKV_HEADS, RWKV_N), 0.1),
        'rwkv_ln_w': gain((E, RWKV_W)),
        'rwkv_ln_b': nrm((E, RWKV_W), 0.01),
        'nsa_w_in': nrm((O, D_MODEL, NSA_IN_W), D_MODEL ** -0.5),
        'nsa_w_out': nrm((O, NSA_OUT_W, D_MODEL), NSA_OUT_W ** -0.5),
        'nsa_pe_k': nrm((O, CMP_LEN, NSA_HD), 0.1),
        'nsa_w1_k': nrm((O, CMP_LEN * NSA_HD, CMP_HIDDEN), (CMP_LEN * NSA_HD) ** -0.5),
        'nsa_w2_k': nrm((O, CMP_HIDDEN, NSA_HD), CMP_HIDDEN ** -0.5),
        'nsa_pe_v': nrm((O, CMP_LEN, NSA_HD), 0.1),
        'nsa_w1_v': nrm((O, CMP_LEN * NSA_HD, CMP_HIDDEN), (CMP_LEN * NSA_HD) ** -0.5),
        'nsa_w2_v': nrm((O, CMP_HIDDEN, NSA_HD), CMP_HIDDEN ** -0.5),
    }

def reference(x, positions, norm_mix_pre, norm_mix_post, norm_ffn_pre, norm_ffn_post,
              w_ffn_up, w_ffn_down, ab_w_in, ab_w_out, gdn_conv, gdn_a_log, gdn_dt_bias,
              gdn_norm, rwkv_mu, rwkv_w0, rwkv_w2, rwkv_a0, rwkv_a2, rwkv_g2, rwkv_k_k,
              rwkv_k_a, rwkv_r_k, rwkv_ln_w, rwkv_ln_b, nsa_w_in, nsa_w_out, nsa_pe_k,
              nsa_w1_k, nsa_w2_k, nsa_pe_v, nsa_w1_v, nsa_w2_v):
    h = x
    for layer in range(DEPTH):
        u = rmsnorm(h, norm_mix_pre[layer])
        j = layer // 2
        if layer % 2 == 0:
            f = (u @ ab_w_in[j]).astype(jnp.float32)
            o_a = gdn_mixer(f[..., :GDN_W], gdn_conv[j], gdn_a_log[j], gdn_dt_bias[j], gdn_norm[j])
            o_b = rwkv7_mixer(f[..., GDN_W:], rwkv_mu[j], rwkv_w0[j], rwkv_w2[j], rwkv_a0[j],
                              rwkv_a2[j], rwkv_g2[j], rwkv_k_k[j], rwkv_k_a[j], rwkv_r_k[j],
                              rwkv_ln_w[j], rwkv_ln_b[j])
            mix = jnp.concatenate([o_a, o_b], axis=-1).astype(h.dtype) @ ab_w_out[j]
        else:
            f = u @ nsa_w_in[j]
            o_c = nsa_mixer(f, positions, nsa_pe_k[j], nsa_w1_k[j], nsa_w2_k[j],
                            nsa_pe_v[j], nsa_w1_v[j], nsa_w2_v[j])
            mix = o_c.astype(h.dtype) @ nsa_w_out[j]
        h = h + rmsnorm(mix, norm_mix_post[layer])
        u = rmsnorm(h, norm_ffn_pre[layer])
        ff = jnp.square(jax.nn.relu(u @ w_ffn_up[layer])) @ w_ffn_down[layer]
        h = h + rmsnorm(ff, norm_ffn_post[layer])
    return h


_drawn_inputs = setup_inputs


def setup_inputs(seed=0):
    import zlib

    import numpy as np

    out = dict(_drawn_inputs(seed))
    spreads = {}
    factors = {'rwkv_w2': 4.991, 'rwkv_a0': 2.697, 'rwkv_k_k': 2.682, 'rwkv_ln_b': 7.624, 'nsa_pe_k': 8.0}
    for name, (base, spread) in spreads.items():
        noise = np.random.default_rng([zlib.crc32(name.encode()), seed]).standard_normal(out[name].shape)
        drawn = base * np.exp(spread * noise) if base else spread * noise
        out[name] = __import__('jax').numpy.asarray(drawn.astype(out[name].dtype))
    for name, factor in factors.items():
        out[name] = (out[name] * factor).astype(out[name].dtype)
    return out
```

```python
from contextlib import ExitStack

import numpy as np

import concourse.bass as bass
from concourse import mybir

F32 = mybir.dt.float32
F32R = mybir.dt.float32r
I32 = mybir.dt.int32
ALU = mybir.AluOpType
ACT = mybir.ActivationFunctionType
AX = mybir.AxisListType

P = 128
T = 512
NT = T // P
D = 1024
KD = D // P
FF = 4096
NF = FF // P
RING = 4
GH, RH = 4, 8
RP = RH // 2
PAD = 4
EPS = 1e-6
LN_EPS = 64e-5
QH, KG, HD = 16, 2, 64
HPG = QH // KG
NCMP = 32
HALF = 8
LEVELS = 7

C_IN0 = 0
N_IN0 = 30
C_OUT0 = 32
C_MLP0 = 40
C_IN1 = 104
C_CMP = 120
C_OUT1 = 128
C_MLP1 = 136
N_CHUNK = 200


def columns(parts):
    at, off = 0, {}
    for name, n in parts:
        off[name] = (at, at + n)
        at += n
    return off, at


CONST_PARTS = [("ident", P), ("ones", P), ("strict", P), ("incl", P), ("bones", P), ("cum", 2 * P + 2),
               ("level", LEVELS * P), ("level0t", P), ("neg", P), ("cmask", NT * NCMP), ("cneg", NT * NCMP),
               ("ifreq", HALF), ("hsel", 4), ("eps", 4)]
C_OFF, C_N = columns(CONST_PARTS)
PAR_PARTS = [("conv", 48), ("gnorm", 1), ("mu", 14),
             ("k_k", 4), ("k_a", 4), ("r_k", 4), ("a0", 4), ("pe_k", 16), ("pe_v", 16), ("ba", 64),
             ("w2a2", 512), ("g2", 512), ("w2k", 128), ("w2v", 128), ("alog", 4), ("dtb", 4), ("w0", 512)]
P_OFF, P_N = columns(PAR_PARTS)


def constants():
    c = np.zeros((P, C_N), np.float32)

    def put(name, a):
        lo, hi = C_OFF[name]
        c[:, lo:hi] = np.asarray(a, np.float32).reshape(P, hi - lo)

    r, q = np.arange(P)[:, None], np.arange(P)[None, :]
    put("ident", r == q)
    put("ones", np.ones((P, P)))
    put("strict", r < q)
    put("incl", r <= q)
    put("bones", (r // 64) == (q // 64))
    half = (r < 64).astype(np.float32)
    cum = np.concatenate([(r < q) - half, (r <= q) - half, half, 1 - half], 1) * -np.exp(np.float32(-0.5))
    put("cum", cum)
    lev = [((r // (2 * b)) == (q // (2 * b))) & ((r // b) % 2 == 1) & ((q // b) % 2 == 0)
           for b in (1 << i for i in range(LEVELS))]
    put("level", np.stack(lev, 1))
    put("level0t", lev[0].T)
    put("neg", np.where(q > r, -1e30, 0.0))
    t = np.arange(NT)[None, :, None] * P + np.arange(P)[:, None, None]
    n = np.arange(NCMP)[None, None, :]
    ok = (16 * n + 31 <= t) & (n < NCMP - 1)
    put("cmask", ok)
    put("cneg", np.where(ok, 0.0, -1e30))
    put("ifreq", np.broadcast_to(np.float32(500000.0) ** (-np.arange(HALF, dtype=np.float32) * np.float32(2.0 / 16)), (P, HALF)))
    put("hsel", (r // 32) == np.arange(4)[None, :])
    put("eps", np.broadcast_to(np.array([EPS, LN_EPS, 0.0, 0.0]), (P, 4)))
    return c


class Chain:

    def __init__(self, eng, sem):
        self.e, self.sem, self.base, self.n = eng, sem, 0, 0

    def link(self, ins):
        ins.then_inc(self.sem, 1)
        self.n += 1
        self.e.wait_ge(self.sem, self.base + self.n)

    def sig(self, ins, sem, value):
        ins.then_inc(sem, 1)
        self.e.wait_ge(sem, value)

    def hold(self, spare):
        self.e.tensor_tensor(spare, spare, spare, ALU.add)

    def enter(self, i, per):
        self.start, self.per = self.base + self.n, per
        self.base, self.n = self.start + i * per, 0

    def leave(self, times):
        assert self.n == self.per, f"links in the loop: {self.n}, declared {self.per}"
        self.base, self.n = self.start + self.per * times, 0


DVE_LINKS, ACT_LINKS, POOL_LINKS = 44, 13, 5


def program(nc, wstream, x, pos, params, consts, rows, out):
    with ExitStack() as ctx:
        sems = {}

        def sem(name):
            if name not in sems:
                sems[name] = ctx.enter_context(nc.semaphore(name))
            return sems[name]

        def sb(name, shape, dt=F32, c=ctx):
            return c.enter_context(nc.sbuf_tensor(name, shape, dt))

        bank = [ctx.enter_context(nc.psum_tensor(f"bank{i}", [P, 512], F32)) for i in range(8)]
        ring = sb("ring", [P, RING, D])
        con = sb("con", [P, C_N])
        par = sb("par", [P, P_N])
        xres = sb("xres", [P, NT, D])
        rowbuf = sb("rowbuf", [P, D])
        spare = sb("spare", [P, 1])
        st = sb("st", [P, 32])

        def C(name):
            return con[:, C_OFF[name][0]:C_OFF[name][1]]

        def PR(name):
            return par[:, P_OFF[name][0]:P_OFF[name][1]]

        ident, ones, incl, bones = C("ident"), C("ones"), C("incl"), C("bones")
        eps = C("eps")[:, 0:1]
        ln_eps = C("eps")[:, 1:2]
        x_d = x.rearrange("(i p) d -> p i d", p=P)
        out_d = out.rearrange("(i p) d -> p i d", p=P)


        def dense(c, tag):
            return [sb(f"{n}{tag}", [P, k, w], F32R, c=c) for n, k, w in
                    (("uh", KD, T), ("ul", KD, T), ("wh", RING, D), ("wl", RING, D))]

        l0 = ExitStack()
        fT = sb("fT", [P, 26, PAD + T], c=l0)
        z = sb("z", [P, NT, 512], c=l0)
        lws = sb("lws", [P, NT, 512], c=l0)
        gst = sb("gst", [P, 4, 16], c=l0)
        gs = sb("gs", [P, NT, 7, GH], c=l0)
        QB, KB, VB, RB, KRB, VRB, WA, GD = 0, 4, 8, 12, 16, 20, 24, 25
        bonus = sb("bonus", [P, NT, RH], c=l0)
        l0p = ExitStack()
        D0 = dense(l0p, "0")
        utok0 = sb("utok0", [P, 2, D], c=l0p)
        bah = sb("bah", [P, 8 * KD], F32R, c=l0p)
        bal = sb("bal", [P, 8 * KD], F32R, c=l0p)
        l0p.close()
        kkT = sb("kkT", [P, 4, T], c=l0)
        aT = sb("aT", [P, 4, T], c=l0)
        l0s = ExitStack()
        tmpc = sb("tmpc", [P, 2, T], c=l0s)
        tmpd = sb("tmpd", [P, 2, T], c=l0s)
        sq = sb("sq", [P, 2, T], c=l0s)
        rt = sb("rt", [P, 12, T], c=l0s)
        rk = sb("rk", [P, 4, T], c=l0s)
        l0s.close()
        l0t = ExitStack()
        exq = sb("exq", [P, RP, 2 * P + 2], c=l0t)
        exn = sb("exn", [P, RP, P], c=l0t)
        RA = sb("RA", [P, RP, 2, P], c=l0t)
        NB = sb("NB", [P, RP, P], c=l0t)
        KT = sb("KT", [P, RP, P], c=l0t)
        KTt = sb("KTt", [P, RP, P], c=l0t)
        Vt = sb("Vt", [P, RP, P], c=l0t)
        Xb = sb("Xb", [P, 3, 4, P], c=l0t)
        Ti = sb("Ti", [P, 3, 4, P], c=l0t)
        TTi = sb("TTi", [P, 3, 4, P], c=l0t)
        KQ = sb("KQ", [P, GH, 2, P], c=l0t)
        vG = sb("vG", [P, GH, P], c=l0t)
        vR = sb("vR", [P, RP, P], c=l0t)
        lwt = sb("lwt", [P, 512], c=l0t)
        gB = sb("gB", [P, GH, P], c=l0t)
        Dn = sb("Dn", [P, GH, P], c=l0t)
        Ds = sb("Ds", [P, GH, P], c=l0t)
        kdt = sb("kdt", [P, GH, P], c=l0t)
        vGt = sb("vGt", [P, GH, P], c=l0t)
        S = sb("S", [P, GH, P], c=l0t)
        Sr = sb("Sr", [P, RP, P], c=l0t)
        sm = sb("sm", [P, 7, GH], c=l0t)
        VV, VN, O1, Wb, NBt = gB, vG, lwt, vR, exn
        Ub = vGt[:, :, :].rearrange("p a c -> p (a c)")
        SC = xres[:, :, :].rearrange("p a (b c) -> p (a b) c", b=2)
        l0t.close()
        l0m = ExitStack()
        o_n = sb("o_n", [P, NT, 512], c=l0m)
        y_n = sb("y_n", [P, NT, 512], c=l0m)
        t1 = sb("t1", [P, NT, 512], c=l0m)
        hst = sb("hst", [P, 8, NT, RH], c=l0m)
        l0m.close()
        l0.close()
        ml = ExitStack()
        HF = NF // 2
        mh = ExitStack()
        hh = sb("hh", [P, HF, T], F32R, c=mh)
        hl = sb("hl", [P, HF, T], F32R, c=mh)
        mh.close()
        utok = sb("utok", [P, 2, D], c=ml)
        sb("rest", [P, 2 * HF * T - 2 * D], c=ml)
        wh_m, wl_m = (sb(n, [P, RING, D], F32R, c=ml) for n in ("wh_m", "wl_m"))
        ffo = sb("ffo", [P, NT, D], c=ml)
        prerow = sb("prerow", [P, D], c=ml)
        uh_m, ul_m = (sb(n, [P, KD, T], F32R, c=ml) for n in ("uh_m", "ul_m"))
        DM = [uh_m, ul_m, wh_m, wl_m]
        hraw = sb("hraw", [P, 2, T], c=ml)
        ml.close()


        def meet(eng, n):
            eng.drain().then_inc(sem("stage_done"), 1)
            eng.wait_ge(sem("stage_done"), 4 * n)

        slot_sems = [sem(f"w_loaded{s}") for s in range(RING)]

        def slot(c):
            return ring[:, c % RING, :]

        def stream(sp):
            for c in range(RING):
                sp.dma_start(slot(c), wstream[c]).then_inc(slot_sems[c], 16)
            with sp.Fori(0, N_CHUNK // RING - 1) as it:
                for c in range(RING):
                    sp.wait_ge(sem("w_lo"), it * RING + c + 1)
                    sp.dma_start(slot(c), wstream[bass.ds(it * RING + RING + c, 1)].rearrange("a p d -> (a p) d")).then_inc(slot_sems[c], 16)

        def split_hi(a, dn, c, it=0, per=0):
            a.e.wait_ge(slot_sems[c % RING], it * (16 * per // RING) + 16 * (c // RING + 1))
            a.e.wait_ge(sem("w_used"), it * per + c + 1)
            a.sig(a.e.activation(dn[2][:, c % RING, :], slot(c), ACT.Copy), sem("w_hi"), it * per + c + 1)

        def used(eng, c, it=0, per=0):
            eng.wait_ge(sem("w_used"), it * per + (c + 1 + RING))

        def split_lo(v, dn, c, it=0, per=0):
            v.e.wait_ge(sem("w_hi"), it * per + c + 1)
            v.sig(v.e.tensor_tensor(dn[3][:, c % RING, :], slot(c), dn[2][:, c % RING, :].bitcast(F32), ALU.subtract), sem("w_lo"), it * per + c + 1)

        def weights(pe, c, it=0, per=0):
            pe.wait_ge(sem("w_lo"), it * per + c + 1)

        def mm3(pe, out, lh, ll, rh, rl, start, stop):
            pe.matmul(out, lh, rh, start=start, stop=False)
            pe.matmul(out, lh, rl, start=False, stop=False)
            return pe.matmul(out, ll, rh, start=False, stop=stop)

        NORM_TURN = (0, 2, 3, 5)

        def norm_pe(pe, c, ut):
            if c % 2:
                pe.wait_ge(sem("ffo_left"), 4 * (c // 2) + 4)
                pe.wait_ge(sem("ffo_right"), 4 * (c // 2) + 4)
            for i in range(NT):
                pe.wait_ge(sem("norm_u"), 4 * c + i + 1)
                for k in range(KD):
                    ins = pe.transpose(bank[2 * i + k // 4][:, (k % 4) * P:(k % 4 + 1) * P],
                                       ut[:, i % 2, k * P:(k + 1) * P], ident)
                ins.then_inc(sem("turned"), 1)

        def turned(dn, i, h):
            v = (slice(None), slice(4 * h, 4 * h + 4), slice(i * P, (i + 1) * P))
            return dn[0][v], dn[1][v], bank[2 * i + h][:, :].rearrange("p (k t) -> p k t", k=4)

        def norm_act(a, c, dn, ut):
            def high(i):
                a.e.wait_ge(sem("turned"), 4 * NORM_TURN[c] + i + 1)
                for h in range(2):
                    hi, _, src = turned(dn, i, h)
                    a.sig(a.e.activation(hi, src, ACT.Copy), sem("high_done"), 8 * NORM_TURN[c] + 2 * i + h + 1)
            for i in range(NT):
                if c > 0:
                    a.e.wait_ge(sem("x_updated"), 4 * (c - 1) + i + 1)
                if i >= 2:
                    a.e.wait_ge(sem("turned"), 4 * NORM_TURN[c] + i - 1)
                a.link(a.e.activation(ut[:, i % 2, :], xres[:, i, :], ACT.Square, accum_out=st[:, i:i + 1]))
                a.sig(a.e.activation(st[:, 4 + i:5 + i], st[:, i:i + 1], ACT.Sqrt, bias=eps, scale=1.0 / D),
                      sem("norm_root"), 4 * c + i + 1)
                if i >= 1:
                    high(i - 1)
            high(NT - 1)

        def norm_dve(v, c, dn, ut, row):
            def low(i):
                for h in range(2):
                    hi, lo, src = turned(dn, i, h)
                    v.e.wait_ge(sem("high_done"), 8 * NORM_TURN[c] + 2 * i + h + 1)
                    v.link(v.e.tensor_tensor(lo, src, hi.bitcast(F32), ALU.subtract))
            v.e.wait_ge(sem("pre_loaded"), 16 * (c + 1))
            for i in range(NT):
                v.e.wait_ge(sem("norm_root"), 4 * c + i + 1)
                v.link(v.e.reciprocal(st[:, 8 + i:9 + i], st[:, 4 + i:5 + i]))
                v.sig(v.e.scalar_tensor_tensor(ut[:, i % 2, :], xres[:, i, :], st[:, 8 + i:9 + i], row[:, :], ALU.mult, ALU.mult),
                      sem("norm_u"), 4 * c + i + 1)
                if i >= 1:
                    low(i - 1)
            low(NT - 1)

        def pre_in(act, c, row):
            act.dma_start(row[:, :], rows[5 + c:6 + c, :].to_broadcast([P, D])).then_inc(sem("pre_loaded"), 16)

        def post_act(a, c):
            for i in range(NT):
                if i >= 2:
                    a.e.wait_ge(sem("post_root"), 4 * c + i - 1)
                a.link(a.e.activation(utok[:, i % 2, :], ffo[:, i, :], ACT.Square, accum_out=st[:, 16 + i:17 + i]))
                a.sig(a.e.activation(st[:, 20 + i:21 + i], st[:, 16 + i:17 + i], ACT.Sqrt, bias=eps, scale=1.0 / D),
                      sem("post_root"), 4 * c + i + 1)

        def post_dve(v, c):
            v.e.wait_ge(sem("row_loaded"), 16 * (c + 1))
            for i in range(NT):
                v.e.wait_ge(sem("post_root"), 4 * c + i + 1)
                v.link(v.e.reciprocal(st[:, 24 + i:25 + i], st[:, 20 + i:21 + i]))
                v.link(v.e.scalar_tensor_tensor(ffo[:, i, :], ffo[:, i, :], st[:, 24 + i:25 + i], rowbuf[:, :],
                                                ALU.mult, ALU.mult))
                v.sig(v.e.tensor_tensor(xres[:, i, :], xres[:, i, :], ffo[:, i, :], ALU.add),
                      sem("x_updated"), 4 * c + i + 1)

        N_LOOP, BODY, NTB = 3, 8, 26

        def proj0_pe(pe):
            uh, ul, wh, wl = D0

            def blk(c, b, it, per, wait):
                weights(pe, c, it, per)
                pe.wait_ge(sem("fT_even" if b % 2 == 0 else "fT_odd"), wait)
                for k in range(KD):
                    w = slice(k * P, (k + 1) * P)
                    ins = mm3(pe, bank[b][:, :], wh[:, c % RING, w], wl[:, c % RING, w], uh[:, k, :], ul[:, k, :], k == 0, k == KD - 1)
                ins.then_inc(sem("w_used"), 1)
            with pe.Fori(0, N_LOOP) as it:
                for s in range(BODY):
                    blk(s, s, it, BODY, it * 4 + s // 2 + 1)
            for b in range(2):
                blk(24 + b, b, 0, 0, N_LOOP * 4 + 1)
            for nm in ("fT_even", "fT_odd"):
                pe.wait_ge(sem(nm), N_LOOP * 4 + 4)
            for c in range(NTB, N_IN0):
                weights(pe, c)
                for kk in range(2):
                    k = 2 * (c - NTB) + kk
                    for i in range(NT):
                        t, w = slice(i * P, (i + 1) * P), slice(kk * 512, (kk + 1) * 512)
                        ins = mm3(pe, bank[4 + i][:, :], uh[:, k, t], ul[:, k, t], wh[:, c % RING, w], wl[:, c % RING, w], k == 0, k == KD - 1)
                ins.then_inc(sem("w_used"), 1)
            pe.wait_ge(sem("ba_lo"), 1)
            for i in range(NT):
                for k in range(KD):
                    t, w = slice(i * P, (i + 1) * P), slice(8 * k, 8 * k + 8)
                    ins = mm3(pe, bank[2][:, 8 * i:8 * i + 8], uh[:, k, t], ul[:, k, t], bah[:, w], bal[:, w], k == 0, k == KD - 1)
            ins.then_inc(sem("zba_ready"), 1)
            for c in (30, 31):
                pass_over(pe, c)
                pe.sem_inc(sem("w_used"), 1)

        def pass_over(pe, c):
            pe.wait_ge(slot_sems[c % RING], 16 * (c // RING + 1))
            pe.wait_ge(sem("w_lo"), c)
            for nm in ("w_hi", "w_lo"):
                pe.sem_inc(sem(nm), 1)

        def proj0_dve(v):
            v.e.sem_inc(sem("fT_even"), 4)
            v.e.wait_ge(sem("ba_hi"), 1)
            v.sig(v.e.tensor_tensor(bal[:, :], PR("ba"), bah[:, :].bitcast(F32), ALU.subtract), sem("ba_lo"), 1)
            with v.e.Fori(0, N_LOOP) as it:
                for s in range(2):
                    split_lo(v, D0, s, it, BODY)
                for s in range(BODY):
                    if s + 2 < BODY:
                        split_lo(v, D0, s + 2, it, BODY)
                    if s % 2 == 0:
                        used(v.e, s, it, BODY)
                        v.sig(v.e.tensor_scalar(fT[:, bass.ds(it * BODY + s, 1), PAD:].rearrange("p a t -> p (a t)"), bank[s][:, :], 1.0, None, ALU.mult),
                              sem("fT_even"), it * 4 + 4 + s // 2 + 1)
            for c in range(24, N_IN0):
                split_lo(v, D0, c)
                if c == 26:
                    used(v.e, 24)
                    v.link(v.e.tensor_copy(fT[:, 24, PAD:], bank[0][:, :]))
            v.e.wait_ge(sem("zba_ready"), 1)
            for i in range(0, NT, 2):
                v.link(v.e.tensor_copy(z[:, i, :], bank[4 + i][:, :]))
            ba = bank[2][:, 0:32].rearrange("p (i c) -> p i c", i=NT)
            v.link(v.e.tensor_copy(gst[:, 0, :].rearrange("p (i c) -> p i c", i=NT), ba[:, :, 0:4]))
            v.link(v.e.tensor_tensor(gst[:, 1, :].rearrange("p (i c) -> p i c", i=NT), ba[:, :, 4:8],
                                     PR("dtb").unsqueeze(1).to_broadcast([P, NT, GH]), ALU.add))

        def proj0_act(a):
            a.e.sem_inc(sem("fT_odd"), 4)
            a.sig(a.e.activation(bah[:, :], PR("ba"), ACT.Copy), sem("ba_hi"), 1)
            with a.e.Fori(0, N_LOOP) as it:
                for s in range(2):
                    split_hi(a, D0, s, it, BODY)
                for s in range(BODY):
                    if s + 2 < BODY:
                        split_hi(a, D0, s + 2, it, BODY)
                    if s % 2 == 1:
                        used(a.e, s, it, BODY)
                        a.sig(a.e.activation(fT[:, bass.ds(it * BODY + s, 1), PAD:].rearrange("p a t -> p (a t)"), bank[s][:, :], ACT.Copy),
                              sem("fT_odd"), it * 4 + 4 + s // 2 + 1)
            for c in range(24, N_IN0):
                split_hi(a, D0, c)
                if c == 27:
                    used(a.e, 25)
                    a.link(a.e.activation(fT[:, 25, PAD:], bank[1][:, :], ACT.Copy))
            a.e.wait_ge(sem("zba_ready"), 1)
            for i in range(1, NT, 2):
                a.link(a.e.activation(z[:, i, :], bank[4 + i][:, :], ACT.Copy))

        def F(b):
            return fT[:, b, PAD:]

        def elem0_pool(g):
            for j in range(14):
                if j >= 2:
                    g.e.wait_ge(sem("shifted"), j - 1)
                b = RB + j
                g.sig(g.e.tensor_tensor(tmpd[:, j % 2, :], fT[:, b, PAD - 1:PAD - 1 + T], F(b), ALU.subtract), sem("diff"), j + 1)

        def elem0_dve(v):
            for j in range(14):
                v.e.wait_ge(sem("diff"), j + 1)
                v.sig(v.e.scalar_tensor_tensor(F(RB + j), tmpd[:, j % 2, :], PR("mu")[:, j:j + 1], F(RB + j), ALU.mult, ALU.add),
                      sem("shifted"), j + 1)
            for b in range(12):
                if b >= 2:
                    v.e.wait_ge(sem("silu"), b - 1)
                cw = PR("conv")[:, 4 * b:4 * b + 4]
                acc = tmpc[:, b % 2, :]
                v.link(v.e.tensor_scalar(acc, fT[:, b, 1:1 + T], cw[:, 0:1], None, ALU.mult))
                for i in range(1, 3):
                    v.link(v.e.scalar_tensor_tensor(acc, fT[:, b, 1 + i:1 + i + T], cw[:, i:i + 1], acc, ALU.mult, ALU.add))
                v.sig(v.e.scalar_tensor_tensor(acc, fT[:, b, 4:4 + T], cw[:, 3:4], acc, ALU.mult, ALU.add), sem("conv_done"), b + 1)
            for b in range(4):
                v.sig(v.e.tensor_scalar(kkT[:, b, :], F(KRB + b), PR("k_k")[:, b:b + 1], None, ALU.mult), sem("kk_raw"), b + 1)
            v.e.wait_ge(sem("a_done"), 4)
            for b in range(4):
                v.link(v.e.tensor_scalar(rk[:, b, :], aT[:, b, :], -1.0, PR("k_a")[:, b:b + 1], ALU.add, ALU.mult))
                v.link(v.e.scalar_tensor_tensor(F(KRB + b), rk[:, b, :], 1.0, F(KRB + b), ALU.add, ALU.mult))
                v.sig(v.e.scalar_tensor_tensor(rk[:, b, :], F(RB + b), PR("r_k")[:, b:b + 1], F(KRB + b), ALU.mult, ALU.mult),
                      sem("rk_done"), b + 1)
            for j in range(12):
                v.e.wait_ge(sem("root"), j + 1)
                v.link(v.e.reciprocal(rt[:, j, :], rt[:, j, :]))
                if j < 4:
                    v.link(v.e.scalar_tensor_tensor(F(j), F(j), float(P) ** -0.5, rt[:, j, :], ALU.mult, ALU.mult))
                elif j < 8:
                    v.link(v.e.tensor_tensor(F(j), F(j), rt[:, j, :], ALU.mult))
                else:
                    b = j - 8
                    v.link(v.e.tensor_tensor(kkT[:, b, :], kkT[:, b, :], rt[:, j, :], ALU.mult))
                    v.link(v.e.scalar_tensor_tensor(aT[:, b, :], kkT[:, b, :], -1.0, aT[:, b, :], ALU.mult, ALU.mult))
            v.e.wait_ge(sem("bonus_ready"), 1)
            v.link(v.e.tensor_copy(bonus[:, :, :], bank[6][:, 0:NT * RH].rearrange("p (i h) -> p i h", i=NT)))
            v.e.wait_ge(sem("gate_ln"), 1)
            v.link(v.e.scalar_tensor_tensor(gst[:, 2, :], gst[:, 1, :], 0.0, gst[:, 2, :], ALU.max, ALU.add))
            v.e.wait_ge(sem("gate_a"), 1)
            sp = gst[:, 2, :].rearrange("p (i h) -> p i h", i=NT)
            g3 = gst[:, 3, 0:4].unsqueeze(1).to_broadcast([P, NT, GH])
            v.link(v.e.tensor_tensor(sp, sp, g3, ALU.mult))
            v.sig(v.e.tensor_scalar(gs[:, :, 0, :], sp, -1.0, None, ALU.mult), sem("g_done"), 1)
            v.link(v.e.tensor_copy(gs[:, :, 3, :], gst[:, 0, :].rearrange("p (i h) -> p i h", i=NT)))
            v.link(v.e.tensor_scalar(gs[:, :, 6, :], gst[:, 0, :].rearrange("p (i h) -> p i h", i=NT), -1.0, None, ALU.mult))
            v.e.wait_ge(sem("gc_ready"), 1)
            gc = bank[7][:, 0:16].rearrange("p (i h) -> p i h", i=NT)
            gt = bank[7][:, 16:32].rearrange("p (i h) -> p i h", i=NT)
            v.link(v.e.tensor_copy(gs[:, :, 1, :], gc))
            v.link(v.e.tensor_copy(gs[:, :, 5, :], gt))
            v.sig(v.e.tensor_tensor(gs[:, :, 4, :], gs[:, :, 5, :], gs[:, :, 1, :], ALU.subtract), sem("gc_sb"), 1)
            v.e.wait_ge(sem("gexp_done"), 1)
            v.link(v.e.tensor_scalar(gs[:, :, 2, :], gs[:, :, 2, :], -1.0, None, ALU.mult))

        def elem0_act(a):
            a.e.wait_ge(sem("shifted"), 14)
            a.sig(a.e.activation(fT[0:64, WA, PAD:], fT[0:64, WA, PAD:], ACT.Tanh), sem("wd_tanh"), 1)
            a.link(a.e.activation(F(GD), F(GD), ACT.Sigmoid))
            a.link(a.e.activation(gst[:, 0, :], gst[:, 0, :], ACT.Sigmoid))
            for b in range(4):
                a.e.wait_ge(sem("a_ready"), b + 1)
                a.sig(a.e.activation(aT[:, b, :], bank[b][:, :], ACT.Sigmoid, bias=PR("a0")[:, b:b + 1]), sem("a_done"), b + 1)
            for i in range(NT):
                a.e.wait_ge(sem("lw_ready"), i + 1)
                a.sig(a.e.activation(lws[:, i, :], bank[4 + i][:, :], ACT.Sigmoid), sem("lw_done"), i + 1)
            for b in range(12):
                a.e.wait_ge(sem("conv_done"), b + 1)
                a.sig(a.e.activation(F(b), tmpc[:, b % 2, :], ACT.Silu), sem("silu"), b + 1)
            for j in range(12):
                if j >= 8:
                    a.e.wait_ge(sem("kk_raw"), j - 7)
                if j >= 2:
                    a.e.wait_ge(sem("ss_ready"), j - 1)
                a.sig(a.e.activation(sq[:, j % 2, :], F(j) if j < 8 else kkT[:, j - 8, :], ACT.Square), sem("sq_done"), j + 1)
                if j >= 1:
                    root(a, j - 1)
            root(a, 11)
            a.link(a.e.activation(gst[:, 2, :], gst[:, 1, :], ACT.Abs))
            a.link(a.e.activation(gst[:, 2, :], gst[:, 2, :], ACT.Exp, scale=-1.0))
            a.sig(a.e.activation(gst[:, 2, :], gst[:, 2, :], ACT.Ln, bias=1.0), sem("gate_ln"), 1)
            a.sig(a.e.activation(gst[:, 3, 0:4], PR("alog"), ACT.Exp), sem("gate_a"), 1)
            a.e.wait_ge(sem("gc_sb"), 1)
            a.link(a.e.activation(gs[:, :, 2, :], gs[:, :, 1, :], ACT.Exp))
            a.link(a.e.activation(gs[:, :, 4, :], gs[:, :, 4, :], ACT.Exp))
            a.sig(a.e.activation(gs[:, :, 5, :], gs[:, :, 5, :], ACT.Exp), sem("gexp_done"), 1)

        def root(a, j):
            a.e.wait_ge(sem("ss_ready"), j + 1)
            a.sig(a.e.activation(rt[:, j, :], bank[j % 2][:, :], ACT.Sqrt, bias=eps), sem("root"), j + 1)

        def elem0_pe(pe):
            pe.wait_ge(sem("shifted"), 14)
            for b in range(4):
                pe.matmul(bank[b][:, :], PR("w2a2")[64:128, b * P:(b + 1) * P], fT[64:128, WA, PAD:],
                          start=True, stop=True).then_inc(sem("a_ready"), 1)
            pe.wait_ge(sem("wd_tanh"), 1)
            for i in range(NT):
                pe.matmul(bank[4 + i][:, :], fT[0:64, WA, PAD + i * P:PAD + (i + 1) * P], PR("w2a2")[0:64, :],
                          start=True, stop=False)
                pe.matmul(bank[4 + i][:, :], ones[0:1, :], PR("w0")[0:1, :], start=False, stop=True).then_inc(sem("lw_ready"), 1)
            pe.wait_ge(sem("a_done"), 4)
            for j in range(12):
                pe.wait_ge(sem("sq_done"), j + 1)
                if j >= 2:
                    pe.wait_ge(sem("root"), j - 1)
                pe.matmul(bank[j % 2][:, :], ones if j < 8 else bones, sq[:, j % 2, :], start=True, stop=True).then_inc(sem("ss_ready"), 1)
            pe.wait_ge(sem("rk_done"), 4)
            pe.wait_ge(sem("lw_done"), 4)
            for i in range(NT):
                for b in range(4):
                    ins = pe.matmul(bank[6][:, i * RH + 2 * b:i * RH + 2 * b + 2], rk[:, b, i * P:(i + 1) * P], bones[:, 0:P:64],
                                    start=True, stop=True)
            ins.then_inc(sem("bonus_ready"), 1)
            pe.wait_ge(sem("g_done"), 1)
            pe.matmul(bank[7][:, 0:16].rearrange("p (i h) -> p i h", i=NT), incl, gs[:, :, 0, :], start=True, stop=True)
            pe.matmul(bank[7][:, 16:32].rearrange("p (i h) -> p i h", i=NT), ones, gs[:, :, 0, :], start=True, stop=True).then_inc(sem("gc_ready"), 1)

        def AT(g, q):
            return Ds[:, q, :] if g == 0 else SC[:, 4 * (g - 1) + q, 0:P]

        def ATg(g):
            return Ds[:, :, :] if g == 0 else SC[:, 4 * (g - 1):4 * g, 0:P]

        BANK_A, BANK_B = (6, 0, 2), (7, 1, 3)
        X_PER, T_PER = 3 * (LEVELS - 1), 3 * LEVELS

        def tcol(n):
            return bass.ds(n * P + PAD, P)

        def b4(i):
            return bank[i][:, :].rearrange("p (h c) -> p h c", h=4)

        def rep4(m):
            return m.unsqueeze(1).to_broadcast([P, 4, P])

        def chunk_pool(g):
            e = g.e
            g.link(e.memset(S[:, :, :], 0.0))
            g.link(e.memset(Sr[:, :, :], 0.0))
            e.sem_inc(sem("state_init"), 1)
            with e.Fori(0, NT) as n:
                g.enter(n, POOL_LINKS)
                e.wait_ge(sem("state_done"), n + 1)
                g.hold(spare[:, :])
                e.tensor_copy(lwt[:, :], lws[:, bass.ds(n, 1), :].rearrange("p a c -> p (a c)")).then_inc(sem("lwt_in"), 1)
                e.tensor_copy(KQ[:, :, 0, :], fT[:, KB:KB + 4, tcol(n)])
                e.tensor_copy(KQ[:, :, 1, :], fT[:, QB:QB + 4, tcol(n)]).then_inc(sem("kq_in"), 1)
                e.tensor_copy(sm[:, :, :], gs[:, bass.ds(n, 1), :, :].rearrange("p a c h -> p (a c) h")).then_inc(sem("sm_in"), 1)
                e.tensor_copy(vG[:, :, :], fT[:, VB:VB + 4, tcol(n)]).then_inc(sem("vG_in"), 1)
                e.tensor_copy(vR[:, :, :], fT[:, VRB:VRB + 4, tcol(n)]).then_inc(sem("vR_in"), 1)
                e.wait_ge(sem("sm_in"), n + 1)
                g.hold(spare[:, :])
                e.tensor_copy(gB[:, :, :], sm[:, 0, :].unsqueeze(2).to_broadcast([P, GH, P])).then_inc(sem("gB_in"), 1)
                e.wait_ge(sem("d_exp"), n + 1)
                g.link(e.tensor_tensor(Ds[:, :, :], Dn[:, :, :], rep4(C("strict")), ALU.mult))
                g.sig(e.tensor_tensor(Dn[:, :, :], Dn[:, :, :], rep4(incl), ALU.mult), sem("d_masked"), n + 1)
                for q in range(3):
                    if q == 0:
                        e.wait_ge(sem("qk_masked"), n + 1)
                    else:
                        e.wait_ge(sem("sc_sb"), RH * n + 4 * q)
                    g.link(e.tensor_tensor(TTi[:, q], ATg(q), rep4(C("level0t")), ALU.mult))
                    g.sig(e.tensor_tensor(TTi[:, q], TTi[:, q], rep4(ident), ALU.add), sem("tt_init"), 3 * n + q + 1)
                e.wait_ge(sem("vrt_sb"), n + 1)
                g.hold(spare[:, :])
                g.link(e.tensor_copy(fT[:, VRB:VRB + 4, tcol(n)], Vt[:, :, :]))
                g.leave(NT)

        def chunk_pe(pe):
            def turn(src, dst, event):
                for q in range(4):
                    ins = pe.transpose(bank[dst][:, q * P:(q + 1) * P], src[:, q, :], ident)
                ins.then_inc(sem(event), 1)

            pe.wait_ge(sem("state_init"), 1)
            with pe.Fori(0, NT) as n:
                pe.wait_ge(sem("lwt_in"), n + 1)
                for b in range(RP):
                    pe.matmul(bank[b][:, 0:2 * P + 2], lwt[:, b * P:(b + 1) * P], C("cum"), start=True, stop=True).then_inc(sem("cum_ready"), 1)
                pe.wait_ge(sem("kq_in"), n + 1)
                for h in range(GH):
                    c = (h % 2) * 2 * P
                    ins = pe.matmul(bank[4 + h // 2][:, c:c + 2 * P].rearrange("p (a t) -> p a t", a=2), KQ[:, h, 0, :], KQ[:, h, :, :],
                                    start=True, stop=True)
                ins.then_inc(sem("kkq_ready"), 1)
                pe.wait_ge(sem("gB_in"), n + 1)
                for h in range(GH):
                    ins = pe.matmul(bank[6][:, h * P:(h + 1) * P], gB[:, h, :], incl, start=True, stop=True)
                ins.then_inc(sem("gbc_ready"), 1)
                pe.wait_ge(sem("vG_in"), n + 1)
                turn(vG, 7, "vg_turned")
                pe.wait_ge(sem("d_made"), n + 1)
                for h in range(GH):
                    ins = pe.matmul(bank[6][:, h * P:(h + 1) * P], KQ[:, h, 0, :], S[:, h, :], start=True, stop=True)
                ins.then_inc(sem("ks_ready"), 1)
                pe.wait_ge(sem("vgt_sb"), n + 1)
                for h in range(GH):
                    ins = pe.transpose(bank[7][:, h * P:(h + 1) * P], KQ[:, h, 0, :], ident)
                ins.then_inc(sem("k_turned"), 1)
                pe.wait_ge(sem("rk_ready"), n + 1)
                for h in range(RH):
                    p, r = h // 2, slice(64 * (h % 2), 64 * (h % 2) + 64)
                    if h < 4:
                        pe.wait_ge(sem("cum_read"), RP * n + h + 1)
                    else:
                        pe.wait_ge(sem("sc_sb"), RH * n + h - 3)
                    pe.matmul(bank[h % 4][:, 0:256], NB[r, p, :], RA[r, p].rearrange("p a t -> p (a t)"), start=True, stop=True)
                    pe.matmul(bank[h % 4][:, 256:512], KT[r, p, :], RA[r, p].rearrange("p a t -> p (a t)"),
                              start=True, stop=True).then_inc(sem("sc_ready"), 1)
                pe.wait_ge(sem("kdt_sb"), n + 1)
                for h in range(GH):
                    ins = pe.matmul(bank[7][:, h * P:(h + 1) * P], KQ[:, h, 1, :], S[:, h, :], start=True, stop=True)
                ins.then_inc(sem("o1_ready"), 1)
                pe.wait_ge(sem("qk_masked"), n + 1)
                turn(NB, 4, "nb_turned")
                turn(KT, 5, "kt_turned")
                pe.wait_ge(sem("vR_in"), n + 1)
                pe.wait_ge(sem("nbt_sb"), n + 1)
                turn(vR, 4, "vr_turned")
                pe.wait_ge(sem("vv_done"), n + 1)
                for g in range(3):
                    if g > 0:
                        pe.wait_ge(sem("sc_sb"), RH * n + RH)
                    for q in range(4):
                        ins = pe.transpose(bank[BANK_A[g]][:, q * P:(q + 1) * P], AT(g, q), ident)
                    ins.then_inc(sem("a_turned"), 1)
                pe.wait_ge(sem("o1_sb"), n + 1)
                for lv in range(1, LEVELS):
                    for g in range(3):
                        pe.wait_ge(sem("t_sb"), T_PER * n + 3 * (lv - 1) + g + 1)
                        for q in range(4):
                            ins = pe.matmul(bank[BANK_A[g]][:, q * P:(q + 1) * P], AT(g, q), Ti[:, g, q, :], start=True, stop=True)
                        ins.then_inc(sem("x_ready"), 1)
                    for g in range(3):
                        if lv == 1:
                            pe.wait_ge(sem("tt_init"), 3 * n + g + 1)
                        pe.wait_ge(sem("x_sb"), X_PER * n + 3 * (lv - 1) + g + 1)
                        if lv < LEVELS - 1:
                            for q in range(4):
                                pe.matmul(bank[BANK_A[g]][:, q * P:(q + 1) * P], TTi[:, g, q, :], Xb[:, g, q, :], start=True, stop=True)
                        for q in range(4):
                            ins = pe.matmul(bank[BANK_B[g]][:, q * P:(q + 1) * P], Xb[:, g, q, :], TTi[:, g, q, :], start=True, stop=True)
                        ins.then_inc(sem("y_ready"), 1)
                pe.wait_ge(sem("t_sb"), T_PER * n + 3 * (LEVELS - 1) + 1)
                pe.wait_ge(sem("vrt_sb"), n + 1)
                for h in range(GH):
                    ins = pe.matmul(bank[4][:, h * P:(h + 1) * P], TTi[:, 0, h, :], VV[:, h, :], start=True, stop=True)
                ins.then_inc(sem("vn_ready"), 1)
                pe.wait_ge(sem("sr_scaled"), n + 1)
                for p in range(RP):
                    pe.matmul(bank[6][:, p * P:(p + 1) * P], RA[:, p, 0, :], Sr[:, p, :], start=True, stop=False)
                    for h in (2 * p, 2 * p + 1):
                        ins = pe.matmul(bank[6][:, 64 * h:64 * h + 64], SC[:, h, 256:384], Vt[:, p, 64 * (h % 2):64 * (h % 2) + 64],
                                        start=False, stop=(h % 2 == 1))
                ins.then_inc(sem("w_ready"), 1)
                pe.wait_ge(sem("t_sb"), T_PER * n + 3 * (LEVELS - 1) + 3)
                pe.wait_ge(sem("w_sb"), n + 1)
                for h in range(RH):
                    ins = pe.matmul(bank[7][:, 64 * h:64 * h + 64], TTi[:, 1 + h // 4, h % 4, :], Wb[:, :, :].rearrange("p a c -> p (a c)")[:, 64 * h:64 * h + 64],
                                    start=True, stop=True)
                ins.then_inc(sem("u_ready"), 1)
                pe.wait_ge(sem("vn_sb"), n + 1)
                pe.wait_ge(sem("ktt_sb"), n + 1)
                for h in range(GH):
                    ins = pe.matmul(bank[5][:, h * P:(h + 1) * P], Dn[:, h, :], VN[:, h, :], start=True, stop=True)
                ins.then_inc(sem("o2_ready"), 1)
                for h in range(GH):
                    ins = pe.matmul(bank[4][:, h * P:(h + 1) * P], kdt[:, h, :], VN[:, h, :], start=True, stop=True)
                ins.then_inc(sem("s_ready"), 1)
                pe.wait_ge(sem("u_sb"), n + 1)
                for p in range(RP):
                    pe.matmul(bank[6][:, p * P:(p + 1) * P], RA[:, p, 1, :], Sr[:, p, :], start=True, stop=False)
                    for h in (2 * p, 2 * p + 1):
                        pe.matmul(bank[6][:, 64 * h:64 * h + 64], SC[:, h, 128:256], Ub[:, 64 * h:64 * h + 64], start=False, stop=False)
                        ins = pe.matmul(bank[6][:, 64 * h:64 * h + 64], SC[:, h, 384:512], Vt[:, p, 64 * (h % 2):64 * (h % 2) + 64],
                                        start=False, stop=(h % 2 == 1))
                ins.then_inc(sem("yr_ready"), 1)
                for p in range(RP):
                    pe.matmul(bank[7][:, p * P:(p + 1) * P], NBt[:, p, :], Ub[:, p * P:(p + 1) * P], start=True, stop=False)
                    pe.matmul(bank[7][:, p * P:(p + 1) * P], KTt[:, p, :], Vt[:, p, :], start=False, stop=False)
                    ins = pe.matmul(bank[7][:, p * P:(p + 1) * P], ident, Sr[:, p, :], start=False, stop=True)
                ins.then_inc(sem("p_ready"), 1)
                pe.wait_ge(sem("state_done"), n + 2)

        def chunk_act(a):
            e = a.e
            with e.Fori(0, NT) as n:
                a.enter(n, ACT_LINKS)
                e.wait_ge(sem("state_done"), n + 1)
                for b in range(RP):
                    e.wait_ge(sem("cum_ready"), RP * n + b + 1)
                    a.link(e.activation(exq[:, b, :], bank[b][:, 0:2 * P + 2], ACT.Exp))
                    a.sig(e.activation(exn[:, b, :], bank[b][:, P:2 * P], ACT.Exp, scale=-1.0), sem("cum_read"), RP * n + b + 1)
                e.wait_ge(sem("vg_turned"), n + 1)
                a.sig(e.activation(vGt[:, :, :], b4(7), ACT.Copy), sem("vgt_sb"), n + 1)
                e.wait_ge(sem("d_made"), n + 1)
                a.sig(e.activation(Dn[:, :, :], Dn[:, :, :], ACT.Exp), sem("d_exp"), n + 1)
                e.wait_ge(sem("k_turned"), n + 1)
                for h in range(GH - 1):
                    a.link(e.activation(kdt[:, h, :], b4(7)[:, h, :], ACT.Copy, scale=sm[:, 4, h:h + 1]))
                a.sig(e.activation(kdt[:, GH - 1, :], b4(7)[:, GH - 1, :], ACT.Copy, scale=sm[:, 4, GH - 1:GH]), sem("kdt_sb"), n + 1)
                e.wait_ge(sem("o1_ready"), n + 1)
                for h in range(GH):
                    ins = e.activation(O1[:, h * P:(h + 1) * P], b4(7)[:, h, :], ACT.Copy, scale=sm[:, 2, h:h + 1])
                    a.link(ins) if h < GH - 1 else a.sig(ins, sem("o1_sb"), n + 1)
                for ready, i, dst, done in (("nb_turned", 4, NBt, "nbt_sb"), ("kt_turned", 5, KTt, "ktt_sb"), ("vr_turned", 4, Vt, "vrt_sb")):
                    e.wait_ge(sem(ready), n + 1)
                    a.sig(e.activation(dst[:, :, :], b4(i), ACT.Copy), sem(done), n + 1)
                e.wait_ge(sem("vn_ready"), n + 1)
                for h in range(GH):
                    ins = e.activation(VN[:, h, :], b4(4)[:, h, :], ACT.Copy, scale=sm[:, 3, h:h + 1])
                    a.link(ins) if h < GH - 1 else a.sig(ins, sem("vn_sb"), n + 1)
                e.wait_ge(sem("w_ready"), n + 1)
                a.sig(e.activation(Wb[:, :, :], b4(6), ACT.Copy), sem("w_sb"), n + 1)
                e.wait_ge(sem("u_ready"), n + 1)
                a.sig(e.activation(Ub[:, :], bank[7][:, :], ACT.Copy), sem("u_sb"), n + 1)
                a.leave(NT)

        def chunk_dve(v):
            e = v.e
            e.wait_ge(sem("state_init"), 1)
            e.sem_inc(sem("state_done"), 1)
            with e.Fori(0, NT) as n:
                v.enter(n, DVE_LINKS)
                e.wait_ge(sem("sm_in"), n + 1)
                e.wait_ge(sem("gbc_ready"), n + 1)
                for h in range(GH):
                    ins = e.tensor_scalar(Dn[:, h, :], b4(6)[:, h, :], sm[:, 1, h:h + 1], 0.0, ALU.subtract, ALU.min)
                    v.link(ins) if h < GH - 1 else v.sig(ins, sem("d_made"), n + 1)
                e.wait_ge(sem("cum_read"), RP * n + RP)
                v.link(e.tensor_tensor(RA[:, :, 0, :], kkT[:, :, bass.ds(n * P, P)], exq[:, :, 0:P], ALU.mult))
                v.link(e.tensor_tensor(RA[:, :, 1, :], fT[:, RB:RB + 4, tcol(n)], exq[:, :, P:2 * P], ALU.mult))
                v.link(e.tensor_tensor(KT[:, :, :], fT[:, KRB:KRB + 4, tcol(n)], exn[:, :, :], ALU.mult))
                v.sig(e.tensor_tensor(NB[:, :, :], aT[:, :, bass.ds(n * P, P)], exn[:, :, :], ALU.mult), sem("rk_ready"), n + 1)
                e.wait_ge(sem("ks_ready"), n + 1)
                e.wait_ge(sem("vgt_sb"), n + 1)
                for h in range(GH):
                    ins = e.scalar_tensor_tensor(VV[:, h, :], b4(6)[:, h, :], sm[:, 2, h:h + 1], vGt[:, h, :], ALU.mult, ALU.add)
                    v.link(ins) if h < GH - 1 else v.sig(ins, sem("vv_done"), n + 1)
                e.wait_ge(sem("kkq_ready"), n + 1)
                e.wait_ge(sem("d_masked"), n + 1)
                for h in range(GH):
                    kq = bank[4 + h // 2][:, :].rearrange("p (h a t) -> p h a t", h=2, a=2)[:, h % 2]
                    v.link(e.scalar_tensor_tensor(Ds[:, h, :], kq[:, 0, :], sm[:, 6, h:h + 1], Ds[:, h, :], ALU.mult, ALU.mult))
                for i in range(2):
                    kq = bank[4 + i][:, :].rearrange("p (h a t) -> p h a t", h=2, a=2)[:, :, 1, :]
                    ins = e.tensor_tensor(Dn[:, 2 * i:2 * i + 2, :], kq, Dn[:, 2 * i:2 * i + 2, :], ALU.mult)
                    v.link(ins) if i == 0 else v.sig(ins, sem("qk_masked"), n + 1)
                tri = con[:, C_OFF["strict"][0]:C_OFF["incl"][1]].unsqueeze(1).to_broadcast([P, 2, 2 * P])
                for h in range(RH):
                    e.wait_ge(sem("sc_ready"), RH * n + h + 1)
                    v.sig(e.tensor_tensor(SC[:, h, :].rearrange("p (a t) -> p a t", a=2), bank[h % 4][:, :].rearrange("p (a t) -> p a t", a=2), tri, ALU.mult),
                          sem("sc_sb"), RH * n + h + 1)
                for p in range(RP):
                    ins = e.tensor_scalar(Sr[:, p, :], Sr[:, p, :], exq[:, p, 2 * P:2 * P + 1], None, ALU.mult)
                    v.link(ins) if p < RP - 1 else v.sig(ins, sem("sr_scaled"), n + 1)
                level = C("level").rearrange("p (l c) -> p l c", l=LEVELS)
                for g in range(3):
                    e.wait_ge(sem("a_turned"), 3 * n + g + 1)
                    v.link(e.tensor_tensor(Ti[:, g], b4(BANK_A[g]), rep4(level[:, 0, :]), ALU.mult))
                    v.sig(e.tensor_tensor(Ti[:, g], Ti[:, g], rep4(ident), ALU.add), sem("t_sb"), T_PER * n + g + 1)
                for lv in range(1, LEVELS):
                    for g in range(3):
                        e.wait_ge(sem("x_ready"), X_PER * n + 3 * (lv - 1) + g + 1)
                        v.sig(e.tensor_tensor(Xb[:, g], b4(BANK_A[g]), rep4(level[:, lv, :]), ALU.mult), sem("x_sb"), X_PER * n + 3 * (lv - 1) + g + 1)
                    for g in range(3):
                        e.wait_ge(sem("y_ready"), X_PER * n + 3 * (lv - 1) + g + 1)
                        if lv < LEVELS - 1:
                            v.link(e.tensor_tensor(Ti[:, g], b4(BANK_A[g]), Ti[:, g], ALU.add))
                        v.sig(e.tensor_tensor(TTi[:, g], b4(BANK_B[g]), TTi[:, g], ALU.add), sem("t_sb"), T_PER * n + 3 * lv + g + 1)
                e.wait_ge(sem("o2_ready"), n + 1)
                e.wait_ge(sem("o1_sb"), n + 1)
                v.link(e.tensor_tensor(fT[:, QB:QB + 4, tcol(n)], b4(5), O1[:, :].rearrange("p (h c) -> p h c", h=4), ALU.subtract))
                e.wait_ge(sem("s_ready"), n + 1)
                for h in range(GH):
                    v.link(e.scalar_tensor_tensor(S[:, h, :], S[:, h, :], sm[:, 5, h:h + 1], b4(4)[:, h, :], ALU.mult, ALU.add))
                e.wait_ge(sem("yr_ready"), n + 1)
                v.link(e.tensor_scalar(fT[:, RB:RB + 4, tcol(n)], b4(6), 1.0, None, ALU.mult))
                e.wait_ge(sem("p_ready"), n + 1)
                for p in range(RP):
                    ins = e.scalar_tensor_tensor(Sr[:, p, :], b4(7)[:, p, :], exq[:, p, 2 * P + 1:2 * P + 2], bones, ALU.mult, ALU.mult)
                    v.link(ins) if p < RP - 1 else v.sig(ins, sem("state_done"), n + 2)
                v.leave(NT)

        def out0_act(a):
            e = a.e
            e.dma_start(rowbuf[:, :], rows[4:5, :].to_broadcast([P, D])).then_inc(sem("aux_loaded"), 16)
            a.link(e.activation(z[:, :, :], z[:, :, :], ACT.Silu))
            e.sem_inc(sem("z_silu"), 1)
            e.wait_ge(sem("ss_sb"), 1)
            a.link(e.activation(hst[:, 0, :, 0:GH], hst[:, 0, :, 0:GH], ACT.Sqrt, bias=eps, scale=1.0 / P))
            a.sig(e.activation(hst[:, 3, :, :], hst[:, 3, :, :], ACT.Sqrt, bias=ln_eps, scale=1.0 / 64), sem("hroot"), 1)
            for i in range(NT):
                e.wait_ge(sem("turned"), 4 + i + 1)
                for h in range(2):
                    hi, _, src = turned(DM, i, h)
                    a.sig(e.activation(hi, src, ACT.Copy, scale=PR("gnorm") if h == 0 else 1.0), sem("high_done"), 8 + 2 * i + h + 1)

        def out0_dve(v):
            e = v.e
            hd = lambda x: x.rearrange("p b (c d) -> p b c d", c=2)
            h8 = lambda k, i: hst[:, k, i, :].rearrange("p (b c) -> p b c", c=2)
            w3 = lambda x: x.unsqueeze(3).to_broadcast([P, 4, 2, 64])
            for i in range(NT):
                o = fT[:, QB:QB + 4, PAD + i * P:PAD + (i + 1) * P]
                t = t1[:, i, :].rearrange("p (b c) -> p b c", b=4)
                v.link(e.tensor_tensor(t, o, o, ALU.mult))
                v.link(e.tensor_reduce(hst[:, 0, i, 0:GH], t, AX.X, ALU.add))
            for i in range(NT):
                y = fT[:, RB:RB + 4, PAD + i * P:PAD + (i + 1) * P]
                yn = y_n[:, i, :].rearrange("p (b c) -> p b c", b=4)
                t = t1[:, i, :].rearrange("p (b c) -> p b c", b=4)
                v.link(e.tensor_reduce(h8(2, i), hd(y), AX.X, ALU.add))
                v.link(e.tensor_scalar(h8(2, i), h8(2, i), 1.0 / 64, None, ALU.mult))
                v.link(e.tensor_tensor(hd(yn), hd(y), w3(h8(2, i)), ALU.subtract))
                v.link(e.tensor_tensor(t, yn, yn, ALU.mult))
                ins = e.tensor_reduce(h8(3, i), hd(t), AX.X, ALU.add)
                v.link(ins) if i < NT - 1 else v.sig(ins, sem("ss_sb"), 1)
            e.wait_ge(sem("hroot"), 1)
            v.link(e.reciprocal(hst[:, 1, :, 0:GH], hst[:, 0, :, 0:GH]))
            v.link(e.reciprocal(hst[:, 4, :, :], hst[:, 3, :, :]))
            e.wait_ge(sem("z_silu"), 1)
            e.wait_ge(sem("aux_loaded"), 16)
            e.wait_ge(sem("g_ready"), 1)
            for i in range(NT):
                o = fT[:, QB:QB + 4, PAD + i * P:PAD + (i + 1) * P]
                on = o_n[:, i, :].rearrange("p (b c) -> p b c", b=4)
                v.link(e.tensor_tensor(on, o, hst[:, 1, i, 0:GH].unsqueeze(2).to_broadcast([P, GH, P]), ALU.mult))
                v.link(e.tensor_tensor(o_n[:, i, :], o_n[:, i, :], z[:, i, :], ALU.mult))
                yn = y_n[:, i, :].rearrange("p (b c) -> p b c", b=4)
                v.link(e.tensor_tensor(hd(yn), hd(yn), w3(h8(4, i)), ALU.mult))
                v.link(e.tensor_tensor(y_n[:, i, :], y_n[:, i, :], rowbuf[:, 0:512], ALU.mult))
                v.link(e.tensor_tensor(y_n[:, i, :], y_n[:, i, :], rowbuf[:, 512:1024], ALU.add))
                t = t1[:, i, :].rearrange("p (b c) -> p b c", b=4)
                vt = fT[:, VRB:VRB + 4, PAD + i * P:PAD + (i + 1) * P]
                v.link(e.tensor_tensor(hd(t), hd(vt), w3(bonus[:, i, :].rearrange("p (b c) -> p b c", c=2)), ALU.mult))
                v.link(e.tensor_tensor(y_n[:, i, :], y_n[:, i, :], t1[:, i, :], ALU.add))
                v.sig(e.tensor_tensor(y_n[:, i, :], bank[i][:, :], y_n[:, i, :], ALU.mult), sem("m_sb"), i + 1)
            for i in range(NT):
                for h in range(2):
                    e.wait_ge(sem("high_done"), 8 + 2 * i + h + 1)
                    hi, lo, src = turned(DM, i, h)
                    v.link(e.scalar_tensor_tensor(lo, src, PR("gnorm") if h == 0 else 1.0, hi.bitcast(F32), ALU.mult, ALU.subtract))

        def out0_pe(pe):
            for i in range(NT):
                ins = pe.matmul(bank[i][:, :], fT[:, GD, PAD + i * P:PAD + (i + 1) * P], PR("g2"), start=True, stop=True)
            ins.then_inc(sem("g_ready"), 1)
            pe.wait_ge(sem("m_sb"), NT)
            for i in range(NT):
                for q in range(4):
                    pe.transpose(bank[2 * i][:, q * P:(q + 1) * P], o_n[:, i, q * P:(q + 1) * P], ident)
                for q in range(4):
                    ins = pe.transpose(bank[2 * i + 1][:, q * P:(q + 1) * P], y_n[:, i, q * P:(q + 1) * P], ident)
                ins.then_inc(sem("turned"), 1)

        def oproj_pe(pe, first):
            mh, ml_, wh, wl = DM
            for k in range(KD):
                c = first + k
                weights(pe, c)
                for i in range(NT):
                    t = slice(i * P, (i + 1) * P)
                    for h in range(2):
                        w = slice(h * 512, (h + 1) * 512)
                        ins = mm3(pe, bank[2 * i + h][:, :], mh[:, k, t], ml_[:, k, t], wh[:, c % RING, w], wl[:, c % RING, w], k == 0, k == KD - 1)
                ins.then_inc(sem("w_used"), 1)

        def row_in(act, r):
            act.dma_start(rowbuf[:, :], rows[r:r + 1, :].to_broadcast([P, D])).then_inc(sem("row_loaded"), 16)

        def oproj_act(a, c, first):
            if c == 0:
                a.e.dma_start(xres[:, :, :], x_d).then_inc(sem("aux_loaded"), 16)
            row_in(a.e, 2 * c)
            pre_in(a.e, 2 * c + 1, prerow)
            for k in range(KD):
                split_hi(a, DM, first + k)
            used(a.e, first + KD - 1)
            for i in range(NT):
                a.sig(a.e.activation(ffo[:, i, 512:1024], bank[2 * i + 1][:, :], ACT.Copy), sem("ffo_right"), 4 * c + i + 1)
            a.e.wait_ge(sem("ffo_left"), 4 * c + 4)

        def oproj_dve(v, c, first):
            for k in range(KD):
                split_lo(v, DM, first + k)
            used(v.e, first + KD - 1)
            for i in range(NT):
                v.sig(v.e.tensor_copy(ffo[:, i, 0:512], bank[2 * i][:, :]), sem("ffo_left"), 4 * c + i + 1)
            if c == 0:
                v.e.wait_ge(sem("aux_loaded"), 32)

        MB = 2 * HF

        def mlp_pe(pe, first, c):
            uh, ul, wh, wl = DM
            with pe.Fori(0, 2) as it:
                for s in range(HF):
                    ch = first + s
                    weights(pe, ch, it, MB)
                    if s < 4:
                        pe.wait_ge(sem("right_out"), it * 4 + (12 * c + s + 1))
                    else:
                        pe.wait_ge(sem("relu_done"), it * HF + (2 * HF * c + s - 3))
                    for k in range(KD):
                        w = slice(k * P, (k + 1) * P)
                        ins = mm3(pe, bank[s % 4][:, :], wh[:, ch % RING, w], wl[:, ch % RING, w], uh[:, k, :], ul[:, k, :], k == 0, k == KD - 1)
                    ins.then_inc(sem("w_used"), 1)
                for half in range(2):
                    b0 = 4 * (1 - half)
                    if half == 0:
                        pe.wait_ge(sem("left_out"), it * 4 + (12 * c + 4))
                    for j in range(HF // 2):
                        ch = first + HF + half * HF // 2 + j
                        weights(pe, ch, it, MB)
                        pe.wait_ge(sem("h_lo"), it * HF + (2 * HF * c + (2 * j + 2 if half == 0 else HF)))
                        for f in (2 * j, 2 * j + 1):
                            w = slice((f % 2) * 512, (f % 2 + 1) * 512)
                            for i in range(NT):
                                t = slice(i * P, (i + 1) * P)
                                ins = mm3(pe, bank[b0 + i][:, :], hh[:, f, t], hl[:, f, t], wh[:, ch % RING, w], wl[:, ch % RING, w], f == 0, f == HF - 1)
                        ins.then_inc(sem("w_used"), 1)

        def mlp_act(a, first, c):
            e, hb = a.e, 2 * HF * c
            with e.Fori(0, 2) as it:
                for s in range(2):
                    split_hi(a, DM, first + s, it, MB)
                for s in range(MB):
                    if s + 2 < MB:
                        split_hi(a, DM, first + s + 2, it, MB)
                    if s < HF:
                        used(e, first + s, it, MB)
                        e.wait_ge(sem("hraw_free"), it * HF + ((2 * HF + 2) * c + s + 1))
                        a.sig(e.activation(hraw[:, s % 2, :], bank[s % 4][:, :], ACT.Relu), sem("relu_done"), it * HF + (hb + s + 1))
                    if 1 <= s <= HF:
                        e.wait_ge(sem("h_sq"), it * HF + (hb + s))
                        a.sig(e.activation(hh[:, s - 1, :], hraw[:, (s - 1) % 2, :], ACT.Copy), sem("h_hi"), it * HF + (hb + s))

        def mlp_dve(v, first, c):
            e, hb = v.e, 2 * HF * c
            for nm in ("right_out", "left_out"):
                e.sem_inc(sem(nm), 4)
            e.sem_inc(sem("hraw_free"), 2)
            e.wait_ge(sem("ffo_zero"), c + 1)
            with e.Fori(0, 2) as it:
                for s in range(2):
                    split_lo(v, DM, first + s, it, MB)
                for s in range(MB):
                    if s + 2 < MB:
                        split_lo(v, DM, first + s + 2, it, MB)
                    if s < HF:
                        h = hraw[:, s % 2, :]
                        e.wait_ge(sem("relu_done"), it * HF + (hb + s + 1))
                        v.sig(e.tensor_tensor(h, h, h, ALU.mult), sem("h_sq"), it * HF + (hb + s + 1))
                    if 1 <= s <= HF:
                        e.wait_ge(sem("h_hi"), it * HF + (hb + s))
                        v.sig(e.tensor_tensor(hl[:, s - 1, :], hraw[:, (s - 1) % 2, :], hh[:, s - 1, :].bitcast(F32), ALU.subtract), sem("h_lo"), it * HF + (hb + s))
                        e.sem_inc(sem("hraw_free"), 1)
                    for half, end in ((0, HF + HF // 2 - 1), (1, MB - 1)):
                        if s == end:
                            used(e, first + s, it, MB)
                            for i in range(NT):
                                o = ffo[:, i, 512 * half:512 * half + 512]
                                nm = "right_out" if half else "left_out"
                                v.sig(e.tensor_tensor(o, bank[4 * (1 - half) + i][:, :], o, ALU.add), sem(nm), it * 4 + (12 * c + 4 + i + 1))

        l1 = ExitStack()
        KVW = 2 * HD
        QW = QH * HD
        f1 = sb("f1", [P, NT, QW + 6 * KVW + 3 * QH], c=l1)
        posi = sb("posi", [P, NT + 1], I32, c=l1)
        posf = sb("posf", [P, NT + 1], c=l1)
        ang = sb("ang", [P, NT + 1, 2, HALF], c=l1)
        rnd = sb("rnd", [P, NT + 1, 2, HALF], c=l1)
        l1p = ExitStack()
        D1 = dense(l1p, "1")
        l1p.close()
        qT = sb("qT", [P, QH, T], F32R, c=l1)
        kH = sb("kH", [P, 2, KG, T], F32R, c=l1)
        kL = sb("kL", [P, 2, KG, T], F32R, c=l1)
        msk = sb("msk", [P, 2, P], F32R, c=l1)
        l1y = ExitStack()
        dupq = sb("dupq", [P, 2, QH, 2, HD], c=l1y)
        l1y.close()
        yat = sb("yat", [P, NT, QW], c=l1)
        kcT = sb("kcT", [P, 2 * NCMP], c=l1)
        vcb = sb("vcb", [P, KG, 4, HD], c=l1)
        gat = sb("gat", [P, QH, 2, NT], c=l1)
        csn = sb("csn", [P, NT + 1, 2, HALF], c=l1)
        l1a = ExitStack()
        rot = sb("rot", [P, 4, NT, QH * HALF], c=l1a)
        dup = sb("dup", [P, 2, KG, NT, 2, HD], c=l1a)
        X2 = sb("X2", [P, 2, KG, T + 32], c=l1a)
        XP = sb("XP", [P, 2, 16, KG, NCMP], c=l1a)
        hc = sb("hc", [2 * NCMP, 2, 256], c=l1a)
        hcT = sb("hcT", [P, 4, 2 * NCMP], c=l1a)
        hrep = sb("hrep", [P, 2, KG, 4, NCMP], c=l1a)
        kcs = sb("kcs", [2 * NCMP, HD], c=l1a)
        kcp = sb("kcp", [2 * NCMP, 2, HD], c=l1a)
        vcr = sb("vcr", [P, KG, HD], c=l1a)
        l1a.close()
        l1b = ExitStack()
        sc_c = sb("sc_c", [P, QH, NCMP], c=l1b)
        pc = sb("pc", [P, KG, HPG, NCMP], c=l1b)
        pcT = sb("pcT", [P, 4, P], c=l1b)
        cst = sb("cst", [P, 4, QH], c=l1b)
        l1b.close()
        l1c = ExitStack()
        qb = sb("qb", [P, 2, T], F32R, c=l1c)
        pb = sb("pb", [P, 4, T], c=l1c)
        pT = sb("pT", [P, 4, T], c=l1c)
        nmax = sb("nmax", [P, 16], c=l1c)
        rsum = sb("rsum", [P, 16], c=l1c)
        rsc = sb("rsc", [P, 8], c=l1c)
        om = sb("om", [P, 2, NT, HD], c=l1c)
        l1c.close()
        l1.close()
        KC, VC, KS, VS, KW, VW = (QW + i * KVW for i in range(6))
        GT = QW + 6 * KVW
        GROUP_W = [512, 512, 512, GT + 3 * QH - 1536]

        def proj1_pe(pe):
            uh, ul, wh, wl = D1
            for gr in range(4):
                if gr >= 2:
                    pe.wait_ge(sem("f1_even"), 2 * (gr - 1))
                    pe.wait_ge(sem("f1_odd"), 2 * (gr - 1))
                for c in range(4):
                    ch = C_IN1 + 4 * gr + c
                    weights(pe, ch)
                    for kk in range(2):
                        k, w = 2 * c + kk, GROUP_W[gr]
                        ws = slice(kk * 512, kk * 512 + w)
                        for i in range(NT):
                            t = slice(i * P, (i + 1) * P)
                            ins = mm3(pe, bank[(gr % 2) * 4 + i][:, 0:w], uh[:, k, t], ul[:, k, t], wh[:, ch % RING, ws], wl[:, ch % RING, ws], k == 0, k == KD - 1)
                    ins.then_inc(sem("w_used"), 1)

        def proj1_out(ch, odd):
            split = split_hi if odd else split_lo
            for c in range(2):
                split(ch, D1, C_IN1 + c)
            for gr in range(4):
                for c in range(4 * gr, 4 * gr + 4):
                    if c + 2 < 16:
                        split(ch, D1, C_IN1 + c + 2)
                used(ch.e, C_IN1 + 4 * gr + 3)
                for m, i in enumerate((1, 3) if odd else (0, 2)):
                    w = GROUP_W[gr]
                    dst, src = f1[:, i, gr * 512:gr * 512 + w], bank[(gr % 2) * 4 + i][:, 0:w]
                    ins = ch.e.activation(dst, src, ACT.Copy) if odd else ch.e.tensor_copy(dst, src)
                    ch.sig(ins, sem("f1_odd" if odd else "f1_even"), 2 * gr + m + 1)

        def proj1_act(a):
            a.e.dma_start(posi[:, :], pos).then_inc(sem("aux_loaded"), 16)
            proj1_out(a, True)

        TWO_PI = (6.28125, 0.0019350051879882812, 3.019916050561733e-07)
        ROUND = 12582912.0

        def proj1_dve(v):
            proj1_out(v, False)
            e = v.e
            e.wait_ge(sem("aux_loaded"), 48)
            v.link(e.tensor_copy(posf[:, :], posi[:, :]))
            for m in range(2):
                v.link(e.tensor_tensor(ang[:, :, m, :], posf[:, :].unsqueeze(2).to_broadcast([P, NT + 1, HALF]),
                                       C("ifreq").unsqueeze(1).to_broadcast([P, NT + 1, HALF]), ALU.mult))
                v.link(e.tensor_scalar(rnd[:, :, m, :], ang[:, :, m, :], float(1 / (2 * np.pi)), 0.25 * m, ALU.mult, ALU.add))
            v.link(e.tensor_scalar(rnd[:, :, :, :], rnd[:, :, :, :], ROUND, None, ALU.add))
            v.link(e.tensor_scalar(rnd[:, :, :, :], rnd[:, :, :, :], ROUND, None, ALU.subtract))
            for part in TWO_PI:
                v.link(e.scalar_tensor_tensor(ang[:, :, :, :], rnd[:, :, :, :], -part, ang[:, :, :, :], ALU.mult, ALU.add))
            v.link(e.tensor_scalar(ang[:, :, 1, :], ang[:, :, 1, :], float(np.pi / 2), None, ALU.add))
            v.sig(e.tensor_scalar(ang[:, :, :, :], ang[:, :, :, :], 3.1415925, -3.1415925, ALU.min, ALU.max), sem("ang_done"), 1)

        def rotary(v, x1, x2, sn, cs, t):
            e = v.e
            v.link(e.tensor_tensor(t[0], x1, cs, ALU.mult))
            v.link(e.tensor_tensor(t[1], x2, sn, ALU.mult))
            v.link(e.tensor_tensor(t[2], x2, cs, ALU.mult))
            v.link(e.tensor_tensor(t[3], x1, sn, ALU.mult))
            v.link(e.tensor_tensor(x1, t[0], t[1], ALU.subtract))
            v.link(e.tensor_tensor(x2, t[2], t[3], ALU.add))

        def prep_pool(g):
            for kv in range(2):
                for gr in range(KG):
                    src = f1[:, :, KC + kv * KVW + gr * HD:KC + kv * KVW + (gr + 1) * HD].unsqueeze(2).to_broadcast([P, NT, 2, HD])
                    g.sig(g.e.tensor_copy(dup[:, kv, gr], src), sem("dup_done"), 2 * kv + gr + 1)
            g.sig(g.e.memset(X2[:, :, :, T - 1:], 0.0), sem("zeroed"), 1)
            g.e.wait_ge(sem("rotated"), 1)
            for i in range(NT):
                if i >= 2:
                    g.e.wait_ge(sem("q_turned"), 4 + 4 * (i - 1))
                src = f1[:, i, 0:QW].rearrange("p (h d) -> p h d", d=HD).unsqueeze(2).to_broadcast([P, QH, 2, HD])
                g.sig(g.e.tensor_copy(dupq[:, i % 2], src), sem("dupq_done"), i + 1)

        def prep_act(a):
            e = a.e
            a.sig(e.activation(csn[:, :, :, :], ang[:, :, :, :], ACT.Sin), sem("sin_done"), 1)
            e.wait_ge(sem("zeroed"), 1)
            for m in range(4):
                e.wait_ge(sem("c_turned"), m + 1)
                kv, gr = m // 2, m % 2
                a.link(e.activation(X2[0:64, kv, gr, 0:T], bank[m][0:64, :], ACT.Copy))
                a.sig(e.activation(X2[64:128, kv, gr, 0:T - 1], bank[m][64:128, 1:T], ACT.Copy), sem("x2_done"), m + 1)
            for n in range(20):
                e.wait_ge(sem("q_turned"), n + 1)
                hi, _, src, scale = split_task(n)
                a.sig(e.activation(hi, src, ACT.Copy, scale=scale), sem("q_hi"), n + 1)
                if n == 7:
                    for kv in range(2):
                        used(e, C_CMP + 4 * kv + 3)
                        a.sig(e.activation(hc[:, kv, :], bank[kv][0:64, 0:256], ACT.Silu), sem("hc_done"), kv + 1)

        def split_task(n):
            if n < 4:
                return kH[:, n // 2, n % 2, :], kL[:, n // 2, n % 2, :], bank[4 + n][:, :], 1.0
            i, h = (n - 4) // 4, (n - 4) % 4
            q = qT[:, 4 * h:4 * h + 4, i * P:(i + 1) * P]
            return q, q[64:128], b4(4 + n % 4), HD ** -0.5

        def prep_dve(v):
            e = v.e
            e.wait_ge(sem("sin_done"), 1)
            for off, nh in ((0, QH), (KS, 2), (KW, 2)):
                x = f1[:, :, off:off + nh * HD].rearrange("p i (h d) -> p i h d", d=HD)
                sn, cs = (csn[:, 0:NT, m, :].unsqueeze(2).to_broadcast([P, NT, nh, HALF]) for m in range(2))
                t = [rot[:, m, :, 0:nh * HALF].rearrange("p i (h d) -> p i h d", d=HALF) for m in range(4)]
                rotary(v, x[:, :, :, 0:HALF], x[:, :, :, HALF:2 * HALF], sn, cs, t)
                e.sem_inc(sem("rotated"), 1)
            e.wait_ge(sem("c_turned"), 4)
            for b, off in enumerate((KS, KW)):
                for gr in range(KG):
                    src = f1[:, :, off + gr * HD:off + (gr + 1) * HD].unsqueeze(2).to_broadcast([P, NT, 2, HD])
                    v.sig(e.tensor_copy(dup[:, b, gr], src), sem("dup_done"), 5 + 2 * b + gr)
            for kv in range(2):
                pe_c = PR("pe_k" if kv == 0 else "pe_v")
                for gr in range(KG):
                    e.wait_ge(sem("x2_done"), 2 * kv + gr + 1)
                    for half in range(2):
                        src = X2[:, kv, gr, 16 * half:16 * half + 512].rearrange("p (n b two) -> p b n two", b=8, two=2)[:, :, :, 0]
                        pw = pe_c[:, 8 * half:8 * half + 8].unsqueeze(2).to_broadcast([P, 8, NCMP])
                        v.link(e.tensor_tensor(XP[:, kv, 8 * half:8 * half + 8, gr, :], src, pw, ALU.add))
                e.sem_inc(sem("xp_done"), 1)
            for n in range(20):
                hi, lo, src, scale = split_task(n)
                e.wait_ge(sem("q_hi"), n + 1)
                if n < 4:
                    ins = e.tensor_tensor(lo, src, hi.bitcast(F32), ALU.subtract)
                else:
                    ins = e.scalar_tensor_tensor(lo, src[64:128], scale, lo.bitcast(F32), ALU.mult, ALU.subtract)
                v.sig(ins, sem("q_lo"), n + 1)
            e.wait_ge(sem("hc_turned"), 1)
            v.sig(e.tensor_copy(hcT[:, :, :], bank[2][:, 0:256].rearrange("p (a c) -> p a c", a=4)), sem("hcT_done"), 1)
            for m in range(2):
                for gr in range(KG):
                    src = hcT[:, 2 + m, gr * NCMP:(gr + 1) * NCMP].unsqueeze(1).to_broadcast([P, 4, NCMP])
                    v.link(e.tensor_copy(hrep[:, m, gr], src))
            e.sem_inc(sem("hrep_done"), 1)
            e.wait_ge(sem("kc_ready"), 1)
            v.link(e.tensor_copy(kcs[:, :], bank[3][0:64, 0:64]))
            t = [rot[0:64, m, 0, 0:HALF] for m in range(4)]
            rotary(v, kcs[:, 0:HALF], kcs[:, HALF:2 * HALF], csn[0:64, NT, 0, :], csn[0:64, NT, 1, :], t)
            v.sig(e.tensor_copy(kcp[:, :, :], kcs[:, :].unsqueeze(1).to_broadcast([2 * NCMP, 2, HD])), sem("kcp_done"), 1)
            e.wait_ge(sem("vc_ready"), 1)
            v.link(e.tensor_copy(vcr[:, :, :], bank[0][:, 0:128].rearrange("p (g d) -> p g d", g=2)))
            for j in range(4):
                v.link(e.tensor_scalar(vcb[:, :, j, :], vcr[:, :, :], C("hsel")[:, j:j + 1], None, ALU.mult))
            e.wait_ge(sem("kcT_ready"), 1)
            v.link(e.tensor_copy(kcT[:, :], bank[1][:, 0:64]))

        def prep_pe(pe):
            for m in range(4):
                pe.wait_ge(sem("dup_done"), m + 1)
                for i in range(NT):
                    ins = pe.transpose(bank[m][:, i * P:(i + 1) * P], dup[:, m // 2, m % 2, i].rearrange("p a d -> p (a d)"), ident)
                ins.then_inc(sem("c_turned"), 1)
            for m in range(4):
                pe.wait_ge(sem("dup_done"), 5 + m)
                for i in range(NT):
                    ins = pe.transpose(bank[4 + m][:, i * P:(i + 1) * P], dup[:, m // 2, m % 2, i].rearrange("p a d -> p (a d)"), ident)
                ins.then_inc(sem("q_turned"), 1)
            pe.wait_ge(sem("x2_done"), 4)
            for kv in range(2):
                pe.wait_ge(sem("xp_done"), kv + 1)
                for c in range(4):
                    ch = C_CMP + 4 * kv + c
                    pe.wait_ge(slot_sems[ch % RING], 16 * (ch // RING + 1))
                    for q in range(4):
                        lp = 4 * c + q
                        ins = pe.matmul(bank[kv][0:64, 0:256], XP[:, kv, lp].rearrange("p g n -> p (g n)"), ring[:, ch % RING, q * 256:(q + 1) * 256],
                                        start=(lp == 0), stop=(lp == 15))
                    ins.then_inc(sem("w_used"), 1)
                    used(pe, ch)
                    pass_over(pe, ch)
            for n in range(4, 20):
                i, h = (n - 4) // 4, (n - 4) % 4
                pe.wait_ge(sem("dupq_done"), i + 1)
                pe.wait_ge(sem("q_lo"), n - 3)
                for j in range(4):
                    ins = pe.transpose(bank[4 + n % 4][:, j * P:(j + 1) * P], dupq[:, i % 2, 4 * h + j].rearrange("p a d -> p (a d)"), ident)
                ins.then_inc(sem("q_turned"), 1)
            pe.wait_ge(sem("hc_done"), 2)
            for m in range(4):
                ins = pe.transpose(bank[2][:, m * 64:(m + 1) * 64], hc[:, m // 2, (m % 2) * P:(m % 2 + 1) * P], ident[0:64, 0:64])
            ins.then_inc(sem("hc_turned"), 1)
            pe.wait_ge(sem("hcT_done"), 1)
            for m in range(2):
                ins = pe.matmul(bank[3][0:64, 0:64], hcT[:, m, :], PR("w2k")[:, m * 64:(m + 1) * 64], start=(m == 0), stop=(m == 1))
            ins.then_inc(sem("kc_ready"), 1)
            pe.wait_ge(sem("hrep_done"), 1)
            for gr in range(KG):
                for m in range(2):
                    ins = pe.matmul(bank[0][:, gr * 64:(gr + 1) * 64], hrep[:, m, gr].rearrange("p j n -> p (j n)"), PR("w2v")[:, m * 64:(m + 1) * 64],
                                    start=(m == 0), stop=(m == 1))
            ins.then_inc(sem("vc_ready"), 1)
            pe.wait_ge(sem("kcp_done"), 1)
            pe.transpose(bank[1][:, 0:64], kcp[:, :, :].rearrange("p a d -> p (a d)"), ident[0:64, 0:64]).then_inc(sem("kcT_ready"), 1)

        def cmp_pe(pe):
            for i in range(NT):
                if i > 0:
                    pe.wait_ge(sem("cs_read"), i)
                for h in range(QH):
                    ins = pe.matmul(bank[0][:, h * NCMP:(h + 1) * NCMP], qT[:, h, i * P:(i + 1) * P].bitcast(F32),
                                    kcT[:, (h % KG) * NCMP:(h % KG + 1) * NCMP], start=True, stop=True)
                ins.then_inc(sem("cs_ready"), 1)
                pe.wait_ge(sem("pc_done"), i + 1)
                for q in range(4):
                    ins = pe.transpose(bank[1][:, q * P:(q + 1) * P], pc[:, q // 2, 4 * (q % 2):4 * (q % 2) + 4, :].rearrange("p j n -> p (j n)"), ident)
                ins.then_inc(sem("pc_turned"), 1)
                pe.wait_ge(sem("pcT_done"), i + 1)
                if i > 0:
                    pe.wait_ge(sem("oc_done"), i)
                for q in range(4):
                    ins = pe.matmul(bank[2 + q // 2][:, (q % 2) * 256:(q % 2 + 1) * 256], pcT[:, q, :], vcb[:, q // 2].rearrange("p j d -> p (j d)"),
                                    start=True, stop=True)
                ins.then_inc(sem("oc_ready"), 1)

        def cmp_act(a):
            e = a.e
            a.sig(e.activation(f1[:, :, GT:GT + 3 * QH], f1[:, :, GT:GT + 3 * QH], ACT.Sigmoid), sem("gates"), 1)
            a.link(e.activation(msk[:, 0, :], ident, ACT.Copy))
            a.link(e.activation(msk[:, 1, :], C("neg"), ACT.Copy))
            for i in range(NT):
                e.wait_ge(sem("cs_sub"), i + 1)
                a.sig(e.activation(sc_c[:, :, :], sc_c[:, :, :], ACT.Exp), sem("cs_exp"), i + 1)
                e.wait_ge(sem("pc_turned"), i + 1)
                a.sig(e.activation(pcT[:, :, :], b4(1), ACT.Copy), sem("pcT_done"), i + 1)

        def cmp_dve(v):
            e = v.e
            e.wait_ge(sem("gates"), 1)
            for b in range(2):
                src = f1[:, :, GT + QH * (1 + b):GT + QH * (2 + b)].rearrange("p i h -> p h i")
                v.link(e.tensor_copy(gat[:, :, b, :], src))
            cm = C("cmask").rearrange("p (i n) -> p i n", i=NT)
            cn = C("cneg").rearrange("p (i n) -> p i n", i=NT)
            w = lambda k: cst[:, k, :].unsqueeze(2).to_broadcast([P, QH, NCMP])
            for i in range(NT):
                e.wait_ge(sem("cs_ready"), i + 1)
                m = lambda x: x[:, i, :].unsqueeze(1).to_broadcast([P, QH, NCMP])
                v.sig(e.tensor_tensor(sc_c[:, :, :], bank[0][:, :].rearrange("p (h n) -> p h n", n=NCMP), m(cn), ALU.add), sem("cs_read"), i + 1)
                v.link(e.tensor_reduce(cst[:, 0, :], sc_c[:, :, :], AX.X, ALU.max))
                v.sig(e.tensor_tensor(sc_c[:, :, :], sc_c[:, :, :], w(0), ALU.subtract), sem("cs_sub"), i + 1)
                e.wait_ge(sem("cs_exp"), i + 1)
                v.link(e.tensor_tensor(sc_c[:, :, :], sc_c[:, :, :], m(cm), ALU.mult))
                v.link(e.tensor_reduce(cst[:, 1, :], sc_c[:, :, :], AX.X, ALU.add))
                v.link(e.tensor_scalar(cst[:, 1, :], cst[:, 1, :], 1e-30, None, ALU.max))
                v.link(e.reciprocal(cst[:, 2, :], cst[:, 1, :]))
                v.link(e.tensor_tensor(cst[:, 3, :], cst[:, 2, :], f1[:, i, GT:GT + QH], ALU.mult))
                for gr in range(KG):
                    src = sc_c[:, :, :].rearrange("p (j g) n -> p g j n", g=2)[:, gr]
                    wg = cst[:, 3, :].rearrange("p (j g) -> p g j", g=2)[:, gr].unsqueeze(2).to_broadcast([P, HPG, NCMP])
                    ins = e.tensor_tensor(pc[:, gr], src, wg, ALU.mult)
                    v.link(ins) if gr == 0 else v.sig(ins, sem("pc_done"), i + 1)
                e.wait_ge(sem("oc_ready"), i + 1)
                for gr in range(KG):
                    dst = yat[:, i, :].rearrange("p (j g d) -> p g j d", g=2, d=HD)[:, gr]
                    ins = e.tensor_copy(dst, bank[2 + gr][:, :].rearrange("p (j d) -> p j d", d=HD))
                    v.link(ins) if gr == 0 else v.sig(ins, sem("oc_done"), i + 1)

        UNITS = [(hb, b, i) for hb in range(2) for b in range(2) for i in range(NT)]
        NU, NBLK, LEAD = len(UNITS), QH // 2, 3
        SC_FREE, PB_FREE, PT_FREE, O_FREE = 4, 4, 4, 2

        def over_blocks(eng, block, chain=None, links=0):
            block(0, 0, True, False)
            with eng.Fori(0, NBLK - 2) as it:
                if chain:
                    chain.enter(it, links)
                block(it, 1, False, False)
                if chain:
                    chain.leave(NBLK - 2)
            block(0, NBLK - 1, False, True)

        def att_pool(g):
            for h in range(2):
                g.e.tensor_copy(qb[:, h, :], qT[:, h, :]).then_inc(sem("qb_in"), 1)
            with g.e.Fori(0, NBLK - 1) as it:
                for h in range(2):
                    g.e.wait_ge(sem("q_free"), it * 2 + h + 1)
                    g.e.wait_ge(sem("qb_in"), it * 2 + h + 2)
                    g.hold(spare[:, :])
                    g.e.tensor_copy(qb[:, h, :], qT[:, bass.ds(it * 2 + 2 + h, 1), :].rearrange("p a t -> p (a t)")).then_inc(sem("qb_in"), 1)

        def att_pe(pe):
            pe.sem_inc(sem("p_turned"), PB_FREE)
            pe.sem_inc(sem("pv_done"), PT_FREE)

            def scores(it, n0, u):
                hb, b, i = UNITS[u % NU]
                w = (i + 1) * P
                g, s = hb % KG, bank[u % 4]
                if u % 8 == 0:
                    pe.wait_ge(sem("qb_in"), it * 2 + ((n0 + u) // 8 + 1))
                pe.wait_ge(sem("p_sb"), it * NU + (n0 + u + 1))
                q = qb[:, hb, i * P:(i + 1) * P]
                pe.matmul(s[:, 0:w], q, kH[:, b, g, 0:w], start=True, stop=False)
                pe.matmul(s[:, 0:w], q, kL[:, b, g, 0:w], start=False, stop=False)
                pe.matmul(s[:, i * P:w], msk[:, 0, :], msk[:, 1, :], start=False, stop=True).then_inc(sem("s_psum"), 1)
                if u % 8 == 7:
                    pe.wait_ge(sem("s_psum"), it * NU + (n0 + u + 1))
                    pe.sem_inc(sem("q_free"), 1)

            def turn(it, n0, u):
                hb, b, i = UNITS[u]
                pe.wait_ge(sem("p_sb"), it * NU + (n0 + u + 1 + SC_FREE))
                pe.wait_ge(sem("pT_even" if u % 2 == 0 else "pT_odd"), it * (NU // 2) + ((n0 + u) // 2 + 1))
                for k in range(i + 1):
                    ins = pe.transpose(bank[4 + u % 2][:, k * P:(k + 1) * P], pb[:, u % 4, k * P:(k + 1) * P], ident)
                ins.then_inc(sem("p_turned"), 1)

            def values(it, n0, u):
                hb, b, i = UNITS[u % NU]
                pe.wait_ge(sem("pT_even" if u % 2 == 0 else "pT_odd"), it * (NU // 2) + ((n0 + u) // 2 + 2))
                if u % 8 == 0:
                    pe.wait_ge(sem("combined"), it * 2 + ((n0 + u) // 8 + 1))
                v0 = (VS if b == 0 else VW) + (hb % KG) * HD
                c = (b * NT + i) * HD
                for k in range(i + 1):
                    ins = pe.matmul(bank[6 + hb][:, c:c + HD], pT[:, u % 4, k * P:(k + 1) * P], f1[:, k, v0:v0 + HD],
                                    start=(k == 0), stop=(k == i))
                ins.then_inc(sem("pv_done"), 1)

            def block(it, blk, first, last):
                n0 = blk * NU
                for u in range(NU):
                    if not last or u + LEAD < NU:
                        scores(it, n0, u + LEAD)
                    turn(it, n0, u)
                    if not first or u >= 2:
                        values(it, n0, u - 2)
                if last:
                    values(it, n0, NU - 2)
                    values(it, n0, NU - 1)

            for u in range(LEAD):
                scores(0, 0, u)
            over_blocks(pe, block)

        def turned_out(eng, it, n0, u):
            hb, b, i = UNITS[u % NU]
            w, odd = (i + 1) * P, u % 2
            eng.wait_ge(sem("p_turned"), it * NU + (n0 + u + 1 + PB_FREE))
            eng.wait_ge(sem("pv_done"), it * NU + (n0 + u + 1))
            dst, src = pT[:, u % 4, 0:w], bank[4 + odd][:, 0:w]
            ins = eng.activation(dst, src, ACT.Copy) if odd else eng.tensor_scalar(dst, src, 1.0, None, ALU.mult)
            ins.then_inc(sem("pT_odd" if odd else "pT_even"), 1)

        def att_act(a):
            e = a.e
            e.sem_inc(sem("p_sb"), SC_FREE)
            e.sem_inc(sem("pT_odd"), 1)

            def block(it, blk, first, last):
                n0 = blk * NU
                for u, (hb, b, i) in enumerate(UNITS):
                    w = (i + 1) * P
                    if (u - LEAD) % 2 == 1 and (not first or u >= LEAD):
                        turned_out(e, it, n0, u - LEAD)
                    e.wait_ge(sem("s_max"), it * NU + (n0 + u + 1))
                    e.wait_ge(sem("p_turned"), it * NU + (n0 + u + 1))
                    e.activation(pb[:, u % 4, 0:w], bank[u % 4][:, 0:w], ACT.Exp, bias=nmax[:, u:u + 1],
                                 accum_out=rsum[:, u:u + 1]).then_inc(sem("p_sb"), 1)
                if last:
                    turned_out(e, it, n0, NU - 3)
                    turned_out(e, it, n0, NU - 1)
            over_blocks(e, block)

        def att_dve(v):
            e = v.e
            e.sem_inc(sem("pT_even"), 1)
            e.sem_inc(sem("combined"), O_FREE)

            def combine(it, n0, hb):
                h = n0 // 8 + hb
                hb = hb % 2
                e.wait_ge(sem("pv_done"), it * NU + (8 * h + 8 + PT_FREE))
                v.link(e.reciprocal(rsc[:, :], rsum[:, 8 * hb:8 * hb + 8]))
                v.link(e.tensor_tensor(rsc[:, :], rsc[:, :], gat[:, bass.ds(it * 2 + h, 1), :, :].rearrange("p a b i -> p (a b i)"), ALU.mult))
                v.sig(e.tensor_tensor(om[:, :, :, :].rearrange("p b i d -> p (b i) d"), bank[6 + hb][:, :].rearrange("p (u d) -> p u d", d=HD),
                                      rsc[:, :].unsqueeze(2).to_broadcast([P, 8, HD]), ALU.mult), sem("combined"), it * 2 + (h + 1 + O_FREE))
                v.link(e.tensor_tensor(om[:, 0], om[:, 0], om[:, 1], ALU.add))
                y = yat[:, :, bass.ds((it * 2 + h) * HD, HD)]
                v.link(e.tensor_tensor(y, y, om[:, 0], ALU.add))

            def block(it, blk, first, last):
                n0 = blk * NU
                for u, (hb, b, i) in enumerate(UNITS):
                    w = (i + 1) * P
                    e.wait_ge(sem("s_psum"), it * NU + (n0 + u + 1))
                    e.tensor_reduce(nmax[:, u:u + 1], bank[u % 4][:, 0:w], AX.X, ALU.max, negate=True).then_inc(sem("s_max"), 1)
                    if (u - LEAD) % 2 == 0 and (not first or u >= LEAD):
                        turned_out(e, it, n0, u - LEAD)
                    if u == 13:
                        combine(it, n0, 0)
                    if u == 5 and not first:
                        combine(it, n0, -1)
                if last:
                    turned_out(e, it, n0, NU - 2)
                    combine(it, n0, 1)
            over_blocks(e, block, v, 2 * 4)

        def yturn_pe(pe):
            for i in range(NT):
                for k in range(KD):
                    ins = pe.transpose(bank[2 * i + k // 4][:, (k % 4) * P:(k % 4 + 1) * P], yat[:, i, k * P:(k + 1) * P], ident)
                ins.then_inc(sem("turned"), 1)

        def yturn_act(a):
            for i in range(NT):
                a.e.wait_ge(sem("turned"), 16 + i + 1)
                for h in range(2):
                    hi, _, src = turned(DM, i, h)
                    a.sig(a.e.activation(hi, src, ACT.Copy), sem("high_done"), 32 + 2 * i + h + 1)

        def yturn_dve(v):
            for i in range(NT):
                for h in range(2):
                    v.e.wait_ge(sem("high_done"), 32 + 2 * i + h + 1)
                    hi, lo, src = turned(DM, i, h)
                    v.link(v.e.tensor_tensor(lo, src, hi.bitcast(F32), ALU.subtract))

        block = ctx.enter_context(nc.Block())

        @block.sync
        def _(sp):
            sp.dma_start(xres[:, :, :], x_d).then_inc(sem("loaded"), 16)
            sp.dma_start(con[:, :], consts).then_inc(sem("loaded"), 16)
            sp.dma_start(par[:, :], params).then_inc(sem("loaded"), 16)
            stream(sp)

        @block.gpsimd
        def _(pool):
            g = Chain(pool, sem("pool_chain"))
            pool.wait_ge(sem("loaded"), 48)
            g.link(pool.memset(spare[:, :], 0.0))
            meet(pool, 1)
            g.link(pool.memset(fT[:, :, 0:PAD], 0.0))
            meet(pool, 2)
            elem0_pool(g)
            meet(pool, 3)
            chunk_pool(g)
            meet(pool, 4)
            meet(pool, 5)
            meet(pool, 6)
            g.sig(pool.memset(ffo[:, :, :], 0.0), sem("ffo_zero"), 1)
            meet(pool, 7)
            meet(pool, 8)
            meet(pool, 9)
            prep_pool(g)
            meet(pool, 10)
            meet(pool, 11)
            att_pool(g)
            meet(pool, 12)
            meet(pool, 13)
            meet(pool, 14)
            g.sig(pool.memset(ffo[:, :, :], 0.0), sem("ffo_zero"), 2)
            meet(pool, 15)

        @block.tensor
        def _(pe):
            pe.sem_inc(sem("w_used"), RING)
            pe.wait_ge(sem("loaded"), 48)
            norm_pe(pe, 0, utok0)
            meet(pe, 1)
            proj0_pe(pe)
            meet(pe, 2)
            elem0_pe(pe)
            meet(pe, 3)
            chunk_pe(pe)
            meet(pe, 4)
            out0_pe(pe)
            meet(pe, 5)
            oproj_pe(pe, C_OUT0)
            norm_pe(pe, 1, utok)
            meet(pe, 6)
            mlp_pe(pe, C_MLP0, 0)
            meet(pe, 7)
            norm_pe(pe, 2, utok)
            meet(pe, 8)
            proj1_pe(pe)
            meet(pe, 9)
            prep_pe(pe)
            meet(pe, 10)
            cmp_pe(pe)
            meet(pe, 11)
            att_pe(pe)
            meet(pe, 12)
            yturn_pe(pe)
            meet(pe, 13)
            oproj_pe(pe, C_OUT1)
            norm_pe(pe, 3, utok)
            meet(pe, 14)
            mlp_pe(pe, C_MLP1, 1)
            meet(pe, 15)

        @block.scalar
        def _(act):
            a = Chain(act, sem("act_chain"))
            pre_in(act, 0, rowbuf)
            act.wait_ge(sem("loaded"), 48)
            norm_act(a, 0, D0, utok0)
            meet(act, 1)
            proj0_act(a)
            meet(act, 2)
            elem0_act(a)
            meet(act, 3)
            chunk_act(a)
            meet(act, 4)
            out0_act(a)
            meet(act, 5)
            oproj_act(a, 0, C_OUT0)
            post_act(a, 0)
            norm_act(a, 1, DM, utok)
            meet(act, 6)
            row_in(act, 1)
            pre_in(act, 2, prerow)
            mlp_act(a, C_MLP0, 0)
            meet(act, 7)
            post_act(a, 1)
            norm_act(a, 2, D1, utok)
            meet(act, 8)
            proj1_act(a)
            meet(act, 9)
            prep_act(a)
            meet(act, 10)
            cmp_act(a)
            meet(act, 11)
            att_act(a)
            meet(act, 12)
            yturn_act(a)
            meet(act, 13)
            oproj_act(a, 1, C_OUT1)
            post_act(a, 2)
            norm_act(a, 3, DM, utok)
            meet(act, 14)
            row_in(act, 3)
            mlp_act(a, C_MLP1, 1)
            meet(act, 15)
            post_act(a, 3)
            for i in range(NT):
                act.wait_ge(sem("x_updated"), 12 + i + 1)
                act.dma_start(out_d[:, i, :], xres[:, i, :]).then_inc(sem("out_stored"), 16)
            act.wait_ge(sem("out_stored"), 16 * NT)

        @block.vector
        def _(dve):
            v = Chain(dve, sem("dve_chain"))
            dve.wait_ge(sem("loaded"), 48)
            norm_dve(v, 0, D0, utok0, rowbuf)
            meet(dve, 1)
            proj0_dve(v)
            meet(dve, 2)
            elem0_dve(v)
            meet(dve, 3)
            chunk_dve(v)
            meet(dve, 4)
            out0_dve(v)
            meet(dve, 5)
            oproj_dve(v, 0, C_OUT0)
            post_dve(v, 0)
            norm_dve(v, 1, DM, utok, prerow)
            meet(dve, 6)
            mlp_dve(v, C_MLP0, 0)
            meet(dve, 7)
            post_dve(v, 1)
            norm_dve(v, 2, D1, utok, prerow)
            meet(dve, 8)
            proj1_dve(v)
            meet(dve, 9)
            prep_dve(v)
            meet(dve, 10)
            cmp_dve(v)
            meet(dve, 11)
            att_dve(v)
            meet(dve, 12)
            yturn_dve(v)
            meet(dve, 13)
            oproj_dve(v, 1, C_OUT1)
            post_dve(v, 2)
            norm_dve(v, 3, DM, utok, prerow)
            meet(dve, 14)
            mlp_dve(v, C_MLP1, 1)
            meet(dve, 15)
            post_dve(v, 3)


def chunks_of(w, cols, kper):
    k, n = w.shape[0] // P, w.shape[1] // cols
    a = w.reshape(k // kper, kper, P, n, cols).transpose(3, 0, 2, 1, 4)
    return a.reshape(n * (k // kper), P, kper * cols)


def kernel(**inputs):
    import numpy as _np
    import concourse.bacc as _bacc
    from concourse import mybir as _mybir
    from concourse.bass_utils import run_bass_kernel_spmd as _run

    w = {k: _np.asarray(v) for k, v in inputs.items()}

    def zeros(*s):
        return _np.zeros(s, _np.float32)

    def col(v):
        return v.reshape(-1, P).T

    ab = w["ab_w_in"][0]
    tb = _np.concatenate([ab[:, 0:1536], ab[:, 2056:3848]], 1)
    nq = w["nsa_w_in"][0]
    q = nq[:, 0:1024].reshape(D, KG, HPG, HD).transpose(0, 2, 1, 3).reshape(D, 1024)
    gates = nq[:, 1792:1840].reshape(D, KG, HPG, 3).transpose(0, 3, 2, 1).reshape(D, 48)
    in1 = _np.concatenate([q, nq[:, 1024:1792], gates, zeros(D, 2048 - 1840)], 1)
    wo1 = w["nsa_w_out"][0].reshape(KG, HPG, HD, D).transpose(1, 0, 2, 3).reshape(1024, D)
    parts = [chunks_of(tb, P, KD), chunks_of(ab[:, 1536:2048], 512, 2), zeros(2, P, D), w["ab_w_out"][0].reshape(KD, P, D)]
    half = FF // 2
    mlp = [[chunks_of(m, c, k) for f in range(2)
            for m, c, k in ((w["w_ffn_up"][l][:, f * half:(f + 1) * half], P, KD), (w["w_ffn_down"][l][f * half:(f + 1) * half], 512, 2))]
           for l in range(2)]
    parts += mlp[0] + [chunks_of(in1, 512, 2), chunks_of(w["nsa_w1_k"][0], 256, 4), chunks_of(w["nsa_w1_v"][0], 256, 4), wo1.reshape(KD, P, D)] + mlp[1]
    stream = _np.concatenate(parts, 0)

    def pos_embed(a):
        return a.reshape(16, 2 * HD).T

    par = {
        "conv": w["gdn_conv"][0].reshape(4, 12, P).transpose(2, 1, 0).reshape(P, 48),
        "gnorm": col(w["gdn_norm"][0]), "mu": col(w["rwkv_mu"][0]), "k_k": col(w["rwkv_k_k"][0]),
        "k_a": col(w["rwkv_k_a"][0]), "r_k": col(w["rwkv_r_k"][0].reshape(-1)), "a0": col(w["rwkv_a0"][0]),
        "pe_k": pos_embed(w["nsa_pe_k"][0]), "pe_v": pos_embed(w["nsa_pe_v"][0]),
        "ba": ab[:, 2048:2056].reshape(KD, P, 8).transpose(1, 0, 2).reshape(P, 64),
        "w2a2": _np.concatenate([w["rwkv_w2"][0], w["rwkv_a2"][0]], 0), "g2": w["rwkv_g2"][0],
        "w2k": w["nsa_w2_k"][0].reshape(2, P, HD).transpose(1, 0, 2).reshape(P, 128),
        "w2v": w["nsa_w2_v"][0].reshape(2, P, HD).transpose(1, 0, 2).reshape(P, 128),
        "alog": _np.broadcast_to(w["gdn_a_log"][0], (P, 4)), "dtb": _np.broadcast_to(w["gdn_dt_bias"][0], (P, 4)),
        "w0": _np.broadcast_to(w["rwkv_w0"][0], (P, 512)),
    }
    params = _np.concatenate([par[name] for name, _ in PAR_PARTS], 1)
    rows = _np.stack([w["norm_mix_post"][0], w["norm_ffn_post"][0], w["norm_mix_post"][1], w["norm_ffn_post"][1],
                      _np.concatenate([w["rwkv_ln_w"][0], w["rwkv_ln_b"][0]]),
                      w["norm_mix_pre"][0], w["norm_ffn_pre"][0], w["norm_mix_pre"][1], w["norm_ffn_pre"][1]])
    p = w["positions"][0]
    pc = _np.concatenate([p[31::16], p[-1:]])
    pos = _np.concatenate([p.reshape(NT, P).T, _np.concatenate([pc, pc, pc, pc])[:, None]], 1)

    nc = _bacc.Bacc("TRN2", target_bir_lowering=False, num_devices=1)
    arrays, args = {}, []
    for name, a in (("wstream", stream), ("x", w["x"][0]), ("pos", pos), ("params", params), ("consts", constants()), ("rows", rows)):
        a = _np.ascontiguousarray(a)
        arrays[f"in_{name}_dram"] = a
        args.append(nc.dram_tensor(f"in_{name}_dram", a.shape, _mybir.dt.from_np(a.dtype), kind="ExternalInput").ap())
    out = nc.dram_tensor("out_0_dram", (T, D), _mybir.dt.float32, kind="ExternalOutput").ap()
    program(nc, *args, out)
    r = _run(nc, [arrays], core_ids=[0])
    return r.results[0]["out_0_dram"].reshape(1, T, D)
```

```python
from contextlib import ExitStack

import numpy as np

import concourse.bass as bass
from concourse import mybir

F32 = mybir.dt.float32
F32R = mybir.dt.float32r
I32 = mybir.dt.int32
ALU = mybir.AluOpType
ACT = mybir.ActivationFunctionType
AX = mybir.AxisListType

P = 128
T = 512
NT = T // P
D = 1024
KD = D // P
FF = 4096
NF = FF // P
RING = 4
GH, RH = 4, 8
RP = RH // 2
PAD = 4
EPS = 1e-6
LN_EPS = 64e-5
QH, KG, HD = 16, 2, 64
HPG = QH // KG
NCMP = 32
HALF = 8
LEVELS = 7

C_IN0 = 0
N_IN0 = 31
C_OUT0 = 32
C_MLP0 = 40
C_IN1 = 104
C_CMP = 120
C_OUT1 = 128
C_MLP1 = 136
N_CHUNK = 200


def columns(parts):
    at, off = 0, {}
    for name, n in parts:
        off[name] = (at, at + n)
        at += n
    return off, at


CONST_PARTS = [("ident", P), ("ones", P), ("strict", P), ("incl", P), ("bones", P), ("cum", 2 * P + 2),
               ("level", LEVELS * P), ("level0t", P), ("row", 31), ("rows2", 32), ("first", 1), ("neg", P), ("cmask", NT * NCMP), ("cneg", NT * NCMP),
               ("ifreq", HALF), ("hsel", 4), ("eps", 4)]
C_OFF, C_N = columns(CONST_PARTS)
PAR_PARTS = [("conv", 48), ("gnorm", 1), ("mu", 14),
             ("k_k", 4), ("k_a", 4), ("r_k", 4), ("a0", 4), ("pe_k", 16), ("pe_v", 16),
             ("w2a2", 512), ("g2", 512), ("w2k", 128), ("w2v", 128), ("alog", 4), ("dtb", 4), ("w0", 512)]
P_OFF, P_N = columns(PAR_PARTS)


def constants():
    c = np.zeros((P, C_N), np.float32)

    def put(name, a):
        lo, hi = C_OFF[name]
        c[:, lo:hi] = np.asarray(a, np.float32).reshape(P, hi - lo)

    r, q = np.arange(P)[:, None], np.arange(P)[None, :]
    put("ident", r == q)
    put("ones", np.ones((P, P)))
    put("strict", r < q)
    put("incl", r <= q)
    put("bones", (r // 64) == (q // 64))
    half = (r < 64).astype(np.float32)
    cum = np.concatenate([(r < q) - half, (r <= q) - half, half, 1 - half], 1) * -np.exp(np.float32(-0.5))
    put("cum", cum)
    lev = [((r // (2 * b)) == (q // (2 * b))) & ((r // b) % 2 == 1) & ((q // b) % 2 == 0)
           for b in (1 << i for i in range(LEVELS))]
    put("level", np.stack(lev, 1))
    put("level0t", lev[0].T)
    put("row", np.broadcast_to(np.arange(31)[None] == 15, (P, 31)))
    put("rows2", np.arange(32)[None] == 15 + r // 64)
    put("first", r < P // 2)
    put("neg", np.where(q > r, -1e30, 0.0))
    t = np.arange(NT)[None, :, None] * P + np.arange(P)[:, None, None]
    n = np.arange(NCMP)[None, None, :]
    ok = (16 * n + 31 <= t) & (n < NCMP - 1)
    put("cmask", ok)
    put("cneg", np.where(ok, 0.0, -1e30))
    put("ifreq", np.broadcast_to(np.float32(500000.0) ** (-np.arange(HALF, dtype=np.float32) * np.float32(2.0 / 16)), (P, HALF)))
    put("hsel", (r // 32) == np.arange(4)[None, :])
    put("eps", np.broadcast_to(np.array([EPS, LN_EPS, 0.0, 0.0]), (P, 4)))
    return c


class Chain:

    def __init__(self, eng, sem):
        self.e, self.sem, self.base, self.n = eng, sem, 0, 0

    def link(self, ins):
        ins.then_inc(self.sem, 1)
        self.n += 1
        self.e.wait_ge(self.sem, self.base + self.n)

    def sig(self, ins, sem, value):
        ins.then_inc(sem, 1)
        self.e.wait_ge(sem, value)

    def hold(self, spare):
        self.e.tensor_tensor(spare, spare, spare, ALU.add)

    def enter(self, i, per):
        self.start, self.per = self.base + self.n, per
        self.base, self.n = self.start + i * per, 0

    def leave(self, times):
        assert self.n == self.per, f"links in the loop: {self.n}, declared {self.per}"
        self.base, self.n = self.start + self.per * times, 0


DVE_LINKS, ACT_LINKS, POOL_LINKS = 29, 13, 5


def program(nc, wstream, x, pos, params, consts, rows, out):
    with ExitStack() as ctx:
        sems = {}

        def sem(name):
            if name not in sems:
                sems[name] = ctx.enter_context(nc.semaphore(name))
            return sems[name]

        def sb(name, shape, dt=F32, c=ctx):
            return c.enter_context(nc.sbuf_tensor(name, shape, dt))

        bank = [ctx.enter_context(nc.psum_tensor(f"bank{i}", [P, 512], F32)) for i in range(8)]
        ring = sb("ring", [P, RING, D])
        con = sb("con", [P, C_N])
        par = sb("par", [P, P_N])
        xres = sb("xres", [P, NT, D])
        rowbuf = sb("rowbuf", [P, D])
        spare = sb("spare", [P, 1])
        spare_act = sb("spare_act", [P, 1])
        st = sb("st", [P, 32])

        def C(name):
            return con[:, C_OFF[name][0]:C_OFF[name][1]]

        def PR(name):
            return par[:, P_OFF[name][0]:P_OFF[name][1]]

        ident, ones, incl, bones = C("ident"), C("ones"), C("incl"), C("bones")
        eps = C("eps")[:, 0:1]
        ln_eps = C("eps")[:, 1:2]
        x_d = x.rearrange("(i p) d -> p i d", p=P)
        out_d = out.rearrange("(i p) d -> p i d", p=P)


        def dense(c, tag):
            return [sb(f"{n}{tag}", [P, k, w], F32R, c=c) for n, k, w in
                    (("uh", KD, T), ("ul", KD, T), ("wh", RING, D), ("wl", RING, D))]

        l0 = ExitStack()
        fT = sb("fT", [P, 26, PAD + T], c=l0)
        z = sb("z", [P, NT, 512], c=l0)
        lws = sb("lws", [P, NT, 512], c=l0)
        gst = sb("gst", [P, 4, 16], c=l0)
        gs = sb("gs", [P, NT, 7, GH], c=l0)
        QB, KB, VB, RB, KRB, VRB, WA, GD = 0, 4, 8, 12, 16, 20, 24, 25
        bonus = sb("bonus", [P, NT, RH], c=l0)
        l0p = ExitStack()
        D0 = dense(l0p, "0")
        utok0 = sb("utok0", [P, 2, D], c=l0p)
        baT = sb("baT", [2 * GH, T], c=l0p)
        tmpc = sb("tmpc", [P, 2, T], c=l0p)
        tmpd = sb("tmpd", [P, 2, T], c=l0p)
        l0p.close()
        kkT = sb("kkT", [P, 4, T], c=l0)
        aT = sb("aT", [P, 4, T], c=l0)
        l0s = ExitStack()
        sq = sb("sq", [P, 2, T], c=l0s)
        nr = sb("nr", [16, T], c=l0s)
        spread = sb("spread", [P, 12, P], c=l0s)
        rk = sb("rk", [P, 4, T], c=l0s)
        l0s.close()
        l0t = ExitStack()
        exq = sb("exq", [P, RP, 2 * P + 2], c=l0t)
        exn = sb("exn", [P, RP, P], c=l0t)
        RA = sb("RA", [P, RP, 2, P], c=l0t)
        NB = sb("NB", [P, RP, P], c=l0t)
        KT = sb("KT", [P, RP, P], c=l0t)
        KTt = sb("KTt", [P, RP, P], c=l0t)
        Vt = sb("Vt", [P, RP, P], c=l0t)
        Xb = sb("Xb", [P, 3, 4, P], c=l0t)
        Ti = sb("Ti", [P, 3, 4, P], c=l0t)
        TTi = sb("TTi", [P, 3, 4, P], c=l0t)
        KQ = sb("KQ", [P, GH, 2, P], c=l0t)
        vG = sb("vG", [P, GH, P], c=l0t)
        vR = sb("vR", [P, RP, P], c=l0t)
        lwt = sb("lwt", [P, 512], c=l0t)
        gB = sb("gB", [P, GH, P], c=l0t)
        Dn = sb("Dn", [P, GH, P], c=l0t)
        Ds = sb("Ds", [P, GH, P], c=l0t)
        kdt = sb("kdt", [P, GH, P], c=l0t)
        vGt = sb("vGt", [P, GH, P], c=l0t)
        S = sb("S", [P, GH, P], c=l0t)
        Sr = sb("Sr", [P, RP, P], c=l0t)
        sm = sb("sm", [P, 7, GH], c=l0t)
        VV = sb("VV", [P, GH, P], c=l0t)
        VN = sb("VN", [P, GH, P], c=l0t)
        O1 = sb("O1", [P, 512], c=l0t)
        Wb = sb("Wb", [P, RP, P], c=l0t)
        NBt = exn
        Ub = vGt[:, :, :].rearrange("p a c -> p (a c)")
        SC = xres[:, :, :].rearrange("p a (b c) -> p (a b) c", b=2)
        l0t.close()
        l0m = ExitStack()
        o_n = sb("o_n", [P, NT, 512], c=l0m)
        y_n = sb("y_n", [P, NT, 512], c=l0m)
        t1 = sb("t1", [P, NT, 512], c=l0m)
        t2 = kkT
        hst = sb("hst", [P, 8, NT, RH], c=l0m)
        l0m.close()
        l0.close()
        ml = ExitStack()
        HF = NF // 2
        mh = ExitStack()
        hh = sb("hh", [P, HF, T], F32R, c=mh)
        hl = sb("hl", [P, HF, T], F32R, c=mh)
        mh.close()
        utok = sb("utok", [P, 2, D], c=ml)
        sb("rest", [P, 2 * HF * T - 2 * D], c=ml)
        wh_m, wl_m = (sb(n, [P, RING, D], F32R, c=ml) for n in ("wh_m", "wl_m"))
        ffo = sb("ffo", [P, NT, D], c=ml)
        prerow = sb("prerow", [P, D], c=ml)
        uh_m, ul_m = (sb(n, [P, KD, T], F32R, c=ml) for n in ("uh_m", "ul_m"))
        DM = [uh_m, ul_m, wh_m, wl_m]
        hraw = sb("hraw", [P, 2, T], c=ml)
        ml.close()


        def meet(eng, n):
            eng.drain().then_inc(sem("stage_done"), 1)
            eng.wait_ge(sem("stage_done"), 4 * n)

        slot_sems = [sem(f"w_loaded{s}") for s in range(RING)]

        def slot(c):
            return ring[:, c % RING, :]

        def stream(sp):
            for c in range(RING):
                sp.dma_start(slot(c), wstream[c]).then_inc(slot_sems[c], 16)
            with sp.Fori(0, N_CHUNK // RING - 1) as it:
                for c in range(RING):
                    sp.wait_ge(sem("w_lo"), it * RING + c + 1)
                    sp.dma_start(slot(c), wstream[bass.ds(it * RING + RING + c, 1)].rearrange("a p d -> (a p) d")).then_inc(slot_sems[c], 16)

        def split_hi(a, dn, c, it=0, per=0):
            a.e.wait_ge(slot_sems[c % RING], it * (16 * per // RING) + 16 * (c // RING + 1))
            a.e.wait_ge(sem("w_used"), it * per + c + 1)
            a.sig(a.e.activation(dn[2][:, c % RING, :], slot(c), ACT.Copy), sem("w_hi"), it * per + c + 1)

        def used(eng, c, it=0, per=0):
            eng.wait_ge(sem("w_used"), it * per + (c + 1 + RING))

        def split_lo(v, dn, c, it=0, per=0):
            v.e.wait_ge(sem("w_hi"), it * per + c + 1)
            v.sig(v.e.tensor_tensor(dn[3][:, c % RING, :], slot(c), dn[2][:, c % RING, :].bitcast(F32), ALU.subtract), sem("w_lo"), it * per + c + 1)

        def weights(pe, c, it=0, per=0):
            pe.wait_ge(sem("w_lo"), it * per + c + 1)

        def mm3(pe, out, lh, ll, rh, rl, start, stop):
            pe.matmul(out, lh, rh, start=start, stop=False)
            pe.matmul(out, lh, rl, start=False, stop=False)
            return pe.matmul(out, ll, rh, start=False, stop=stop)

        NORM_TURN = (0, 2, 3, 5)

        def norm_pe(pe, c, ut):
            if c % 2:
                pe.wait_ge(sem("ffo_left"), 4 * (c // 2) + 4)
                pe.wait_ge(sem("ffo_right"), 4 * (c // 2) + 4)
            for i in range(NT):
                pe.wait_ge(sem("norm_u"), 4 * c + i + 1)
                for k in range(KD):
                    ins = pe.transpose(bank[2 * i + k // 4][:, (k % 4) * P:(k % 4 + 1) * P],
                                       ut[:, i % 2, k * P:(k + 1) * P], ident)
                ins.then_inc(sem("turned"), 1)

        def turned(dn, i, h):
            v = (slice(None), slice(4 * h, 4 * h + 4), slice(i * P, (i + 1) * P))
            return dn[0][v], dn[1][v], bank[2 * i + h][:, :].rearrange("p (k t) -> p k t", k=4)

        def norm_act(a, c, dn, ut):
            def high(i):
                a.e.wait_ge(sem("turned"), 4 * NORM_TURN[c] + i + 1)
                for h in range(2):
                    hi, _, src = turned(dn, i, h)
                    a.sig(a.e.activation(hi, src, ACT.Copy), sem("high_done"), 8 * NORM_TURN[c] + 2 * i + h + 1)
            for i in range(NT):
                if c > 0:
                    a.e.wait_ge(sem("x_updated"), 4 * (c - 1) + i + 1)
                if i >= 2:
                    a.e.wait_ge(sem("turned"), 4 * NORM_TURN[c] + i - 1)
                a.link(a.e.activation(ut[:, i % 2, :], xres[:, i, :], ACT.Square, accum_out=st[:, i:i + 1]))
                a.sig(a.e.activation(st[:, 4 + i:5 + i], st[:, i:i + 1], ACT.Sqrt, bias=eps, scale=1.0 / D),
                      sem("norm_root"), 4 * c + i + 1)
                if i >= 1:
                    high(i - 1)
            high(NT - 1)

        def norm_dve(v, c, dn, ut, row):
            def low(i):
                for h in range(2):
                    hi, lo, src = turned(dn, i, h)
                    v.e.wait_ge(sem("high_done"), 8 * NORM_TURN[c] + 2 * i + h + 1)
                    v.link(v.e.tensor_tensor(lo, src, hi.bitcast(F32), ALU.subtract))
            v.e.wait_ge(sem("pre_loaded"), 16 * (c + 1))
            for i in range(NT):
                v.e.wait_ge(sem("norm_root"), 4 * c + i + 1)
                v.link(v.e.reciprocal(st[:, 8 + i:9 + i], st[:, 4 + i:5 + i]))
                v.sig(v.e.scalar_tensor_tensor(ut[:, i % 2, :], xres[:, i, :], st[:, 8 + i:9 + i], row[:, :], ALU.mult, ALU.mult),
                      sem("norm_u"), 4 * c + i + 1)
                if i >= 1:
                    low(i - 1)
            low(NT - 1)

        def pre_in(act, c, row):
            act.dma_start(row[:, :], rows[5 + c:6 + c, :].to_broadcast([P, D])).then_inc(sem("pre_loaded"), 16)

        def post_act(a, c):
            for i in range(NT):
                if i >= 2:
                    a.e.wait_ge(sem("post_root"), 4 * c + i - 1)
                a.link(a.e.activation(utok[:, i % 2, :], ffo[:, i, :], ACT.Square, accum_out=st[:, 16 + i:17 + i]))
                a.sig(a.e.activation(st[:, 20 + i:21 + i], st[:, 16 + i:17 + i], ACT.Sqrt, bias=eps, scale=1.0 / D),
                      sem("post_root"), 4 * c + i + 1)

        def post_dve(v, c):
            v.e.wait_ge(sem("row_loaded"), 16 * (c + 1))
            for i in range(NT):
                v.e.wait_ge(sem("post_root"), 4 * c + i + 1)
                v.link(v.e.reciprocal(st[:, 24 + i:25 + i], st[:, 20 + i:21 + i]))
                v.link(v.e.scalar_tensor_tensor(ffo[:, i, :], ffo[:, i, :], st[:, 24 + i:25 + i], rowbuf[:, :],
                                                ALU.mult, ALU.mult))
                v.sig(v.e.tensor_tensor(xres[:, i, :], xres[:, i, :], ffo[:, i, :], ALU.add),
                      sem("x_updated"), 4 * c + i + 1)

        N_LOOP, BODY, NTB = 3, 8, 27

        def F(b):
            return fT[:, b, PAD:]

        def blk_of(it, s, lo=PAD, n=T):
            b = it * 4 + (s if s < 4 else 8 + s)
            return fT[:, bass.ds(b, 1), lo:lo + n].rearrange("p a t -> p (a t)")


        def proj0_pe(pe):
            uh, ul, wh, wl = D0

            def blk(c, b, it, per, wait):
                weights(pe, c, it, per)
                pe.wait_ge(sem("fT_even" if b % 2 == 0 else "fT_odd"), wait)
                for k in range(KD):
                    w = slice(k * P, (k + 1) * P)
                    ins = mm3(pe, bank[b][:, :], wh[:, c % RING, w], wl[:, c % RING, w], uh[:, k, :], ul[:, k, :], k == 0, k == KD - 1)
                ins.then_inc(sem("w_used"), 1)
            with pe.Fori(0, N_LOOP) as it:
                for s in range(BODY):
                    blk(s, s, it, BODY, it * 4 + s // 2 + 1)
            for b in range(2):
                blk(24 + b, b, 0, 0, N_LOOP * 4 + 1)
            for nm in ("fT_even", "fT_odd"):
                pe.wait_ge(sem(nm), N_LOOP * 4 + 4)
            blk(26, 2, 0, 0, N_LOOP * 4 + 4)
            for c in range(NTB, N_IN0):
                weights(pe, c)
                for kk in range(2):
                    k = 2 * (c - NTB) + kk
                    for i in range(NT):
                        t, w = slice(i * P, (i + 1) * P), slice(kk * 512, (kk + 1) * 512)
                        ins = mm3(pe, bank[4 + i][:, :], uh[:, k, t], ul[:, k, t], wh[:, c % RING, w], wl[:, c % RING, w], k == 0, k == KD - 1)
                ins.then_inc(sem("w_used"), 1)
            pe.wait_ge(sem("ba_sb"), 1)
            for i in range(NT):
                ins = pe.transpose(bank[3][:, 8 * i:8 * i + 8], baT[:, i * P:(i + 1) * P], ident[0:8, 0:8])
            ins.then_inc(sem("zba_ready"), 1)
            for c in (N_IN0,):
                pass_over(pe, c)
                pe.sem_inc(sem("w_used"), 1)

        def pass_over(pe, c):
            pe.wait_ge(slot_sems[c % RING], 16 * (c // RING + 1))
            pe.wait_ge(sem("w_lo"), c)
            for nm in ("w_hi", "w_lo"):
                pe.sem_inc(sem(nm), 1)

        def proj0_dve(v):
            v.e.sem_inc(sem("fT_even"), 4)
            v.e.sem_inc(sem("shifted"), 2)

            def conv(it, s):
                if s % 2 == 1:
                    v.e.wait_ge(sem("fT_odd"), it * 4 + 5 + s // 2)
                v.e.wait_ge(sem("silu"), it * 4 + s + 1)
                cw = lambda i: PR("conv")[:, bass.ds(it * 16 + 4 * s + i, 1)]
                acc = tmpc[:, s % 2, :]
                v.link(v.e.tensor_scalar(acc, blk_of(it, s, 1), cw(0), None, ALU.mult))
                for i in range(1, 4):
                    ins = v.e.scalar_tensor_tensor(acc, blk_of(it, s, 1 + i), cw(i), acc, ALU.mult, ALU.add)
                    v.link(ins) if i < 3 else v.sig(ins, sem("conv_done"), it * 4 + s + 1)

            def shift(it, s):
                v.e.wait_ge(sem("diff"), it * 4 + s - 4 + 2)
                v.sig(v.e.scalar_tensor_tensor(blk_of(it, s), tmpd[:, s % 2, :], PR("mu")[:, bass.ds(it * 4 + s - 4, 1)], blk_of(it, s), ALU.mult, ALU.add),
                      sem("shifted"), it * 4 + s - 4 + 3)

            for c in range(2):
                split_lo(v, D0, c)
            with v.e.Fori(0, N_LOOP) as it:
                v.enter(it, 4 * 3)
                for s in range(BODY):
                    split_lo(v, D0, s + 2, it, BODY)
                    if s % 2 == 0:
                        used(v.e, s, it, BODY)
                        v.sig(v.e.tensor_scalar(blk_of(it, s), bank[s][:, :], 1.0, None, ALU.mult), sem("fT_even"), it * 4 + 4 + s // 2 + 1)
                    if 1 <= s <= 4:
                        conv(it, s - 1)
                    elif s > 4:
                        shift(it, s - 1)
                shift(it, BODY - 1)
                v.leave(N_LOOP)
            for c in range(26, N_IN0):
                split_lo(v, D0, c)
                if c == 28:
                    used(v.e, 26)
                    v.sig(v.e.tensor_copy(baT[:, :], bank[2][0:8, :]), sem("ba_sb"), 1)
                if c == 26:
                    used(v.e, 24)
                    v.sig(v.e.tensor_copy(fT[:, 24, PAD:], bank[0][:, :]), sem("fT_even"), N_LOOP * 4 + 5)
                if c in (27, 28):
                    j = c - 27 + 12
                    v.e.wait_ge(sem("diff"), j + 2)
                    v.sig(v.e.scalar_tensor_tensor(F(RB + j), tmpd[:, j % 2, :], PR("mu")[:, j:j + 1], F(RB + j), ALU.mult, ALU.add),
                          sem("shifted"), j + 3)
            v.e.wait_ge(sem("zba_ready"), 1)
            for i in range(0, NT, 2):
                v.link(v.e.tensor_copy(z[:, i, :], bank[4 + i][:, :]))
            ba = bank[3][:, 0:32].rearrange("p (i c) -> p i c", i=NT)
            v.link(v.e.tensor_copy(gst[:, 0, :].rearrange("p (i c) -> p i c", i=NT), ba[:, :, 0:4]))
            v.link(v.e.tensor_tensor(gst[:, 1, :].rearrange("p (i c) -> p i c", i=NT), ba[:, :, 4:8],
                                     PR("dtb").unsqueeze(1).to_broadcast([P, NT, GH]), ALU.add))

        def proj0_pool(g):
            g.e.sem_inc(sem("diff"), 1)
            with g.e.Fori(0, N_LOOP) as it:
                for s in range(4, BODY):
                    g.e.wait_ge(sem("fT_odd" if s % 2 else "fT_even"), it * 4 + 4 + s // 2 + 1)
                    g.e.wait_ge(sem("shifted"), it * 4 + s - 4 + 1)
                    g.e.wait_ge(sem("diff"), it * 4 + s - 4 + 1)
                    g.hold(spare[:, :])
                    g.e.tensor_tensor(tmpd[:, s % 2, :], blk_of(it, s, PAD - 1), blk_of(it, s), ALU.subtract).then_inc(sem("diff"), 1)
            for j in (12, 13):
                g.e.wait_ge(sem("fT_odd" if j % 2 else "fT_even"), N_LOOP * 4 + 5)
                g.e.wait_ge(sem("shifted"), j + 1)
                b = RB + j
                g.e.tensor_tensor(tmpd[:, j % 2, :], fT[:, b, PAD - 1:PAD - 1 + T], F(b), ALU.subtract).then_inc(sem("diff"), 1)

        def proj0_act(a):
            a.e.sem_inc(sem("fT_odd"), 4)
            a.e.sem_inc(sem("silu"), 2)
            for c in range(2):
                split_hi(a, D0, c)
            with a.e.Fori(0, N_LOOP) as it:
                for s in range(BODY):
                    split_hi(a, D0, s + 2, it, BODY)
                    if s % 2 == 1 or s == 2 or s == 4:
                        if s % 2 == 1:
                            used(a.e, s, it, BODY)
                        if 2 <= s <= 5:
                            a.e.wait_ge(sem("conv_done"), it * 4 + s - 1)
                        a.e.activation(spare_act[:, :], eps, ACT.Copy)
                    if s % 2 == 1:
                        a.e.activation(blk_of(it, s), bank[s][:, :], ACT.Copy).then_inc(sem("fT_odd"), 1)
                    if 2 <= s <= 5:
                        a.e.activation(blk_of(it, s - 2), tmpc[:, s % 2, :], ACT.Silu).then_inc(sem("silu"), 1)
            for c in range(26, N_IN0):
                split_hi(a, D0, c)
                if c == 27:
                    used(a.e, 25)
                    a.sig(a.e.activation(fT[:, 25, PAD:], bank[1][:, :], ACT.Copy), sem("fT_odd"), N_LOOP * 4 + 5)
            a.e.wait_ge(sem("zba_ready"), 1)
            for i in range(1, NT, 2):
                a.link(a.e.activation(z[:, i, :], bank[4 + i][:, :], ACT.Copy))

        def elem0_pool(g):
            g.link(g.e.tensor_copy(spread[:, 0:8, :], ident[:, 0:8].unsqueeze(2).to_broadcast([P, 8, P])))
            g.sig(g.e.tensor_copy(spread[:, 8:12, :].rearrange("p b (h c) -> p (b h) c", h=2), ident[:, 8:16].unsqueeze(2).to_broadcast([P, 8, 64])),
                  sem("by_pool"), 1)

        def elem0_dve(v):
            v.e.wait_ge(sem("a_done"), 4)
            for b in range(4):
                v.link(v.e.tensor_scalar(rk[:, b, :], aT[:, b, :], -1.0, PR("k_a")[:, b:b + 1], ALU.add, ALU.mult))
                v.link(v.e.scalar_tensor_tensor(F(KRB + b), rk[:, b, :], 1.0, F(KRB + b), ALU.add, ALU.mult))
                v.sig(v.e.scalar_tensor_tensor(rk[:, b, :], F(RB + b), PR("r_k")[:, b:b + 1], F(KRB + b), ALU.mult, ALU.mult),
                      sem("rk_done"), b + 1)
            v.e.wait_ge(sem("root"), 1)
            v.sig(v.e.reciprocal(nr[:, :], nr[:, :]), sem("inv_norm"), 1)
            for j in range(12):
                v.e.wait_ge(sem("spread"), j + 1)
                n = bank[j % 4][:, :]
                if j < 4:
                    ins = v.e.scalar_tensor_tensor(F(j), F(j), float(P) ** -0.5, n, ALU.mult, ALU.mult)
                elif j < 8:
                    ins = v.e.tensor_tensor(F(j), F(j), n, ALU.mult)
                else:
                    ins = v.e.tensor_tensor(kkT[:, j - 8, :], kkT[:, j - 8, :], n, ALU.mult)
                v.sig(ins, sem("normed"), j + 1)
                if j >= 8:
                    v.link(v.e.scalar_tensor_tensor(aT[:, j - 8, :], kkT[:, j - 8, :], -1.0, aT[:, j - 8, :], ALU.mult, ALU.mult))
            v.e.wait_ge(sem("bonus_ready"), 1)
            v.link(v.e.tensor_copy(bonus[:, :, :], bank[6][:, 0:NT * RH].rearrange("p (i h) -> p i h", i=NT)))
            v.e.wait_ge(sem("gate_ln"), 1)
            v.link(v.e.scalar_tensor_tensor(gst[:, 2, :], gst[:, 1, :], 0.0, gst[:, 2, :], ALU.max, ALU.add))
            v.e.wait_ge(sem("gate_a"), 1)
            sp = gst[:, 2, :].rearrange("p (i h) -> p i h", i=NT)
            g3 = gst[:, 3, 0:4].unsqueeze(1).to_broadcast([P, NT, GH])
            v.link(v.e.tensor_tensor(sp, sp, g3, ALU.mult))
            v.sig(v.e.tensor_scalar(gs[:, :, 0, :], sp, -1.0, None, ALU.mult), sem("g_done"), 1)
            v.link(v.e.tensor_copy(gs[:, :, 3, :], gst[:, 0, :].rearrange("p (i h) -> p i h", i=NT)))
            v.link(v.e.tensor_scalar(gs[:, :, 6, :], gst[:, 0, :].rearrange("p (i h) -> p i h", i=NT), -1.0, None, ALU.mult))
            v.e.wait_ge(sem("gc_ready"), 1)
            gc = bank[7][:, 0:16].rearrange("p (i h) -> p i h", i=NT)
            gt = bank[7][:, 16:32].rearrange("p (i h) -> p i h", i=NT)
            v.link(v.e.tensor_copy(gs[:, :, 1, :], gc))
            v.link(v.e.tensor_copy(gs[:, :, 5, :], gt))
            v.sig(v.e.tensor_tensor(gs[:, :, 4, :], gs[:, :, 5, :], gs[:, :, 1, :], ALU.subtract), sem("gc_sb"), 1)
            v.e.wait_ge(sem("gexp_done"), 1)
            v.link(v.e.tensor_scalar(gs[:, :, 2, :], gs[:, :, 2, :], -1.0, None, ALU.mult))

        def elem0_act(a):
            a.sig(a.e.activation(fT[0:64, WA, PAD:], fT[0:64, WA, PAD:], ACT.Tanh), sem("wd_tanh"), 1)
            a.link(a.e.activation(F(GD), F(GD), ACT.Sigmoid))
            for b in range(4):
                a.link(a.e.activation(kkT[:, b, :], F(KRB + b), ACT.Copy, scale=PR("k_k")[:, b:b + 1]))
            a.link(a.e.activation(gst[:, 0, :], gst[:, 0, :], ACT.Sigmoid))
            for b in range(4):
                a.e.wait_ge(sem("a_ready"), b + 1)
                a.sig(a.e.activation(aT[:, b, :], bank[b][:, :], ACT.Sigmoid, bias=PR("a0")[:, b:b + 1]), sem("a_done"), b + 1)
            for i in range(NT):
                a.e.wait_ge(sem("lw_ready"), i + 1)
                a.sig(a.e.activation(lws[:, i, :], bank[4 + i][:, :], ACT.Sigmoid), sem("lw_done"), i + 1)
            for j in range(12):
                if j >= 2:
                    a.e.wait_ge(sem("ss_ready"), j - 1)
                a.e.activation(sq[:, j % 2, :], F(j) if j < 8 else kkT[:, j - 8, :], ACT.Square).then_inc(sem("sq_done"), 1)
            a.e.wait_ge(sem("ss_ready"), 12)
            a.sig(a.e.activation(nr[:, :], bank[0][0:16, :], ACT.Sqrt, bias=eps[0:16]), sem("root"), 1)
            a.link(a.e.activation(gst[:, 2, :], gst[:, 1, :], ACT.Abs))
            a.link(a.e.activation(gst[:, 2, :], gst[:, 2, :], ACT.Exp, scale=-1.0))
            a.sig(a.e.activation(gst[:, 2, :], gst[:, 2, :], ACT.Ln, bias=1.0), sem("gate_ln"), 1)
            a.sig(a.e.activation(gst[:, 3, 0:4], PR("alog"), ACT.Exp), sem("gate_a"), 1)
            a.e.wait_ge(sem("gc_sb"), 1)
            a.link(a.e.activation(gs[:, :, 2, :], gs[:, :, 1, :], ACT.Exp))
            a.link(a.e.activation(gs[:, :, 4, :], gs[:, :, 4, :], ACT.Exp))
            a.sig(a.e.activation(gs[:, :, 5, :], gs[:, :, 5, :], ACT.Exp), sem("gexp_done"), 1)

        def elem0_pe(pe):
            for b in range(4):
                pe.matmul(bank[b][:, :], PR("w2a2")[64:128, b * P:(b + 1) * P], fT[64:128, WA, PAD:],
                          start=True, stop=True).then_inc(sem("a_ready"), 1)
            pe.wait_ge(sem("wd_tanh"), 1)
            for i in range(NT):
                pe.matmul(bank[4 + i][:, :], fT[0:64, WA, PAD + i * P:PAD + (i + 1) * P], PR("w2a2")[0:64, :],
                          start=True, stop=False)
                pe.matmul(bank[4 + i][:, :], ones[0:1, :], PR("w0")[0:1, :], start=False, stop=True).then_inc(sem("lw_ready"), 1)
            pe.wait_ge(sem("a_done"), 4)
            for j in range(12):
                pe.wait_ge(sem("sq_done"), j + 1)
                window = C("row")[:, 15 - j:31 - j] if j < 8 else C("rows2")[:, 23 - 2 * j:39 - 2 * j]
                pe.matmul(bank[0][0:16, :], window, sq[:, j % 2, :], start=(j == 0), stop=(j == 11)).then_inc(sem("ss_ready"), 1)
            pe.wait_ge(sem("inv_norm"), 1)
            pe.wait_ge(sem("by_pool"), 1)
            for j in range(12):
                if j >= 4:
                    pe.wait_ge(sem("normed"), j - 3)
                pe.matmul(bank[j % 4][:, :], spread[0:16, j, :], nr[:, :], start=True, stop=True).then_inc(sem("spread"), 1)
            pe.wait_ge(sem("rk_done"), 4)
            pe.wait_ge(sem("lw_done"), 4)
            for i in range(NT):
                for b in range(4):
                    ins = pe.matmul(bank[6][:, i * RH + 2 * b:i * RH + 2 * b + 2], rk[:, b, i * P:(i + 1) * P], bones[:, 0:P:64],
                                    start=True, stop=True)
            ins.then_inc(sem("bonus_ready"), 1)
            pe.wait_ge(sem("g_done"), 1)
            pe.matmul(bank[7][:, 0:16].rearrange("p (i h) -> p i h", i=NT), incl, gs[:, :, 0, :], start=True, stop=True)
            pe.matmul(bank[7][:, 16:32].rearrange("p (i h) -> p i h", i=NT), ones, gs[:, :, 0, :], start=True, stop=True).then_inc(sem("gc_ready"), 1)

        def AT(g, q):
            return Ds[:, q, :] if g == 0 else SC[:, 4 * (g - 1) + q, 0:P]

        def ATg(g):
            return Ds[:, :, :] if g == 0 else SC[:, 4 * (g - 1):4 * g, 0:P]

        BANK_A, BANK_B = (6, 0, 2), (7, 1, 3)
        X_PER, TT_PER = 3 * (LEVELS - 1), 3 * (LEVELS - 2)

        def tcol(n):
            return bass.ds(n * P + PAD, P)

        def b4(i):
            return bank[i][:, :].rearrange("p (h c) -> p h c", h=4)

        def rep4(m):
            return m.unsqueeze(1).to_broadcast([P, 4, P])

        def cols(m, lv, second):
            return m.rearrange("p q (m two b) -> p q m two b", two=2, b=1 << lv)[:, :, :, second, :]

        def chunk_pool(g):
            e = g.e
            g.link(e.memset(S[:, :, :], 0.0))
            g.link(e.memset(Xb[:, :, :, :], 0.0))
            g.link(e.memset(Sr[:, :, :], 0.0))
            e.sem_inc(sem("state_init"), 1)

            def fetch(n):
                e.tensor_copy(lwt[:, :], lws[:, bass.ds(n, 1), :].rearrange("p a c -> p (a c)")).then_inc(sem("lwt_in"), 1)
                e.tensor_copy(KQ[:, :, 0, :], fT[:, KB:KB + 4, tcol(n)])
                e.tensor_copy(KQ[:, :, 1, :], fT[:, QB:QB + 4, tcol(n)]).then_inc(sem("kq_in"), 1)
                e.tensor_copy(gB[:, :, :], gs[:, bass.ds(n, 1), 0, :].rearrange("p a h -> p (a h)").unsqueeze(2).to_broadcast([P, GH, P])).then_inc(sem("gB_in"), 1)
                e.tensor_copy(vG[:, :, :], fT[:, VB:VB + 4, tcol(n)]).then_inc(sem("vG_in"), 1)
                e.tensor_copy(vR[:, :, :], fT[:, VRB:VRB + 4, tcol(n)]).then_inc(sem("vR_in"), 1)

            def chunk(n, last):
                e.wait_ge(sem("state_done"), n + 1)
                if not last:
                    g.hold(spare[:, :])
                e.tensor_copy(sm[:, :, :], gs[:, bass.ds(n, 1), :, :].rearrange("p a c h -> p (a c) h")).then_inc(sem("sm_in"), 1)
                e.wait_ge(sem("d_exp"), n + 1)
                g.link(e.tensor_tensor(Ds[:, :, :], Dn[:, :, :], rep4(C("strict")), ALU.mult))
                g.sig(e.tensor_tensor(Dn[:, :, :], Dn[:, :, :], rep4(incl), ALU.mult), sem("d_masked"), n + 1)
                for q in range(3):
                    if q == 0:
                        e.wait_ge(sem("qk_masked"), n + 1)
                    else:
                        e.wait_ge(sem("sc_sb"), RH * n + 4 * q)
                    g.link(e.tensor_tensor(TTi[:, q], ATg(q), rep4(C("level0t")), ALU.mult))
                    g.sig(e.tensor_tensor(TTi[:, q], TTi[:, q], rep4(ident), ALU.add), sem("tt_init"), 3 * n + q + 1)
                e.wait_ge(sem("vrt_sb"), n + 1)
                if not last:
                    g.hold(spare[:, :])
                g.link(e.tensor_copy(fT[:, VRB:VRB + 4, tcol(n)], Vt[:, :, :]))
                if not last:
                    fetch(n + 1)

            fetch(0)
            with e.Fori(0, NT - 1) as n:
                g.enter(n, POOL_LINKS)
                chunk(n, False)
                g.leave(NT - 1)
            chunk(NT - 1, True)

        def chunk_pe(pe):
            def turn(src, dst, event):
                for q in range(4):
                    ins = pe.transpose(bank[dst][:, q * P:(q + 1) * P], src[:, q, :], ident)
                ins.then_inc(sem(event), 1)

            pe.wait_ge(sem("state_init"), 1)
            with pe.Fori(0, NT) as n:
                pe.wait_ge(sem("lwt_in"), n + 1)
                for b in range(RP):
                    pe.matmul(bank[b][:, 0:2 * P + 2], lwt[:, b * P:(b + 1) * P], C("cum"), start=True, stop=True).then_inc(sem("cum_ready"), 1)
                pe.wait_ge(sem("gB_in"), n + 1)
                for h in range(GH):
                    ins = pe.matmul(bank[6][:, h * P:(h + 1) * P], gB[:, h, :], incl, start=True, stop=True)
                ins.then_inc(sem("gbc_ready"), 1)
                pe.wait_ge(sem("kq_in"), n + 1)
                for h in range(GH):
                    c = (h % 2) * 2 * P
                    ins = pe.matmul(bank[4 + h // 2][:, c:c + 2 * P].rearrange("p (a t) -> p a t", a=2), KQ[:, h, 0, :], KQ[:, h, :, :],
                                    start=True, stop=True)
                ins.then_inc(sem("kkq_ready"), 1)
                pe.wait_ge(sem("vG_in"), n + 1)
                turn(vG, 7, "vg_turned")
                pe.wait_ge(sem("d_made"), n + 1)
                for h in range(GH):
                    ins = pe.matmul(bank[6][:, h * P:(h + 1) * P], KQ[:, h, 0, :], S[:, h, :], start=True, stop=True)
                ins.then_inc(sem("ks_ready"), 1)
                pe.wait_ge(sem("vgt_sb"), n + 1)
                for h in range(GH):
                    ins = pe.transpose(bank[7][:, h * P:(h + 1) * P], KQ[:, h, 0, :], ident)
                ins.then_inc(sem("k_turned"), 1)
                pe.wait_ge(sem("rk_ready"), n + 1)
                for h in range(RH):
                    p, r = h // 2, slice(64 * (h % 2), 64 * (h % 2) + 64)
                    if h < 4:
                        pe.wait_ge(sem("cum_read"), RP * n + h + 1)
                    else:
                        pe.wait_ge(sem("sc_sb"), RH * n + h - 3)
                    pe.matmul(bank[h % 4][:, 0:256], NB[r, p, :], RA[r, p].rearrange("p a t -> p (a t)"), start=True, stop=True)
                    pe.matmul(bank[h % 4][:, 256:512], KT[r, p, :], RA[r, p].rearrange("p a t -> p (a t)"),
                              start=True, stop=True).then_inc(sem("sc_ready"), 1)
                pe.wait_ge(sem("kdt_sb"), n + 1)
                for h in range(GH):
                    ins = pe.matmul(bank[7][:, h * P:(h + 1) * P], KQ[:, h, 1, :], S[:, h, :], start=True, stop=True)
                ins.then_inc(sem("o1_ready"), 1)
                pe.wait_ge(sem("qk_masked"), n + 1)
                turn(NB, 4, "nb_turned")
                turn(KT, 5, "kt_turned")
                pe.wait_ge(sem("vR_in"), n + 1)
                pe.wait_ge(sem("nbt_sb"), n + 1)
                turn(vR, 4, "vr_turned")
                pe.wait_ge(sem("vv_done"), n + 1)
                for g in range(3):
                    if g > 0:
                        pe.wait_ge(sem("sc_sb"), RH * n + RH)
                    for q in range(4):
                        ins = pe.transpose(bank[BANK_A[g]][:, q * P:(q + 1) * P], AT(g, q), ident)
                    ins.then_inc(sem("a_turned"), 1)
                pe.wait_ge(sem("o1_sb"), n + 1)
                for lv in range(1, LEVELS):
                    at = 3 * (lv - 1)
                    for g in range(3):
                        pe.wait_ge(sem("t_sb"), X_PER * n + at + g + 1)
                        for q in range(4):
                            ins = pe.matmul(bank[BANK_A[g]][:, q * P:(q + 1) * P], AT(g, q), Ti[:, g, q, :], start=True, stop=True)
                        ins.then_inc(sem("x_ready"), 1)
                        if lv > 1:
                            if lv > 2:
                                pe.wait_ge(sem("tt_sb"), TT_PER * n + at + g - 5)
                            for q in range(4):
                                ins = pe.transpose(bank[BANK_B[g]][:, q * P:(q + 1) * P], Ti[:, g, q, :], ident)
                            ins.then_inc(sem("a_turned"), 1)
                    for g in range(3):
                        if lv == 1:
                            pe.wait_ge(sem("tt_init"), 3 * n + g + 1)
                        else:
                            pe.wait_ge(sem("tt_sb"), TT_PER * n + at + g - 2)
                        pe.wait_ge(sem("x_sb"), X_PER * n + at + g + 1)
                        for q in range(4):
                            if lv < LEVELS - 1:
                                ins = pe.matmul(bank[BANK_A[g]][:, q * P:(q + 1) * P], TTi[:, g, q, :], Xb[:, g, q, :], start=True, stop=True)
                            else:
                                ins = pe.matmul(bank[BANK_B[g]][:, q * P:(q + 1) * P], Xb[:, g, q, :], TTi[:, g, q, :], start=True, stop=True)
                        ins.then_inc(sem("y_ready"), 1)
                pe.wait_ge(sem("inv_done"), 3 * n + 1)
                pe.wait_ge(sem("vrt_sb"), n + 1)
                for h in range(GH):
                    ins = pe.matmul(bank[4][:, h * P:(h + 1) * P], TTi[:, 0, h, :], VV[:, h, :], start=True, stop=True)
                ins.then_inc(sem("vn_ready"), 1)
                pe.wait_ge(sem("sr_scaled"), n + 1)
                for p in range(RP):
                    pe.matmul(bank[6][:, p * P:(p + 1) * P], RA[:, p, 0, :], Sr[:, p, :], start=True, stop=False)
                    for h in (2 * p, 2 * p + 1):
                        ins = pe.matmul(bank[6][:, 64 * h:64 * h + 64], SC[:, h, 256:384], Vt[:, p, 64 * (h % 2):64 * (h % 2) + 64],
                                        start=False, stop=(h % 2 == 1))
                ins.then_inc(sem("w_ready"), 1)
                pe.wait_ge(sem("inv_done"), 3 * n + 3)
                pe.wait_ge(sem("w_sb"), n + 1)
                for h in range(RH):
                    ins = pe.matmul(bank[7][:, 64 * h:64 * h + 64], TTi[:, 1 + h // 4, h % 4, :], Wb[:, :, :].rearrange("p a c -> p (a c)")[:, 64 * h:64 * h + 64],
                                    start=True, stop=True)
                ins.then_inc(sem("u_ready"), 1)
                pe.wait_ge(sem("vn_sb"), n + 1)
                pe.wait_ge(sem("ktt_sb"), n + 1)
                for h in range(GH):
                    ins = pe.matmul(bank[5][:, h * P:(h + 1) * P], Dn[:, h, :], VN[:, h, :], start=True, stop=True)
                ins.then_inc(sem("o2_ready"), 1)
                for h in range(GH):
                    ins = pe.matmul(bank[4][:, h * P:(h + 1) * P], kdt[:, h, :], VN[:, h, :], start=True, stop=True)
                ins.then_inc(sem("s_ready"), 1)
                pe.wait_ge(sem("u_sb"), n + 1)
                for p in range(RP):
                    pe.matmul(bank[6][:, p * P:(p + 1) * P], RA[:, p, 1, :], Sr[:, p, :], start=True, stop=False)
                    for h in (2 * p, 2 * p + 1):
                        pe.matmul(bank[6][:, 64 * h:64 * h + 64], SC[:, h, 128:256], Ub[:, 64 * h:64 * h + 64], start=False, stop=False)
                        ins = pe.matmul(bank[6][:, 64 * h:64 * h + 64], SC[:, h, 384:512], Vt[:, p, 64 * (h % 2):64 * (h % 2) + 64],
                                        start=False, stop=(h % 2 == 1))
                ins.then_inc(sem("yr_ready"), 1)
                for p in range(RP):
                    pe.matmul(bank[7][:, p * P:(p + 1) * P], NBt[:, p, :], Ub[:, p * P:(p + 1) * P], start=True, stop=False)
                    pe.matmul(bank[7][:, p * P:(p + 1) * P], KTt[:, p, :], Vt[:, p, :], start=False, stop=False)
                    ins = pe.matmul(bank[7][:, p * P:(p + 1) * P], ident, Sr[:, p, :], start=False, stop=True)
                ins.then_inc(sem("p_ready"), 1)
                pe.wait_ge(sem("state_done"), n + 2)

        def chunk_act(a):
            e = a.e
            with e.Fori(0, NT) as n:
                a.enter(n, ACT_LINKS)
                e.wait_ge(sem("state_done"), n + 1)
                for b in range(RP):
                    e.wait_ge(sem("cum_ready"), RP * n + b + 1)
                    a.link(e.activation(exq[:, b, :], bank[b][:, 0:2 * P + 2], ACT.Exp))
                    a.sig(e.activation(exn[:, b, :], bank[b][:, P:2 * P], ACT.Exp, scale=-1.0), sem("cum_read"), RP * n + b + 1)
                e.wait_ge(sem("vg_turned"), n + 1)
                a.sig(e.activation(vGt[:, :, :], b4(7), ACT.Copy), sem("vgt_sb"), n + 1)
                e.wait_ge(sem("d_made"), n + 1)
                a.sig(e.activation(Dn[:, :, :], Dn[:, :, :], ACT.Exp), sem("d_exp"), n + 1)
                e.wait_ge(sem("k_turned"), n + 1)
                for h in range(GH - 1):
                    a.link(e.activation(kdt[:, h, :], b4(7)[:, h, :], ACT.Copy, scale=sm[:, 4, h:h + 1]))
                a.sig(e.activation(kdt[:, GH - 1, :], b4(7)[:, GH - 1, :], ACT.Copy, scale=sm[:, 4, GH - 1:GH]), sem("kdt_sb"), n + 1)
                e.wait_ge(sem("o1_ready"), n + 1)
                for h in range(GH):
                    ins = e.activation(O1[:, h * P:(h + 1) * P], b4(7)[:, h, :], ACT.Copy, scale=sm[:, 2, h:h + 1])
                    a.link(ins) if h < GH - 1 else a.sig(ins, sem("o1_sb"), n + 1)
                for ready, i, dst, done in (("nb_turned", 4, NBt, "nbt_sb"), ("kt_turned", 5, KTt, "ktt_sb"), ("vr_turned", 4, Vt, "vrt_sb")):
                    e.wait_ge(sem(ready), n + 1)
                    a.sig(e.activation(dst[:, :, :], b4(i), ACT.Copy), sem(done), n + 1)
                for lv in range(1, LEVELS - 1):
                    for g in range(3):
                        m = 3 * (lv - 1) + g
                        e.wait_ge(sem("a_turned"), (TT_PER + 3) * n + m + 4)
                        e.activation(cols(TTi[:, g], lv, 1), cols(b4(BANK_B[g]), lv, 1), ACT.Copy).then_inc(sem("tt_sb"), 1)
                e.wait_ge(sem("vn_ready"), n + 1)
                for h in range(GH):
                    ins = e.activation(VN[:, h, :], b4(4)[:, h, :], ACT.Copy, scale=sm[:, 3, h:h + 1])
                    a.link(ins) if h < GH - 1 else a.sig(ins, sem("vn_sb"), n + 1)
                e.wait_ge(sem("w_ready"), n + 1)
                a.sig(e.activation(Wb[:, :, :], b4(6), ACT.Copy), sem("w_sb"), n + 1)
                e.wait_ge(sem("u_ready"), n + 1)
                a.sig(e.activation(Ub[:, :], bank[7][:, :], ACT.Copy), sem("u_sb"), n + 1)
                a.leave(NT)

        def chunk_dve(v):
            e = v.e
            e.wait_ge(sem("state_init"), 1)
            e.sem_inc(sem("state_done"), 1)
            with e.Fori(0, NT) as n:
                v.enter(n, DVE_LINKS)
                e.wait_ge(sem("sm_in"), n + 1)
                e.wait_ge(sem("gbc_ready"), n + 1)
                for h in range(GH):
                    ins = e.tensor_scalar(Dn[:, h, :], b4(6)[:, h, :], sm[:, 1, h:h + 1], 0.0, ALU.subtract, ALU.min)
                    v.link(ins) if h < GH - 1 else v.sig(ins, sem("d_made"), n + 1)
                e.wait_ge(sem("cum_read"), RP * n + RP)
                v.link(e.tensor_tensor(RA[:, :, 0, :], kkT[:, :, bass.ds(n * P, P)], exq[:, :, 0:P], ALU.mult))
                v.link(e.tensor_tensor(RA[:, :, 1, :], fT[:, RB:RB + 4, tcol(n)], exq[:, :, P:2 * P], ALU.mult))
                v.link(e.tensor_tensor(KT[:, :, :], fT[:, KRB:KRB + 4, tcol(n)], exn[:, :, :], ALU.mult))
                v.sig(e.tensor_tensor(NB[:, :, :], aT[:, :, bass.ds(n * P, P)], exn[:, :, :], ALU.mult), sem("rk_ready"), n + 1)
                e.wait_ge(sem("ks_ready"), n + 1)
                e.wait_ge(sem("vgt_sb"), n + 1)
                for h in range(GH):
                    ins = e.scalar_tensor_tensor(VV[:, h, :], b4(6)[:, h, :], sm[:, 2, h:h + 1], vGt[:, h, :], ALU.mult, ALU.add)
                    v.link(ins) if h < GH - 1 else v.sig(ins, sem("vv_done"), n + 1)
                tri = con[:, C_OFF["strict"][0]:C_OFF["incl"][1]].unsqueeze(1).to_broadcast([P, 2, 2 * P])

                def score(h):
                    e.wait_ge(sem("sc_ready"), RH * n + h + 1)
                    v.sig(e.tensor_tensor(SC[:, h, :].rearrange("p (a t) -> p a t", a=2), bank[h % 4][:, :].rearrange("p (a t) -> p a t", a=2), tri, ALU.mult),
                          sem("sc_sb"), RH * n + h + 1)
                for h in range(4):
                    score(h)
                e.wait_ge(sem("kkq_ready"), n + 1)
                e.wait_ge(sem("d_masked"), n + 1)
                for h in range(GH):
                    kq = bank[4 + h // 2][:, :].rearrange("p (h a t) -> p h a t", h=2, a=2)[:, h % 2]
                    v.link(e.scalar_tensor_tensor(Ds[:, h, :], kq[:, 0, :], sm[:, 6, h:h + 1], Ds[:, h, :], ALU.mult, ALU.mult))
                for i in range(2):
                    kq = bank[4 + i][:, :].rearrange("p (h a t) -> p h a t", h=2, a=2)[:, :, 1, :]
                    ins = e.tensor_tensor(Dn[:, 2 * i:2 * i + 2, :], kq, Dn[:, 2 * i:2 * i + 2, :], ALU.mult)
                    v.link(ins) if i == 0 else v.sig(ins, sem("qk_masked"), n + 1)
                for h in range(4, RH):
                    score(h)
                for p in range(RP):
                    ins = e.tensor_scalar(Sr[:, p, :], Sr[:, p, :], exq[:, p, 2 * P:2 * P + 1], None, ALU.mult)
                    v.link(ins) if p < RP - 1 else v.sig(ins, sem("sr_scaled"), n + 1)
                level = C("level").rearrange("p (l c) -> p l c", l=LEVELS)
                for g in range(3):
                    e.wait_ge(sem("a_turned"), (TT_PER + 3) * n + g + 1)
                    v.link(e.tensor_tensor(Ti[:, g], b4(BANK_A[g]), rep4(level[:, 0, :]), ALU.mult))
                    v.sig(e.tensor_tensor(Ti[:, g], Ti[:, g], rep4(ident), ALU.add), sem("t_sb"), X_PER * n + g + 1)
                for lv in range(1, LEVELS):
                    for g in range(3):
                        e.wait_ge(sem("x_ready"), X_PER * n + 3 * (lv - 1) + g + 1)
                        x = cols(Xb[:, g], lv, 0)
                        m = cols(level[:, lv, :].unsqueeze(1), lv, 0).to_broadcast(list(x.shape))
                        e.tensor_tensor(x, cols(b4(BANK_A[g]), lv, 0), m, ALU.mult).then_inc(sem("x_sb"), 1)
                    for g in range(3):
                        e.wait_ge(sem("y_ready"), X_PER * n + 3 * (lv - 1) + g + 1)
                        if lv < LEVELS - 1:
                            t = cols(Ti[:, g], lv, 0)
                            e.tensor_tensor(t, cols(b4(BANK_A[g]), lv, 0), t, ALU.add).then_inc(sem("t_sb"), 1)
                        else:
                            t = cols(TTi[:, g], lv, 1)
                            v.sig(e.scalar_tensor_tensor(t, cols(b4(BANK_B[g]), lv, 1), C("first")[:, 0:1], t, ALU.mult, ALU.add),
                                  sem("inv_done"), 3 * n + g + 1)
                e.wait_ge(sem("o2_ready"), n + 1)
                e.wait_ge(sem("o1_sb"), n + 1)
                v.link(e.tensor_tensor(fT[:, QB:QB + 4, tcol(n)], b4(5), O1[:, :].rearrange("p (h c) -> p h c", h=4), ALU.subtract))
                e.wait_ge(sem("s_ready"), n + 1)
                for h in range(GH):
                    v.link(e.scalar_tensor_tensor(S[:, h, :], S[:, h, :], sm[:, 5, h:h + 1], b4(4)[:, h, :], ALU.mult, ALU.add))
                e.wait_ge(sem("yr_ready"), n + 1)
                v.link(e.tensor_scalar(fT[:, RB:RB + 4, tcol(n)], b4(6), 1.0, None, ALU.mult))
                e.wait_ge(sem("p_ready"), n + 1)
                for p in range(RP):
                    ins = e.scalar_tensor_tensor(Sr[:, p, :], b4(7)[:, p, :], exq[:, p, 2 * P + 1:2 * P + 2], bones, ALU.mult, ALU.mult)
                    v.link(ins) if p < RP - 1 else v.sig(ins, sem("state_done"), n + 2)
                v.leave(NT)

        def tile4(x, i):
            return x[:, i, :].rearrange("p (b c) -> p b c", b=4)

        def o_of(i):
            return fT[:, QB:QB + 4, PAD + i * P:PAD + (i + 1) * P]

        def v_of(i):
            return fT[:, VRB:VRB + 4, PAD + i * P:PAD + (i + 1) * P]

        def out0_pool(g):
            e = g.e
            e.wait_ge(sem("aux_loaded"), 16)
            for i in range(NT):
                vt = v_of(i)
                w = bonus[:, i, :].rearrange("p (b c) -> p b c", c=2).unsqueeze(3).to_broadcast([P, 4, 2, 64])
                vh = vt.rearrange("p b (c d) -> p b c d", c=2)
                g.link(e.tensor_tensor(vh, vh, w, ALU.mult))
                g.sig(e.tensor_tensor(vt, vt, rowbuf[:, 512:1024].rearrange("p (b c) -> p b c", b=4), ALU.add), sem("by_pool"), 1 + i + 1)
            e.wait_ge(sem("inv_norm"), 2)
            e.wait_ge(sem("z_silu"), 1)
            for i in range(NT):
                g.link(e.tensor_tensor(tile4(o_n, i), o_of(i), hst[:, 1, i, 0:GH].unsqueeze(2).to_broadcast([P, GH, P]), ALU.mult))
                g.sig(e.tensor_tensor(o_n[:, i, :], o_n[:, i, :], z[:, i, :], ALU.mult), sem("by_pool"), 5 + i + 1)

        def out0_act(a):
            e = a.e
            e.dma_start(rowbuf[:, :], rows[4:5, :].to_broadcast([P, D])).then_inc(sem("aux_loaded"), 16)
            for i in range(NT):
                e.activation(tile4(t2, i), o_of(i), ACT.Square).then_inc(sem("sq_done"), 1)
            a.link(e.activation(z[:, :, :], z[:, :, :], ACT.Silu))
            e.sem_inc(sem("z_silu"), 1)
            for i in range(NT):
                e.wait_ge(sem("normed"), 12 + i + 1)
                e.activation(t1[:, i, :], y_n[:, i, :], ACT.Square).then_inc(sem("sq_done"), 1)
            e.wait_ge(sem("ss_sb"), 1)
            a.link(e.activation(hst[:, 0, :, 0:GH], hst[:, 0, :, 0:GH], ACT.Sqrt, bias=eps, scale=1.0 / P))
            a.sig(e.activation(hst[:, 3, :, :], hst[:, 3, :, :], ACT.Sqrt, bias=ln_eps, scale=1.0 / 64), sem("root"), 2)
            for i in range(NT):
                e.wait_ge(sem("turned"), 4 + i + 1)
                for h in range(2):
                    hi, _, src = turned(DM, i, h)
                    a.sig(e.activation(hi, src, ACT.Copy, scale=PR("gnorm") if h == 0 else 1.0), sem("high_done"), 8 + 2 * i + h + 1)

        def out0_dve(v):
            e = v.e
            hd = lambda x: x.rearrange("p b (c d) -> p b c d", c=2)
            h8 = lambda k, i: hst[:, k, i, :].rearrange("p (b c) -> p b c", c=2)
            w3 = lambda x: x.unsqueeze(3).to_broadcast([P, 4, 2, 64])
            for i in range(NT):
                y = fT[:, RB:RB + 4, PAD + i * P:PAD + (i + 1) * P]
                v.link(e.tensor_reduce(h8(2, i), hd(y), AX.X, ALU.add))
                v.link(e.tensor_scalar(h8(2, i), h8(2, i), 1.0 / 64, None, ALU.mult))
                v.sig(e.tensor_tensor(hd(tile4(y_n, i)), hd(y), w3(h8(2, i)), ALU.subtract), sem("normed"), 12 + i + 1)
                e.wait_ge(sem("sq_done"), 12 + i + 1)
                v.link(e.tensor_reduce(hst[:, 0, i, 0:GH], tile4(t2, i), AX.X, ALU.add))
            for i in range(NT):
                e.wait_ge(sem("sq_done"), 16 + i + 1)
                ins = e.tensor_reduce(h8(3, i), hd(tile4(t1, i)), AX.X, ALU.add)
                v.link(ins) if i < NT - 1 else v.sig(ins, sem("ss_sb"), 1)
            e.wait_ge(sem("root"), 2)
            v.sig(e.reciprocal(hst[:, 1, :, 0:GH], hst[:, 0, :, 0:GH]), sem("inv_norm"), 2)
            v.link(e.reciprocal(hst[:, 4, :, :], hst[:, 3, :, :]))
            e.wait_ge(sem("aux_loaded"), 16)
            e.wait_ge(sem("g_ready"), 1)
            for i in range(NT):
                yn = tile4(y_n, i)
                v.link(e.tensor_tensor(hd(yn), hd(yn), w3(h8(4, i)), ALU.mult))
                v.link(e.tensor_tensor(y_n[:, i, :], y_n[:, i, :], rowbuf[:, 0:512], ALU.mult))
                e.wait_ge(sem("by_pool"), 1 + i + 1)
                v.link(e.tensor_tensor(yn, yn, v_of(i), ALU.add))
                v.sig(e.tensor_tensor(y_n[:, i, :], bank[4 + i][:, :], y_n[:, i, :], ALU.mult), sem("m_sb"), i + 1)
            for i in range(NT):
                for h in range(2):
                    e.wait_ge(sem("high_done"), 8 + 2 * i + h + 1)
                    hi, lo, src = turned(DM, i, h)
                    v.link(e.scalar_tensor_tensor(lo, src, PR("gnorm") if h == 0 else 1.0, hi.bitcast(F32), ALU.mult, ALU.subtract))

        def out0_pe(pe):
            for i in range(NT):
                ins = pe.matmul(bank[4 + i][:, :], fT[:, GD, PAD + i * P:PAD + (i + 1) * P], PR("g2"), start=True, stop=True)
            ins.then_inc(sem("g_ready"), 1)
            for i in range(NT):
                pe.wait_ge(sem("m_sb"), i + 1)
                pe.wait_ge(sem("by_pool"), 5 + i + 1)
                for q in range(4):
                    pe.transpose(bank[2 * i][:, q * P:(q + 1) * P], o_n[:, i, q * P:(q + 1) * P], ident)
                for q in range(4):
                    ins = pe.transpose(bank[2 * i + 1][:, q * P:(q + 1) * P], y_n[:, i, q * P:(q + 1) * P], ident)
                ins.then_inc(sem("turned"), 1)

        def oproj_pe(pe, first):
            mh, ml_, wh, wl = DM
            for k in range(KD):
                c = first + k
                weights(pe, c)
                for i in range(NT):
                    t = slice(i * P, (i + 1) * P)
                    for h in range(2):
                        w = slice(h * 512, (h + 1) * 512)
                        ins = mm3(pe, bank[2 * i + h][:, :], mh[:, k, t], ml_[:, k, t], wh[:, c % RING, w], wl[:, c % RING, w], k == 0, k == KD - 1)
                ins.then_inc(sem("w_used"), 1)

        def row_in(act, r):
            act.dma_start(rowbuf[:, :], rows[r:r + 1, :].to_broadcast([P, D])).then_inc(sem("row_loaded"), 16)

        def oproj_act(a, c, first):
            if c == 0:
                a.e.dma_start(xres[:, :, :], x_d).then_inc(sem("aux_loaded"), 16)
            row_in(a.e, 2 * c)
            pre_in(a.e, 2 * c + 1, prerow)
            for k in range(KD):
                split_hi(a, DM, first + k)
            used(a.e, first + KD - 1)
            for i in range(NT):
                a.sig(a.e.activation(ffo[:, i, 512:1024], bank[2 * i + 1][:, :], ACT.Copy), sem("ffo_right"), 4 * c + i + 1)
            a.e.wait_ge(sem("ffo_left"), 4 * c + 4)

        def oproj_dve(v, c, first):
            for k in range(KD):
                split_lo(v, DM, first + k)
            used(v.e, first + KD - 1)
            for i in range(NT):
                v.sig(v.e.tensor_copy(ffo[:, i, 0:512], bank[2 * i][:, :]), sem("ffo_left"), 4 * c + i + 1)
            if c == 0:
                v.e.wait_ge(sem("aux_loaded"), 32)

        MB = 2 * HF

        def mlp_pe(pe, first, c):
            uh, ul, wh, wl = DM
            with pe.Fori(0, 2) as it:
                for s in range(HF):
                    ch = first + s
                    weights(pe, ch, it, MB)
                    if s < 4:
                        pe.wait_ge(sem("right_out"), it * 4 + (12 * c + s + 1))
                    else:
                        pe.wait_ge(sem("relu_done"), it * HF + (2 * HF * c + s - 3))
                    for k in range(KD):
                        w = slice(k * P, (k + 1) * P)
                        ins = mm3(pe, bank[s % 4][:, :], wh[:, ch % RING, w], wl[:, ch % RING, w], uh[:, k, :], ul[:, k, :], k == 0, k == KD - 1)
                    ins.then_inc(sem("w_used"), 1)
                for half in range(2):
                    b0 = 4 * (1 - half)
                    if half == 0:
                        pe.wait_ge(sem("left_out"), it * 4 + (12 * c + 4))
                    for j in range(HF // 2):
                        ch = first + HF + half * HF // 2 + j
                        weights(pe, ch, it, MB)
                        pe.wait_ge(sem("h_lo"), it * HF + (2 * HF * c + (2 * j + 2 if half == 0 else HF)))
                        for f in (2 * j, 2 * j + 1):
                            w = slice((f % 2) * 512, (f % 2 + 1) * 512)
                            for i in range(NT):
                                t = slice(i * P, (i + 1) * P)
                                ins = mm3(pe, bank[b0 + i][:, :], hh[:, f, t], hl[:, f, t], wh[:, ch % RING, w], wl[:, ch % RING, w], f == 0, f == HF - 1)
                        ins.then_inc(sem("w_used"), 1)

        def mlp_act(a, first, c):
            e, hb = a.e, 2 * HF * c
            with e.Fori(0, 2) as it:
                for s in range(2):
                    split_hi(a, DM, first + s, it, MB)
                for s in range(MB):
                    if s + 2 < MB:
                        split_hi(a, DM, first + s + 2, it, MB)
                    if s < HF:
                        used(e, first + s, it, MB)
                        e.wait_ge(sem("hraw_free"), it * HF + ((2 * HF + 2) * c + s + 1))
                        a.sig(e.activation(hraw[:, s % 2, :], bank[s % 4][:, :], ACT.Relu), sem("relu_done"), it * HF + (hb + s + 1))
                    if 1 <= s <= HF:
                        e.wait_ge(sem("h_sq"), it * HF + (hb + s))
                        a.sig(e.activation(hh[:, s - 1, :], hraw[:, (s - 1) % 2, :], ACT.Copy), sem("h_hi"), it * HF + (hb + s))

        def mlp_dve(v, first, c):
            e, hb = v.e, 2 * HF * c
            for nm in ("right_out", "left_out"):
                e.sem_inc(sem(nm), 4)
            e.sem_inc(sem("hraw_free"), 2)
            e.wait_ge(sem("ffo_zero"), c + 1)
            with e.Fori(0, 2) as it:
                for s in range(2):
                    split_lo(v, DM, first + s, it, MB)
                for s in range(MB):
                    if s + 2 < MB:
                        split_lo(v, DM, first + s + 2, it, MB)
                    if s < HF:
                        h = hraw[:, s % 2, :]
                        e.wait_ge(sem("relu_done"), it * HF + (hb + s + 1))
                        v.sig(e.tensor_tensor(h, h, h, ALU.mult), sem("h_sq"), it * HF + (hb + s + 1))
                    if 1 <= s <= HF:
                        e.wait_ge(sem("h_hi"), it * HF + (hb + s))
                        v.sig(e.tensor_tensor(hl[:, s - 1, :], hraw[:, (s - 1) % 2, :], hh[:, s - 1, :].bitcast(F32), ALU.subtract), sem("h_lo"), it * HF + (hb + s))
                        e.sem_inc(sem("hraw_free"), 1)
                    for half, end in ((0, HF + HF // 2 - 1), (1, MB - 1)):
                        if s == end:
                            used(e, first + s, it, MB)
                            for i in range(NT):
                                o = ffo[:, i, 512 * half:512 * half + 512]
                                nm = "right_out" if half else "left_out"
                                v.sig(e.tensor_tensor(o, bank[4 * (1 - half) + i][:, :], o, ALU.add), sem(nm), it * 4 + (12 * c + 4 + i + 1))

        l1 = ExitStack()
        KVW = 2 * HD
        QW = QH * HD
        f1 = sb("f1", [P, NT, QW + 6 * KVW + 3 * QH], c=l1)
        posi = sb("posi", [P, NT + 1], I32, c=l1)
        posf = sb("posf", [P, NT + 1], c=l1)
        ang = sb("ang", [P, NT + 1, 2, HALF], c=l1)
        rnd = sb("rnd", [P, NT + 1, 2, HALF], c=l1)
        l1p = ExitStack()
        D1 = dense(l1p, "1")
        l1p.close()
        qT = sb("qT", [P, QH, T], F32R, c=l1)
        kH = sb("kH", [P, 2, KG, T], F32R, c=l1)
        kL = sb("kL", [P, 2, KG, T], F32R, c=l1)
        msk = sb("msk", [P, 2, P], F32R, c=l1)
        l1y = ExitStack()
        dupq = sb("dupq", [P, 2, QH, 2, HD], c=l1y)
        l1y.close()
        yat = sb("yat", [P, NT, QW], c=l1)
        kcT = sb("kcT", [P, 2 * NCMP], c=l1)
        vcb = sb("vcb", [P, KG, 4, HD], c=l1)
        gat = sb("gat", [P, QH, 2, NT], c=l1)
        csn = sb("csn", [P, NT + 1, 2, HALF], c=l1)
        l1a = ExitStack()
        rot = sb("rot", [P, 4, NT, QH * HALF], c=l1a)
        dup = sb("dup", [P, 2, KG, NT, 2, HD], c=l1a)
        X2 = sb("X2", [P, 2, KG, T + 32], c=l1a)
        XP = sb("XP", [P, 2, 16, KG, NCMP], c=l1a)
        hc = sb("hc", [2 * NCMP, 2, 256], c=l1a)
        hcT = sb("hcT", [P, 4, 2 * NCMP], c=l1a)
        hrep = sb("hrep", [P, 2, KG, 4, NCMP], c=l1a)
        kcs = sb("kcs", [2 * NCMP, HD], c=l1a)
        kcp = sb("kcp", [2 * NCMP, 2, HD], c=l1a)
        vcr = sb("vcr", [P, KG, HD], c=l1a)
        l1a.close()
        l1b = ExitStack()
        sc_c = sb("sc_c", [P, NT, QH, NCMP], c=l1b)
        pc = sb("pc", [P, NT, KG, HPG, NCMP], c=l1b)
        pcT = sb("pcT", [P, NT, 4, P], c=l1b)
        cst = sb("cst", [P, 4, NT, QH], c=l1b)
        l1b.close()
        l1c = ExitStack()
        qb = sb("qb", [P, 2, T], F32R, c=l1c)
        pb = sb("pb", [P, 4, T], c=l1c)
        pT = sb("pT", [P, 4, T], c=l1c)
        nmax = sb("nmax", [P, 16], c=l1c)
        rsum = sb("rsum", [P, 16], c=l1c)
        rsc = sb("rsc", [P, 8], c=l1c)
        om = sb("om", [P, 2, NT, HD], c=l1c)
        l1c.close()
        l1.close()
        KC, VC, KS, VS, KW, VW = (QW + i * KVW for i in range(6))
        GT = QW + 6 * KVW
        GROUP_W = [512, 512, 512, GT + 3 * QH - 1536]

        def proj1_pe(pe):
            uh, ul, wh, wl = D1
            for gr in range(4):
                if gr >= 2:
                    pe.wait_ge(sem("f1_even"), 2 * (gr - 1))
                    pe.wait_ge(sem("f1_odd"), 2 * (gr - 1))
                for c in range(4):
                    ch = C_IN1 + 4 * gr + c
                    weights(pe, ch)
                    for kk in range(2):
                        k, w = 2 * c + kk, GROUP_W[gr]
                        ws = slice(kk * 512, kk * 512 + w)
                        for i in range(NT):
                            t = slice(i * P, (i + 1) * P)
                            ins = mm3(pe, bank[(gr % 2) * 4 + i][:, 0:w], uh[:, k, t], ul[:, k, t], wh[:, ch % RING, ws], wl[:, ch % RING, ws], k == 0, k == KD - 1)
                    ins.then_inc(sem("w_used"), 1)

        def proj1_out(ch, odd):
            split = split_hi if odd else split_lo
            for c in range(2):
                split(ch, D1, C_IN1 + c)
            for gr in range(4):
                for c in range(4 * gr, 4 * gr + 4):
                    if c + 2 < 16:
                        split(ch, D1, C_IN1 + c + 2)
                used(ch.e, C_IN1 + 4 * gr + 3)
                for m, i in enumerate((1, 3) if odd else (0, 2)):
                    w = GROUP_W[gr]
                    dst, src = f1[:, i, gr * 512:gr * 512 + w], bank[(gr % 2) * 4 + i][:, 0:w]
                    ins = ch.e.activation(dst, src, ACT.Copy) if odd else ch.e.tensor_copy(dst, src)
                    ch.sig(ins, sem("f1_odd" if odd else "f1_even"), 2 * gr + m + 1)

        def proj1_act(a):
            a.e.dma_start(posi[:, :], pos).then_inc(sem("aux_loaded"), 16)
            proj1_out(a, True)

        TWO_PI = (6.28125, 0.0019350051879882812, 3.019916050561733e-07)
        ROUND = 12582912.0

        def proj1_dve(v):
            proj1_out(v, False)
            e = v.e
            e.wait_ge(sem("aux_loaded"), 48)
            v.link(e.tensor_copy(posf[:, :], posi[:, :]))
            for m in range(2):
                v.link(e.tensor_tensor(ang[:, :, m, :], posf[:, :].unsqueeze(2).to_broadcast([P, NT + 1, HALF]),
                                       C("ifreq").unsqueeze(1).to_broadcast([P, NT + 1, HALF]), ALU.mult))
                v.link(e.tensor_scalar(rnd[:, :, m, :], ang[:, :, m, :], float(1 / (2 * np.pi)), 0.25 * m, ALU.mult, ALU.add))
            v.link(e.tensor_scalar(rnd[:, :, :, :], rnd[:, :, :, :], ROUND, None, ALU.add))
            v.link(e.tensor_scalar(rnd[:, :, :, :], rnd[:, :, :, :], ROUND, None, ALU.subtract))
            for part in TWO_PI:
                v.link(e.scalar_tensor_tensor(ang[:, :, :, :], rnd[:, :, :, :], -part, ang[:, :, :, :], ALU.mult, ALU.add))
            v.link(e.tensor_scalar(ang[:, :, 1, :], ang[:, :, 1, :], float(np.pi / 2), None, ALU.add))
            v.sig(e.tensor_scalar(ang[:, :, :, :], ang[:, :, :, :], 3.1415925, -3.1415925, ALU.min, ALU.max), sem("angles"), 1)

        def rotary(v, x1, x2, sn, cs, t):
            e = v.e
            v.link(e.tensor_tensor(t[0], x1, cs, ALU.mult))
            v.link(e.tensor_tensor(t[1], x2, sn, ALU.mult))
            v.link(e.tensor_tensor(t[2], x2, cs, ALU.mult))
            v.link(e.tensor_tensor(t[3], x1, sn, ALU.mult))
            v.link(e.tensor_tensor(x1, t[0], t[1], ALU.subtract))
            v.link(e.tensor_tensor(x2, t[2], t[3], ALU.add))

        def prep_pool(g):
            for kv in range(2):
                for gr in range(KG):
                    src = f1[:, :, KC + kv * KVW + gr * HD:KC + kv * KVW + (gr + 1) * HD].unsqueeze(2).to_broadcast([P, NT, 2, HD])
                    g.sig(g.e.tensor_copy(dup[:, kv, gr], src), sem("dup_done"), 2 * kv + gr + 1)
            g.sig(g.e.memset(X2[:, :, :, T - 1:], 0.0), sem("zeroed"), 1)
            g.e.wait_ge(sem("rotated"), 1)
            for i in range(NT):
                if i >= 2:
                    g.e.wait_ge(sem("q_turned"), 4 + 4 * (i - 1))
                src = f1[:, i, 0:QW].rearrange("p (h d) -> p h d", d=HD).unsqueeze(2).to_broadcast([P, QH, 2, HD])
                g.sig(g.e.tensor_copy(dupq[:, i % 2], src), sem("dupq_done"), i + 1)

        def prep_act(a):
            e = a.e
            a.sig(e.activation(csn[:, :, :, :], ang[:, :, :, :], ACT.Sin), sem("angles"), 2)
            e.wait_ge(sem("zeroed"), 1)
            for m in range(4):
                e.wait_ge(sem("c_turned"), m + 1)
                kv, gr = m // 2, m % 2
                a.link(e.activation(X2[0:64, kv, gr, 0:T], bank[m][0:64, :], ACT.Copy))
                a.sig(e.activation(X2[64:128, kv, gr, 0:T - 1], bank[m][64:128, 1:T], ACT.Copy), sem("x2_done"), m + 1)
            for n in range(20):
                e.wait_ge(sem("q_turned"), n + 1)
                hi, _, src, scale = split_task(n)
                a.sig(e.activation(hi, src, ACT.Copy, scale=scale), sem("q_hi"), n + 1)
                if n == 7:
                    for kv in range(2):
                        used(e, C_CMP + 4 * kv + 3)
                        a.sig(e.activation(hc[:, kv, :], bank[kv][0:64, 0:256], ACT.Silu), sem("hc_done"), kv + 1)

        def split_task(n):
            if n < 4:
                return kH[:, n // 2, n % 2, :], kL[:, n // 2, n % 2, :], bank[4 + n][:, :], 1.0
            i, h = (n - 4) // 4, (n - 4) % 4
            q = qT[:, 4 * h:4 * h + 4, i * P:(i + 1) * P]
            return q, q[64:128], b4(4 + n % 4), HD ** -0.5

        def prep_dve(v):
            e = v.e
            e.wait_ge(sem("angles"), 2)
            for off, nh in ((0, QH), (KS, 2), (KW, 2)):
                x = f1[:, :, off:off + nh * HD].rearrange("p i (h d) -> p i h d", d=HD)
                sn, cs = (csn[:, 0:NT, m, :].unsqueeze(2).to_broadcast([P, NT, nh, HALF]) for m in range(2))
                t = [rot[:, m, :, 0:nh * HALF].rearrange("p i (h d) -> p i h d", d=HALF) for m in range(4)]
                rotary(v, x[:, :, :, 0:HALF], x[:, :, :, HALF:2 * HALF], sn, cs, t)
                e.sem_inc(sem("rotated"), 1)
            e.wait_ge(sem("c_turned"), 4)
            for b, off in enumerate((KS, KW)):
                for gr in range(KG):
                    src = f1[:, :, off + gr * HD:off + (gr + 1) * HD].unsqueeze(2).to_broadcast([P, NT, 2, HD])
                    v.sig(e.tensor_copy(dup[:, b, gr], src), sem("dup_done"), 5 + 2 * b + gr)
            for kv in range(2):
                pe_c = PR("pe_k" if kv == 0 else "pe_v")
                for gr in range(KG):
                    e.wait_ge(sem("x2_done"), 2 * kv + gr + 1)
                    for half in range(2):
                        src = X2[:, kv, gr, 16 * half:16 * half + 512].rearrange("p (n b two) -> p b n two", b=8, two=2)[:, :, :, 0]
                        pw = pe_c[:, 8 * half:8 * half + 8].unsqueeze(2).to_broadcast([P, 8, NCMP])
                        v.link(e.tensor_tensor(XP[:, kv, 8 * half:8 * half + 8, gr, :], src, pw, ALU.add))
                e.sem_inc(sem("xp_done"), 1)
            for n in range(20):
                hi, lo, src, scale = split_task(n)
                e.wait_ge(sem("q_hi"), n + 1)
                if n < 4:
                    ins = e.tensor_tensor(lo, src, hi.bitcast(F32), ALU.subtract)
                else:
                    ins = e.scalar_tensor_tensor(lo, src[64:128], scale, lo.bitcast(F32), ALU.mult, ALU.subtract)
                v.sig(ins, sem("q_lo"), n + 1)
            e.wait_ge(sem("hc_turned"), 1)
            v.sig(e.tensor_copy(hcT[:, :, :], bank[2][:, 0:256].rearrange("p (a c) -> p a c", a=4)), sem("hcT_done"), 1)
            for m in range(2):
                for gr in range(KG):
                    src = hcT[:, 2 + m, gr * NCMP:(gr + 1) * NCMP].unsqueeze(1).to_broadcast([P, 4, NCMP])
                    v.link(e.tensor_copy(hrep[:, m, gr], src))
            e.sem_inc(sem("hrep_done"), 1)
            e.wait_ge(sem("kc_ready"), 1)
            v.link(e.tensor_copy(kcs[:, :], bank[3][0:64, 0:64]))
            t = [rot[0:64, m, 0, 0:HALF] for m in range(4)]
            rotary(v, kcs[:, 0:HALF], kcs[:, HALF:2 * HALF], csn[0:64, NT, 0, :], csn[0:64, NT, 1, :], t)
            v.sig(e.tensor_copy(kcp[:, :, :], kcs[:, :].unsqueeze(1).to_broadcast([2 * NCMP, 2, HD])), sem("kcp_done"), 1)
            e.wait_ge(sem("vc_ready"), 1)
            v.link(e.tensor_copy(vcr[:, :, :], bank[0][:, 0:128].rearrange("p (g d) -> p g d", g=2)))
            for j in range(4):
                v.link(e.tensor_scalar(vcb[:, :, j, :], vcr[:, :, :], C("hsel")[:, j:j + 1], None, ALU.mult))
            e.wait_ge(sem("kcT_ready"), 1)
            v.link(e.tensor_copy(kcT[:, :], bank[1][:, 0:64]))

        def prep_pe(pe):
            for m in range(4):
                pe.wait_ge(sem("dup_done"), m + 1)
                for i in range(NT):
                    ins = pe.transpose(bank[m][:, i * P:(i + 1) * P], dup[:, m // 2, m % 2, i].rearrange("p a d -> p (a d)"), ident)
                ins.then_inc(sem("c_turned"), 1)
            for m in range(4):
                pe.wait_ge(sem("dup_done"), 5 + m)
                for i in range(NT):
                    ins = pe.transpose(bank[4 + m][:, i * P:(i + 1) * P], dup[:, m // 2, m % 2, i].rearrange("p a d -> p (a d)"), ident)
                ins.then_inc(sem("q_turned"), 1)
            pe.wait_ge(sem("x2_done"), 4)
            for kv in range(2):
                pe.wait_ge(sem("xp_done"), kv + 1)
                for c in range(4):
                    ch = C_CMP + 4 * kv + c
                    pe.wait_ge(slot_sems[ch % RING], 16 * (ch // RING + 1))
                    for q in range(4):
                        lp = 4 * c + q
                        ins = pe.matmul(bank[kv][0:64, 0:256], XP[:, kv, lp].rearrange("p g n -> p (g n)"), ring[:, ch % RING, q * 256:(q + 1) * 256],
                                        start=(lp == 0), stop=(lp == 15))
                    ins.then_inc(sem("w_used"), 1)
                    used(pe, ch)
                    pass_over(pe, ch)
            for n in range(4, 20):
                i, h = (n - 4) // 4, (n - 4) % 4
                pe.wait_ge(sem("dupq_done"), i + 1)
                pe.wait_ge(sem("q_lo"), n - 3)
                for j in range(4):
                    ins = pe.transpose(bank[4 + n % 4][:, j * P:(j + 1) * P], dupq[:, i % 2, 4 * h + j].rearrange("p a d -> p (a d)"), ident)
                ins.then_inc(sem("q_turned"), 1)
            pe.wait_ge(sem("hc_done"), 2)
            for m in range(4):
                ins = pe.transpose(bank[2][:, m * 64:(m + 1) * 64], hc[:, m // 2, (m % 2) * P:(m % 2 + 1) * P], ident[0:64, 0:64])
            ins.then_inc(sem("hc_turned"), 1)
            pe.wait_ge(sem("hcT_done"), 1)
            for m in range(2):
                ins = pe.matmul(bank[3][0:64, 0:64], hcT[:, m, :], PR("w2k")[:, m * 64:(m + 1) * 64], start=(m == 0), stop=(m == 1))
            ins.then_inc(sem("kc_ready"), 1)
            pe.wait_ge(sem("hrep_done"), 1)
            for gr in range(KG):
                for m in range(2):
                    ins = pe.matmul(bank[0][:, gr * 64:(gr + 1) * 64], hrep[:, m, gr].rearrange("p j n -> p (j n)"), PR("w2v")[:, m * 64:(m + 1) * 64],
                                    start=(m == 0), stop=(m == 1))
            ins.then_inc(sem("vc_ready"), 1)
            pe.wait_ge(sem("kcp_done"), 1)
            pe.transpose(bank[1][:, 0:64], kcp[:, :, :].rearrange("p a d -> p (a d)"), ident[0:64, 0:64]).then_inc(sem("kcT_ready"), 1)

        def cmp_pe(pe):
            for i in range(NT):
                for h in range(QH):
                    ins = pe.matmul(bank[i][:, h * NCMP:(h + 1) * NCMP], qT[:, h, i * P:(i + 1) * P].bitcast(F32),
                                    kcT[:, (h % KG) * NCMP:(h % KG + 1) * NCMP], start=True, stop=True)
                ins.then_inc(sem("cs_ready"), 1)
            for i in range(NT):
                pe.wait_ge(sem("pc_done"), i // 2 + 1)
                if i >= 2:
                    pe.wait_ge(sem("pcT_done"), i - 1)
                for q in range(4):
                    ins = pe.transpose(bank[4 + i % 2][:, q * P:(q + 1) * P], pc[:, i, q // 2, 4 * (q % 2):4 * (q % 2) + 4, :].rearrange("p j n -> p (j n)"), ident)
                ins.then_inc(sem("pc_turned"), 1)
            for i in range(NT):
                pe.wait_ge(sem("pcT_done"), i + 1)
                if i >= 2:
                    pe.wait_ge(sem("oc_done"), i - 1)
                for q in range(4):
                    ins = pe.matmul(bank[OC[i % 2][q // 2]][:, (q % 2) * 256:(q % 2 + 1) * 256], pcT[:, i, q, :], vcb[:, q // 2].rearrange("p j d -> p (j d)"),
                                    start=True, stop=True)
                ins.then_inc(sem("oc_ready"), 1)

        OC = ((6, 7), (0, 1))

        def cmp_act(a):
            e = a.e
            a.sig(e.activation(f1[:, :, GT:GT + 3 * QH], f1[:, :, GT:GT + 3 * QH], ACT.Sigmoid), sem("gates"), 1)
            e.activation(msk[:, 0, :], ident, ACT.Copy)
            e.activation(msk[:, 1, :], C("neg"), ACT.Copy)
            for k in range(2):
                e.wait_ge(sem("cs_sub"), k + 1)
                a.sig(e.activation(sc_c[:, 2 * k:2 * k + 2], sc_c[:, 2 * k:2 * k + 2], ACT.Exp), sem("cs_exp"), k + 1)
            for i in range(NT):
                e.wait_ge(sem("pc_turned"), i + 1)
                e.activation(pcT[:, i, :, :], b4(4 + i % 2), ACT.Copy).then_inc(sem("pcT_done"), 1)

        def cmp_dve(v):
            e = v.e
            cm = C("cmask").rearrange("p (i n) -> p i n", i=NT)
            cn = C("cneg").rearrange("p (i n) -> p i n", i=NT)
            two = lambda k: slice(2 * k, 2 * k + 2)
            w = lambda j, k: cst[:, j, two(k), :].unsqueeze(3).to_broadcast([P, 2, QH, NCMP])
            for k in range(2):
                s2 = sc_c[:, two(k)]
                for i in (2 * k, 2 * k + 1):
                    e.wait_ge(sem("cs_ready"), i + 1)
                    m = cn[:, i, :].unsqueeze(1).to_broadcast([P, QH, NCMP])
                    v.link(e.tensor_tensor(sc_c[:, i], bank[i][:, :].rearrange("p (h n) -> p h n", n=NCMP), m, ALU.add))
                v.link(e.tensor_reduce(cst[:, 0, two(k), :], s2, AX.X, ALU.max))
                v.sig(e.tensor_tensor(s2, s2, w(0, k), ALU.subtract), sem("cs_sub"), k + 1)
            e.wait_ge(sem("gates"), 1)
            for b in range(2):
                src = f1[:, :, GT + QH * (1 + b):GT + QH * (2 + b)].rearrange("p i h -> p h i")
                v.link(e.tensor_copy(gat[:, :, b, :], src))
            for k in range(2):
                s2 = sc_c[:, two(k)]
                e.wait_ge(sem("cs_exp"), k + 1)
                v.link(e.tensor_tensor(s2, s2, cm[:, two(k), :].unsqueeze(2).to_broadcast([P, 2, QH, NCMP]), ALU.mult))
                v.link(e.tensor_reduce(cst[:, 1, two(k), :], s2, AX.X, ALU.add))
                v.link(e.tensor_scalar(cst[:, 1, two(k), :], cst[:, 1, two(k), :], 1e-30, None, ALU.max))
                v.link(e.reciprocal(cst[:, 2, two(k), :], cst[:, 1, two(k), :]))
                v.link(e.tensor_tensor(cst[:, 3, two(k), :], cst[:, 2, two(k), :], f1[:, two(k), GT:GT + QH], ALU.mult))
                for i in (2 * k, 2 * k + 1):
                    src = sc_c[:, i].rearrange("p (j g) n -> p g j n", g=2)
                    wg = cst[:, 3, i, :].rearrange("p (j g) -> p g j", g=2).unsqueeze(3).to_broadcast([P, KG, HPG, NCMP])
                    ins = e.tensor_tensor(pc[:, i], src, wg, ALU.mult)
                    v.link(ins) if i % 2 == 0 else v.sig(ins, sem("pc_done"), k + 1)
            for i in range(NT):
                e.wait_ge(sem("oc_ready"), i + 1)
                for gr in range(KG):
                    dst = yat[:, i, :].rearrange("p (j g d) -> p g j d", g=2, d=HD)[:, gr]
                    ins = e.tensor_copy(dst, bank[OC[i % 2][gr]][:, :].rearrange("p (j d) -> p j d", d=HD))
                    v.link(ins) if gr == 0 else v.sig(ins, sem("oc_done"), i + 1)

        UNITS = [(hb, b, i) for hb in range(2) for b in range(2) for i in range(NT)]
        NU, NBLK, LEAD = len(UNITS), QH // 2, 3
        SC_FREE, PB_FREE, PT_FREE, O_FREE = 4, 4, 4, 2

        def over_blocks(eng, block, chain=None, links=0):
            block(0, 0, True, False)
            with eng.Fori(0, NBLK - 2) as it:
                if chain:
                    chain.enter(it, links)
                block(it, 1, False, False)
                if chain:
                    chain.leave(NBLK - 2)
            block(0, NBLK - 1, False, True)

        def att_pool(g):
            for h in range(2):
                g.e.tensor_copy(qb[:, h, :], qT[:, h, :]).then_inc(sem("qb_in"), 1)
            with g.e.Fori(0, NBLK - 1) as it:
                for h in range(2):
                    g.e.wait_ge(sem("q_free"), it * 2 + h + 1)
                    g.e.wait_ge(sem("qb_in"), it * 2 + h + 2)
                    g.hold(spare[:, :])
                    g.e.tensor_copy(qb[:, h, :], qT[:, bass.ds(it * 2 + 2 + h, 1), :].rearrange("p a t -> p (a t)")).then_inc(sem("qb_in"), 1)

        def att_pe(pe):
            pe.sem_inc(sem("p_turned"), PB_FREE)
            pe.sem_inc(sem("pv_done"), PT_FREE)

            def scores(it, n0, u):
                hb, b, i = UNITS[u % NU]
                w = (i + 1) * P
                g, s = hb % KG, bank[u % 4]
                if u % 8 == 0:
                    pe.wait_ge(sem("qb_in"), it * 2 + ((n0 + u) // 8 + 1))
                pe.wait_ge(sem("p_sb"), it * NU + (n0 + u + 1))
                q = qb[:, hb, i * P:(i + 1) * P]
                pe.matmul(s[:, 0:w], q, kH[:, b, g, 0:w], start=True, stop=False)
                pe.matmul(s[:, 0:w], q, kL[:, b, g, 0:w], start=False, stop=False)
                pe.matmul(s[:, i * P:w], msk[:, 0, :], msk[:, 1, :], start=False, stop=True).then_inc(sem("s_psum"), 1)
                if u % 8 == 7:
                    pe.wait_ge(sem("s_psum"), it * NU + (n0 + u + 1))
                    pe.sem_inc(sem("q_free"), 1)

            def turn(it, n0, u):
                hb, b, i = UNITS[u]
                pe.wait_ge(sem("p_sb"), it * NU + (n0 + u + 1 + SC_FREE))
                pe.wait_ge(sem("pT_even" if u % 2 == 0 else "pT_odd"), it * (NU // 2) + ((n0 + u) // 2 + 1))
                for k in range(i + 1):
                    ins = pe.transpose(bank[4 + u % 2][:, k * P:(k + 1) * P], pb[:, u % 4, k * P:(k + 1) * P], ident)
                ins.then_inc(sem("p_turned"), 1)

            def values(it, n0, u):
                hb, b, i = UNITS[u % NU]
                pe.wait_ge(sem("pT_even" if u % 2 == 0 else "pT_odd"), it * (NU // 2) + ((n0 + u) // 2 + 2))
                if u % 8 == 0:
                    pe.wait_ge(sem("combined"), it * 2 + ((n0 + u) // 8 + 1))
                v0 = (VS if b == 0 else VW) + (hb % KG) * HD
                c = (b * NT + i) * HD
                for k in range(i + 1):
                    ins = pe.matmul(bank[6 + hb][:, c:c + HD], pT[:, u % 4, k * P:(k + 1) * P], f1[:, k, v0:v0 + HD],
                                    start=(k == 0), stop=(k == i))
                ins.then_inc(sem("pv_done"), 1)

            def block(it, blk, first, last):
                n0 = blk * NU
                for u in range(NU):
                    if not last or u + LEAD < NU:
                        scores(it, n0, u + LEAD)
                    turn(it, n0, u)
                    if not first or u >= 2:
                        values(it, n0, u - 2)
                if last:
                    values(it, n0, NU - 2)
                    values(it, n0, NU - 1)

            for u in range(LEAD):
                scores(0, 0, u)
            over_blocks(pe, block)

        def turned_out(eng, it, n0, u):
            hb, b, i = UNITS[u % NU]
            w, odd = (i + 1) * P, u % 2
            eng.wait_ge(sem("p_turned"), it * NU + (n0 + u + 1 + PB_FREE))
            eng.wait_ge(sem("pv_done"), it * NU + (n0 + u + 1))
            dst, src = pT[:, u % 4, 0:w], bank[4 + odd][:, 0:w]
            ins = eng.activation(dst, src, ACT.Copy) if odd else eng.tensor_scalar(dst, src, 1.0, None, ALU.mult)
            ins.then_inc(sem("pT_odd" if odd else "pT_even"), 1)

        def att_act(a):
            e = a.e
            e.sem_inc(sem("p_sb"), SC_FREE)
            e.sem_inc(sem("pT_odd"), 1)

            def block(it, blk, first, last):
                n0 = blk * NU
                for u, (hb, b, i) in enumerate(UNITS):
                    w = (i + 1) * P
                    if (u - LEAD) % 2 == 1 and (not first or u >= LEAD):
                        turned_out(e, it, n0, u - LEAD)
                    e.wait_ge(sem("s_max"), it * NU + (n0 + u + 1))
                    e.wait_ge(sem("p_turned"), it * NU + (n0 + u + 1))
                    e.activation(pb[:, u % 4, 0:w], bank[u % 4][:, 0:w], ACT.Exp, bias=nmax[:, u:u + 1],
                                 accum_out=rsum[:, u:u + 1]).then_inc(sem("p_sb"), 1)
                if last:
                    turned_out(e, it, n0, NU - 3)
                    turned_out(e, it, n0, NU - 1)
            over_blocks(e, block)

        def att_dve(v):
            e = v.e
            e.sem_inc(sem("pT_even"), 1)
            e.sem_inc(sem("combined"), O_FREE)

            def combine(it, n0, hb):
                h = n0 // 8 + hb
                hb = hb % 2
                e.wait_ge(sem("pv_done"), it * NU + (8 * h + 8 + PT_FREE))
                v.link(e.reciprocal(rsc[:, :], rsum[:, 8 * hb:8 * hb + 8]))
                v.link(e.tensor_tensor(rsc[:, :], rsc[:, :], gat[:, bass.ds(it * 2 + h, 1), :, :].rearrange("p a b i -> p (a b i)"), ALU.mult))
                v.sig(e.tensor_tensor(om[:, :, :, :].rearrange("p b i d -> p (b i) d"), bank[6 + hb][:, :].rearrange("p (u d) -> p u d", d=HD),
                                      rsc[:, :].unsqueeze(2).to_broadcast([P, 8, HD]), ALU.mult), sem("combined"), it * 2 + (h + 1 + O_FREE))
                v.link(e.tensor_tensor(om[:, 0], om[:, 0], om[:, 1], ALU.add))
                y = yat[:, :, bass.ds((it * 2 + h) * HD, HD)]
                v.link(e.tensor_tensor(y, y, om[:, 0], ALU.add))

            def block(it, blk, first, last):
                n0 = blk * NU
                for u, (hb, b, i) in enumerate(UNITS):
                    w = (i + 1) * P
                    e.wait_ge(sem("s_psum"), it * NU + (n0 + u + 1))
                    e.tensor_reduce(nmax[:, u:u + 1], bank[u % 4][:, 0:w], AX.X, ALU.max, negate=True).then_inc(sem("s_max"), 1)
                    if (u - LEAD) % 2 == 0 and (not first or u >= LEAD):
                        turned_out(e, it, n0, u - LEAD)
                    if u == 13:
                        combine(it, n0, 0)
                    if u == 5 and not first:
                        combine(it, n0, -1)
                if last:
                    turned_out(e, it, n0, NU - 2)
                    combine(it, n0, 1)
            over_blocks(e, block, v, 2 * 4)

        def yturn_pe(pe):
            for i in range(NT):
                for k in range(KD):
                    ins = pe.transpose(bank[2 * i + k // 4][:, (k % 4) * P:(k % 4 + 1) * P], yat[:, i, k * P:(k + 1) * P], ident)
                ins.then_inc(sem("turned"), 1)

        def yturn_act(a):
            for i in range(NT):
                a.e.wait_ge(sem("turned"), 16 + i + 1)
                for h in range(2):
                    hi, _, src = turned(DM, i, h)
                    a.sig(a.e.activation(hi, src, ACT.Copy), sem("high_done"), 32 + 2 * i + h + 1)

        def yturn_dve(v):
            for i in range(NT):
                for h in range(2):
                    v.e.wait_ge(sem("high_done"), 32 + 2 * i + h + 1)
                    hi, lo, src = turned(DM, i, h)
                    v.link(v.e.tensor_tensor(lo, src, hi.bitcast(F32), ALU.subtract))

        block = ctx.enter_context(nc.Block())

        @block.sync
        def _(sp):
            sp.dma_start(xres[:, :, :], x_d).then_inc(sem("loaded"), 16)
            sp.dma_start(con[:, :], consts).then_inc(sem("loaded"), 16)
            sp.dma_start(par[:, :], params).then_inc(sem("loaded"), 16)
            stream(sp)

        @block.gpsimd
        def _(pool):
            g = Chain(pool, sem("pool_chain"))
            pool.wait_ge(sem("loaded"), 48)
            g.link(pool.memset(spare[:, :], 0.0))
            g.link(pool.memset(fT[:, :, 0:PAD], 0.0))
            meet(pool, 1)
            proj0_pool(g)
            meet(pool, 2)
            elem0_pool(g)
            meet(pool, 3)
            chunk_pool(g)
            meet(pool, 4)
            out0_pool(g)
            meet(pool, 5)
            meet(pool, 6)
            g.sig(pool.memset(ffo[:, :, :], 0.0), sem("ffo_zero"), 1)
            meet(pool, 7)
            meet(pool, 8)
            meet(pool, 9)
            prep_pool(g)
            meet(pool, 10)
            meet(pool, 11)
            att_pool(g)
            meet(pool, 12)
            meet(pool, 13)
            meet(pool, 14)
            g.sig(pool.memset(ffo[:, :, :], 0.0), sem("ffo_zero"), 2)
            meet(pool, 15)

        @block.tensor
        def _(pe):
            pe.sem_inc(sem("w_used"), RING)
            pe.wait_ge(sem("loaded"), 48)
            norm_pe(pe, 0, utok0)
            meet(pe, 1)
            proj0_pe(pe)
            meet(pe, 2)
            elem0_pe(pe)
            meet(pe, 3)
            chunk_pe(pe)
            meet(pe, 4)
            out0_pe(pe)
            meet(pe, 5)
            oproj_pe(pe, C_OUT0)
            norm_pe(pe, 1, utok)
            meet(pe, 6)
            mlp_pe(pe, C_MLP0, 0)
            meet(pe, 7)
            norm_pe(pe, 2, utok)
            meet(pe, 8)
            proj1_pe(pe)
            meet(pe, 9)
            prep_pe(pe)
            meet(pe, 10)
            cmp_pe(pe)
            meet(pe, 11)
            att_pe(pe)
            meet(pe, 12)
            yturn_pe(pe)
            meet(pe, 13)
            oproj_pe(pe, C_OUT1)
            norm_pe(pe, 3, utok)
            meet(pe, 14)
            mlp_pe(pe, C_MLP1, 1)
            meet(pe, 15)

        @block.scalar
        def _(act):
            a = Chain(act, sem("act_chain"))
            pre_in(act, 0, rowbuf)
            act.wait_ge(sem("loaded"), 48)
            norm_act(a, 0, D0, utok0)
            meet(act, 1)
            proj0_act(a)
            meet(act, 2)
            elem0_act(a)
            meet(act, 3)
            chunk_act(a)
            meet(act, 4)
            out0_act(a)
            meet(act, 5)
            oproj_act(a, 0, C_OUT0)
            post_act(a, 0)
            norm_act(a, 1, DM, utok)
            meet(act, 6)
            row_in(act, 1)
            pre_in(act, 2, prerow)
            mlp_act(a, C_MLP0, 0)
            meet(act, 7)
            post_act(a, 1)
            norm_act(a, 2, D1, utok)
            meet(act, 8)
            proj1_act(a)
            meet(act, 9)
            prep_act(a)
            meet(act, 10)
            cmp_act(a)
            meet(act, 11)
            att_act(a)
            meet(act, 12)
            yturn_act(a)
            meet(act, 13)
            oproj_act(a, 1, C_OUT1)
            post_act(a, 2)
            norm_act(a, 3, DM, utok)
            meet(act, 14)
            row_in(act, 3)
            mlp_act(a, C_MLP1, 1)
            meet(act, 15)
            post_act(a, 3)
            for i in range(NT):
                act.wait_ge(sem("x_updated"), 12 + i + 1)
                act.dma_start(out_d[:, i, :], xres[:, i, :]).then_inc(sem("out_stored"), 16)
            act.wait_ge(sem("out_stored"), 16 * NT)

        @block.vector
        def _(dve):
            v = Chain(dve, sem("dve_chain"))
            dve.wait_ge(sem("loaded"), 48)
            norm_dve(v, 0, D0, utok0, rowbuf)
            meet(dve, 1)
            proj0_dve(v)
            meet(dve, 2)
            elem0_dve(v)
            meet(dve, 3)
            chunk_dve(v)
            meet(dve, 4)
            out0_dve(v)
            meet(dve, 5)
            oproj_dve(v, 0, C_OUT0)
            post_dve(v, 0)
            norm_dve(v, 1, DM, utok, prerow)
            meet(dve, 6)
            mlp_dve(v, C_MLP0, 0)
            meet(dve, 7)
            post_dve(v, 1)
            norm_dve(v, 2, D1, utok, prerow)
            meet(dve, 8)
            proj1_dve(v)
            meet(dve, 9)
            prep_dve(v)
            meet(dve, 10)
            cmp_dve(v)
            meet(dve, 11)
            att_dve(v)
            meet(dve, 12)
            yturn_dve(v)
            meet(dve, 13)
            oproj_dve(v, 1, C_OUT1)
            post_dve(v, 2)
            norm_dve(v, 3, DM, utok, prerow)
            meet(dve, 14)
            mlp_dve(v, C_MLP1, 1)
            meet(dve, 15)
            post_dve(v, 3)


def chunks_of(w, cols, kper):
    k, n = w.shape[0] // P, w.shape[1] // cols
    a = w.reshape(k // kper, kper, P, n, cols).transpose(3, 0, 2, 1, 4)
    return a.reshape(n * (k // kper), P, kper * cols)


def kernel(**inputs):
    import numpy as _np
    import concourse.bacc as _bacc
    from concourse import mybir as _mybir
    from concourse.bass_utils import run_bass_kernel_spmd as _run

    w = {k: _np.asarray(v) for k, v in inputs.items()}

    def zeros(*s):
        return _np.zeros(s, _np.float32)

    def col(v):
        return v.reshape(-1, P).T

    ab = w["ab_w_in"][0]
    tb = _np.concatenate([ab[:, 0:1536], ab[:, 2056:3848]], 1)
    nq = w["nsa_w_in"][0]
    q = nq[:, 0:1024].reshape(D, KG, HPG, HD).transpose(0, 2, 1, 3).reshape(D, 1024)
    gates = nq[:, 1792:1840].reshape(D, KG, HPG, 3).transpose(0, 3, 2, 1).reshape(D, 48)
    in1 = _np.concatenate([q, nq[:, 1024:1792], gates, zeros(D, 2048 - 1840)], 1)
    wo1 = w["nsa_w_out"][0].reshape(KG, HPG, HD, D).transpose(1, 0, 2, 3).reshape(1024, D)
    order = [b for it in range(3) for b in list(range(4 * it, 4 * it + 4)) + list(range(12 + 4 * it, 16 + 4 * it))] + [24, 25]
    ba = _np.zeros((D, P), _np.float32)
    ba[:, 0:8] = ab[:, 2048:2056]
    parts = [chunks_of(tb, P, KD)[order], chunks_of(ba, P, KD), chunks_of(ab[:, 1536:2048], 512, 2), zeros(1, P, D), w["ab_w_out"][0].reshape(KD, P, D)]
    half = FF // 2
    mlp = [[chunks_of(m, c, k) for f in range(2)
            for m, c, k in ((w["w_ffn_up"][l][:, f * half:(f + 1) * half], P, KD), (w["w_ffn_down"][l][f * half:(f + 1) * half], 512, 2))]
           for l in range(2)]
    parts += mlp[0] + [chunks_of(in1, 512, 2), chunks_of(w["nsa_w1_k"][0], 256, 4), chunks_of(w["nsa_w1_v"][0], 256, 4), wo1.reshape(KD, P, D)] + mlp[1]
    stream = _np.concatenate(parts, 0)

    def pos_embed(a):
        return a.reshape(16, 2 * HD).T

    par = {
        "conv": w["gdn_conv"][0].reshape(4, 12, P).transpose(2, 1, 0).reshape(P, 48),
        "gnorm": col(w["gdn_norm"][0]), "mu": col(w["rwkv_mu"][0]), "k_k": col(w["rwkv_k_k"][0]),
        "k_a": col(w["rwkv_k_a"][0]), "r_k": col(w["rwkv_r_k"][0].reshape(-1)), "a0": col(w["rwkv_a0"][0]),
        "pe_k": pos_embed(w["nsa_pe_k"][0]), "pe_v": pos_embed(w["nsa_pe_v"][0]),
        "w2a2": _np.concatenate([w["rwkv_w2"][0], w["rwkv_a2"][0]], 0), "g2": w["rwkv_g2"][0],
        "w2k": w["nsa_w2_k"][0].reshape(2, P, HD).transpose(1, 0, 2).reshape(P, 128),
        "w2v": w["nsa_w2_v"][0].reshape(2, P, HD).transpose(1, 0, 2).reshape(P, 128),
        "alog": _np.broadcast_to(w["gdn_a_log"][0], (P, 4)), "dtb": _np.broadcast_to(w["gdn_dt_bias"][0], (P, 4)),
        "w0": _np.broadcast_to(w["rwkv_w0"][0], (P, 512)),
    }
    params = _np.concatenate([par[name] for name, _ in PAR_PARTS], 1)
    rows = _np.stack([w["norm_mix_post"][0], w["norm_ffn_post"][0], w["norm_mix_post"][1], w["norm_ffn_post"][1],
                      _np.concatenate([w["rwkv_ln_w"][0], w["rwkv_ln_b"][0]]),
                      w["norm_mix_pre"][0], w["norm_ffn_pre"][0], w["norm_mix_pre"][1], w["norm_ffn_pre"][1]])
    p = w["positions"][0]
    pc = _np.concatenate([p[31::16], p[-1:]])
    pos = _np.concatenate([p.reshape(NT, P).T, _np.concatenate([pc, pc, pc, pc])[:, None]], 1)

    nc = _bacc.Bacc("TRN2", target_bir_lowering=False, num_devices=1)
    arrays, args = {}, []
    for name, a in (("wstream", stream), ("x", w["x"][0]), ("pos", pos), ("params", params), ("consts", constants()), ("rows", rows)):
        a = _np.ascontiguousarray(a)
        arrays[f"in_{name}_dram"] = a
        args.append(nc.dram_tensor(f"in_{name}_dram", a.shape, _mybir.dt.from_np(a.dtype), kind="ExternalInput").ap())
    out = nc.dram_tensor("out_0_dram", (T, D), _mybir.dt.float32, kind="ExternalOutput").ap()
    program(nc, *args, out)
    r = _run(nc, [arrays], core_ids=[0])
    return r.results[0]["out_0_dram"].reshape(1, T, D)
```
